# Optimizing a Trainium2 kernel written in Bass

```python
import math
import jax, jax.numpy as jnp
from jax import lax
import numpy as np

D_MODEL = 1024
BATCH = 1
SEQ = 512
DEPTH = 2

GRID_W = 64
ROPE_THETA = 500000.0
Q_BLOCK = 128

A_HEADS = 4
A_HEAD_DIM = 64
A_ROT = A_HEAD_DIM // 4
A_Q = A_HEADS * 2 * A_HEAD_DIM
A_K = A_HEADS * 2 * A_HEAD_DIM
A_V = A_HEADS * 2 * A_HEAD_DIM

B_HEADS = 8
B_NOPE = 64
B_ROPE = 32
B_V = 64
B_Q_RANK = 256
B_KV_RANK = 128

C_HEADS = 16
C_HEAD_DIM = 64
C_WIDTH = C_HEADS * C_HEAD_DIM
NA_ROWS = 8
NA_COLS = 16

N_GROUPS = 4
EXPERTS_PER_GROUP = 8
N_EXPERTS = N_GROUPS * EXPERTS_PER_GROUP
TOP_K = 2
D_EXPERT = 512
MOE_BLOCK = 128

DN_ALPHA = (2 * DEPTH) ** 0.25
DN_BETA = (8 * DEPTH) ** -0.25
LN_EPS = 1e-5
RMS_EPS = 1e-6

EVEN_IN = A_Q + A_K + A_V + B_Q_RANK + B_KV_RANK + B_ROPE
EVEN_SPLITS = (A_Q, A_Q + A_K, A_Q + A_K + A_V, A_Q + A_K + A_V + B_Q_RANK,
               A_Q + A_K + A_V + B_Q_RANK + B_KV_RANK)
EVEN_OUT = A_HEADS * 2 * A_HEAD_DIM + B_HEADS * B_V
N_EVEN = (DEPTH + 1) // 2
N_ODD = DEPTH // 2


def layer_norm(x, g, b):
    xf = x.astype(jnp.float32)
    mu = jnp.mean(xf, axis=-1, keepdims=True)
    var = jnp.mean(jnp.square(xf - mu), axis=-1, keepdims=True)
    y = (xf - mu) * lax.rsqrt(var + LN_EPS) * g.astype(jnp.float32) + b.astype(jnp.float32)
    return y.astype(x.dtype)

def rms_norm(x, g):
    xf = x.astype(jnp.float32)
    y = xf * lax.rsqrt(jnp.mean(xf * xf, axis=-1, keepdims=True) + RMS_EPS) * g.astype(jnp.float32)
    return y.astype(x.dtype)

def rope_tables(seq, rot_dim):
    inv_freq = ROPE_THETA ** (-jnp.arange(0, rot_dim, 2, dtype=jnp.float32) / rot_dim)
    ang = jnp.arange(seq, dtype=jnp.float32)[:, None] * inv_freq[None, :]
    return jnp.cos(ang), jnp.sin(ang)

def apply_rope(x, cos, sin):
    half = cos.shape[-1]
    r = 2 * half
    cos = cos.astype(x.dtype)
    sin = sin.astype(x.dtype)
    x1 = x[..., :half]
    x2 = x[..., half:r]
    return jnp.concatenate([x1 * cos - x2 * sin, x2 * cos + x1 * sin, x[..., r:]], axis=-1)

def diff_attention(q, k, v, lam, subln_g, lambda_init, cos, sin):
    B, S, H, _, d = q.shape
    nb = S // Q_BLOCK
    q = apply_rope(q.transpose(0, 2, 3, 1, 4), cos, sin)
    k = apply_rope(k.transpose(0, 2, 3, 1, 4), cos, sin)
    v = v.transpose(0, 2, 1, 3)
    q_blocks = q.reshape(B, H, 2, nb, Q_BLOCK, d).transpose(3, 0, 1, 2, 4, 5)
    scale = d ** -0.5

    def block(qb):
        s = jnp.einsum('bhmqd,bhmkd->bhmqk', qb, k).astype(jnp.float32) * scale
        p = jax.nn.softmax(s, axis=-1)
        w = p[:, :, 0] - lam * p[:, :, 1]
        return jnp.einsum('bhqk,bhke->bhqe', w.astype(v.dtype), v)

    o = lax.map(block, q_blocks)
    o = rms_norm(o, subln_g) * (1.0 - lambda_init)
    return o.transpose(1, 0, 3, 2, 4).reshape(B, S, H * 2 * d)

def latent_attention(c_q, c_kv, k_r, q_norm_g, w_uq, kv_norm_g, w_ukv, cos, sin):
    B, S, _ = c_q.shape
    H = B_HEADS
    nb = S // Q_BLOCK
    q = (rms_norm(c_q, q_norm_g) @ w_uq).reshape(B, S, H, B_NOPE + B_ROPE).transpose(0, 2, 1, 3)
    q_nope = q[..., :B_NOPE]
    q_rope = apply_rope(q[..., B_NOPE:], cos, sin)
    kv = (rms_norm(c_kv, kv_norm_g) @ w_ukv).reshape(B, S, H, B_NOPE + B_V).transpose(0, 2, 1, 3)
    k_nope = kv[..., :B_NOPE]
    v = kv[..., B_NOPE:]
    k_rope = apply_rope(k_r, cos, sin)
    qn_blocks = q_nope.reshape(B, H, nb, Q_BLOCK, B_NOPE).transpose(2, 0, 1, 3, 4)
    qr_blocks = q_rope.reshape(B, H, nb, Q_BLOCK, B_ROPE).transpose(2, 0, 1, 3, 4)
    scale = (B_NOPE + B_ROPE) ** -0.5

    def block(args):
        qn, qr = args
        s = (jnp.einsum('bhqd,bhkd->bhqk', qn, k_nope)
             + jnp.einsum('bhqr,bkr->bhqk', qr, k_rope)).astype(jnp.float32) * scale
        p = jax.nn.softmax(s, axis=-1)
        return jnp.einsum('bhqk,bhke->bhqe', p.astype(v.dtype), v)

    o = lax.map(block, (qn_blocks, qr_blocks))
    return o.transpose(1, 0, 3, 2, 4).reshape(B, S, H * B_V)

def neighbourhood_attention(q, k, v, rel_bias):
    B, S, H, d = q.shape
    rows = S // GRID_W
    kh = min(NA_ROWS, rows)
    kw = NA_COLS
    to_grid = lambda t: t.reshape(B, rows, GRID_W, H, d).transpose(0, 3, 1, 2, 4)
    qg, kg, vg = to_grid(q), to_grid(k), to_grid(v)
    cols = jnp.arange(GRID_W)
    col_start = jnp.clip(cols - kw // 2, 0, GRID_W - kw)
    col_idx = col_start[:, None] + jnp.arange(kw)[None, :]
    col_off = col_idx - cols[:, None] + (NA_COLS - 1)
    scale = d ** -0.5

    def row(args):
        r, q_row = args
        r0 = jnp.clip(r - kh // 2, 0, rows - kh)
        k_band = lax.dynamic_slice_in_dim(kg, r0, kh, axis=2)
        v_band = lax.dynamic_slice_in_dim(vg, r0, kh, axis=2)
        k_win = k_band[:, :, :, col_idx]
        v_win = v_band[:, :, :, col_idx]
        row_off = r0 + jnp.arange(kh) - r + (NA_ROWS - 1)
        bias = rel_bias[:, row_off[:, None, None], col_off[None]]
        bias = bias.transpose(0, 2, 1, 3).astype(jnp.float32)
        s = jnp.einsum('bhcd,bhicjd->bhcij', q_row, k_win).astype(jnp.float32) * scale + bias[None]
        p = jax.nn.softmax(s.reshape(B, H, GRID_W, kh * kw), axis=-1).reshape(B, H, GRID_W, kh, kw)
        return jnp.einsum('bhcij,bhicje->bhce', p.astype(v_win.dtype), v_win)

    o = lax.map(row, (jnp.arange(rows), qg.transpose(2, 0, 1, 3, 4)))
    return o.transpose(1, 0, 3, 2, 4).reshape(B, S, H * d)

def even_mixer(x, w_in, lam_q1, lam_k1, lam_q2, lam_k2, subln_g, q_norm_g, w_uq,
               kv_norm_g, w_ukv, w_o, lambda_init, rope_a, rope_b):
    B, S, _ = x.shape
    h = x @ w_in
    qa, ka, va, cq, ckv, kr = jnp.split(h, EVEN_SPLITS, axis=-1)
    f32 = jnp.float32
    lam = (jnp.exp(jnp.sum(lam_q1.astype(f32) * lam_k1.astype(f32)))
           - jnp.exp(jnp.sum(lam_q2.astype(f32) * lam_k2.astype(f32))) + lambda_init)
    a_out = diff_attention(qa.reshape(B, S, A_HEADS, 2, A_HEAD_DIM),
                           ka.reshape(B, S, A_HEADS, 2, A_HEAD_DIM),
                           va.reshape(B, S, A_HEADS, 2 * A_HEAD_DIM),
                           lam, subln_g, lambda_init, rope_a[0], rope_a[1])
    b_out = latent_attention(cq, ckv, kr, q_norm_g, w_uq, kv_norm_g, w_ukv, rope_b[0], rope_b[1])
    return jnp.concatenate([a_out, b_out], axis=-1) @ w_o

def odd_mixer(x, w_qkv, rel_bias, w_o):
    B, S, _ = x.shape
    q, k, v = jnp.split(x @ w_qkv, 3, axis=-1)
    shp = (B, S, C_HEADS, C_HEAD_DIM)
    o = neighbourhood_attention(q.reshape(shp), k.reshape(shp), v.reshape(shp), rel_bias)
    return o @ w_o

def hier_moe(x, w_rg, b_rg, w_re, b_re, w1, w3, w2):
    B, S, D = x.shape
    N = B * S
    xt = x.reshape(N, D)
    g_prob = jax.nn.softmax((xt @ w_rg).astype(jnp.float32) + b_rg.astype(jnp.float32), axis=-1)
    grp = jnp.argmax(g_prob, axis=-1).astype(jnp.int32)
    g_w = jnp.take_along_axis(g_prob, grp[:, None], axis=-1)
    e_logits = ((xt @ w_re).astype(jnp.float32) + b_re.astype(jnp.float32)).reshape(N, N_GROUPS, EXPERTS_PER_GROUP)
    idx = jnp.broadcast_to(grp[:, None, None], (N, 1, EXPERTS_PER_GROUP))
    e_logits = jnp.take_along_axis(e_logits, idx, axis=1)[:, 0]
    top_v, top_i = lax.top_k(e_logits, TOP_K)
    gate = jax.nn.softmax(top_v, axis=-1) * g_w
    expert = grp[:, None] * EXPERTS_PER_GROUP + top_i.astype(jnp.int32)
    A = N * TOP_K
    e_flat = expert.reshape(A)
    w_flat = gate.reshape(A)
    tok = jnp.repeat(jnp.arange(N, dtype=jnp.int32), TOP_K)
    order = jnp.argsort(e_flat)
    e_s, tok_s, w_s = e_flat[order], tok[order], w_flat[order]
    counts = jnp.bincount(e_flat, length=N_EXPERTS)
    start = jnp.cumsum(counts) - counts
    padded = (counts + MOE_BLOCK - 1) // MOE_BLOCK * MOE_BLOCK
    pad_end = jnp.cumsum(padded)
    pad_start = pad_end - padded
    dest = pad_start[e_s] + jnp.arange(A) - start[e_s]
    n_blocks = -(-A // MOE_BLOCK) + N_EXPERTS
    P = n_blocks * MOE_BLOCK
    slot_tok = jnp.full((P,), N, jnp.int32).at[dest].set(tok_s)
    slot_w = jnp.zeros((P,), jnp.float32).at[dest].set(w_s)
    block_exp = jnp.minimum(jnp.searchsorted(pad_end, jnp.arange(n_blocks) * MOE_BLOCK, side='right'),
                            N_EXPERTS - 1).astype(jnp.int32)
    x_pad = jnp.concatenate([xt, jnp.zeros((1, D), xt.dtype)], axis=0)

    def block(args):
        tids, e, w = args
        xb = x_pad[tids]
        hdn = jax.nn.silu(xb @ w1[e]) * (xb @ w3[e])
        return (hdn @ w2[e]) * w[:, None].astype(xb.dtype)

    y = lax.map(block, (slot_tok.reshape(n_blocks, MOE_BLOCK), block_exp,
                        slot_w.reshape(n_blocks, MOE_BLOCK)))
    out = jax.ops.segment_sum(y.reshape(P, D), slot_tok, num_segments=N + 1)[:N]
    return out.reshape(B, S, D)

def first_inputs(seed: int = 0) -> dict:
    key = jax.random.key(seed)
    ks = iter(jax.random.split(key, 32))
    nrm = lambda shape, scale: jax.random.normal(next(ks), shape, jnp.float32) * scale
    gain = lambda shape: 1.0 + nrm(shape, 0.02)
    D = D_MODEL
    return {
        "x": nrm((BATCH, SEQ, D), 1.0),
        "even_w_in": nrm((N_EVEN, D, EVEN_IN), D ** -0.5),
        "even_lam_q1": nrm((N_EVEN, A_HEAD_DIM), 0.1),
        "even_lam_k1": nrm((N_EVEN, A_HEAD_DIM), 0.1),
        "even_lam_q2": nrm((N_EVEN, A_HEAD_DIM), 0.1),
        "even_lam_k2": nrm((N_EVEN, A_HEAD_DIM), 0.1),
        "even_subln_g": gain((N_EVEN, 2 * A_HEAD_DIM)),
        "even_q_norm_g": gain((N_EVEN, B_Q_RANK)),
        "even_w_uq": nrm((N_EVEN, B_Q_RANK, B_HEADS * (B_NOPE + B_ROPE)), B_Q_RANK ** -0.5),
        "even_kv_norm_g": gain((N_EVEN, B_KV_RANK)),
        "even_w_ukv": nrm((N_EVEN, B_KV_RANK, B_HEADS * (B_NOPE + B_V)), B_KV_RANK ** -0.5),
        "even_w_o": nrm((N_EVEN, EVEN_OUT, D), EVEN_OUT ** -0.5 * DN_BETA),
        "odd_w_qkv": nrm((N_ODD, D, 3 * C_WIDTH), D ** -0.5),
        "odd_rel_bias": nrm((N_ODD, C_HEADS, 2 * NA_ROWS - 1, 2 * NA_COLS - 1), 0.02),
        "odd_w_o": nrm((N_ODD, C_WIDTH, D), C_WIDTH ** -0.5 * DN_BETA),
        "ln1_g": gain((DEPTH, D)),
        "ln1_b": nrm((DEPTH, D), 0.02),
        "ln2_g": gain((DEPTH, D)),
        "ln2_b": nrm((DEPTH, D), 0.02),
        "w_router_group": nrm((DEPTH, D, N_GROUPS), D ** -0.5),
        "b_router_group": nrm((DEPTH, N_GROUPS), 0.01),
        "w_router_expert": nrm((DEPTH, D, N_EXPERTS), D ** -0.5),
        "b_router_expert": nrm((DEPTH, N_EXPERTS), 0.01),
        "w_gate": nrm((DEPTH, N_EXPERTS, D, D_EXPERT), D ** -0.5),
        "w_up": nrm((DEPTH, N_EXPERTS, D, D_EXPERT), D ** -0.5),
        "w_down": nrm((DEPTH, N_EXPERTS, D_EXPERT, D), D_EXPERT ** -0.5 * DN_BETA),
    }

def first_block(x, even_w_in, even_lam_q1, even_lam_k1, even_lam_q2, even_lam_k2, even_subln_g,
              even_q_norm_g, even_w_uq, even_kv_norm_g, even_w_ukv, even_w_o,
              odd_w_qkv, odd_rel_bias, odd_w_o, ln1_g, ln1_b, ln2_g, ln2_b,
              w_router_group, b_router_group, w_router_expert, b_router_expert,
              w_gate, w_up, w_down):
    S = x.shape[1]
    rope_a = rope_tables(S, A_ROT)
    rope_b = rope_tables(S, B_ROPE)
    for i in range(DEPTH):
        j = i // 2
        if i % 2 == 0:
            lambda_init = 0.8 - 0.6 * math.exp(-0.3 * i)
            m = even_mixer(x, even_w_in[j], even_lam_q1[j], even_lam_k1[j], even_lam_q2[j],
                           even_lam_k2[j], even_subln_g[j], even_q_norm_g[j], even_w_uq[j],
                           even_kv_norm_g[j], even_w_ukv[j], even_w_o[j], lambda_init, rope_a, rope_b)
        else:
            m = odd_mixer(x, odd_w_qkv[j], odd_rel_bias[j], odd_w_o[j])
        x = layer_norm(DN_ALPHA * x + m, ln1_g[i], ln1_b[i])
        f = hier_moe(x, w_router_group[i], b_router_group[i], w_router_expert[i], b_router_expert[i],
                     w_gate[i], w_up[i], w_down[i])
        x = layer_norm(DN_ALPHA * x + f, ln2_g[i], ln2_b[i])
    return x


RET_HEADS = 4
RET_DK = 128
RET_DV = 128
RET_CHUNK = 128
ROPE_BASE = 10000.0
GDN_HEADS = 4
GDN_DK = 128
GDN_DV = 128
GDN_CHUNK = 64
SHORT_CONV = 4
RET_WIDTH = RET_HEADS * RET_DV
GDN_WIDTH = GDN_HEADS * GDN_DV
MIX0_OUT = RET_WIDTH + GDN_WIDTH
MIX0_SPLITS = (RET_HEADS * RET_DK, RET_HEADS * RET_DK, RET_WIDTH, RET_WIDTH,
               GDN_HEADS * GDN_DK, GDN_HEADS * GDN_DK, GDN_WIDTH, GDN_WIDTH,
               GDN_HEADS, GDN_HEADS)
MIX0_IN = sum(MIX0_SPLITS)
D_RNN = D_MODEL
LRU_BLOCKS = 8
LRU_BLOCK = D_RNN // LRU_BLOCKS
LRU_CONV = 4
LRU_C = 8.0
D_FF = ((8 * D_MODEL // 3 + 127) // 128) * 128
FFN_CONV = 3
EPS = 1e-6
N_EVEN_2 = (DEPTH + 1) // 2
N_ODD_2 = DEPTH // 2


def _rms(x):
    xf = x.astype(jnp.float32)
    return xf * lax.rsqrt(jnp.mean(xf * xf, axis=-1, keepdims=True) + EPS)

def rms_norm_2(x, gain):
    return (_rms(x) * gain.astype(jnp.float32)).astype(x.dtype)

def l2norm(x):
    return x * lax.rsqrt(jnp.sum(x * x, axis=-1, keepdims=True) + EPS)

def causal_dwconv(x, w):
    width, ch = w.shape
    return lax.conv_general_dilated(
        x, w[:, None, :].astype(x.dtype), window_strides=(1,),
        padding=[(width - 1, 0)], dimension_numbers=('NWC', 'WIO', 'NWC'),
        feature_group_count=ch)

def rotary(x, pos):
    half = x.shape[-1] // 2
    inv_freq = ROPE_BASE ** (-jnp.arange(half, dtype=jnp.float32) / half)
    ang = pos.astype(jnp.float32)[:, None] * inv_freq[None, :]
    cos = jnp.cos(ang)[None, :, None, :]
    sin = jnp.sin(ang)[None, :, None, :]
    x1, x2 = x[..., :half], x[..., half:]
    return jnp.concatenate([x1 * cos - x2 * sin, x1 * sin + x2 * cos], axis=-1)

def to_chunks(x, c):
    b, t, h, d = x.shape
    return x.reshape(b, t // c, c, h, d).transpose(0, 3, 1, 2, 4)

def from_chunks(x):
    b, h, n, c, d = x.shape
    return x.transpose(0, 2, 3, 1, 4).reshape(b, n * c, h, d)

def retention_chunkwise(q, k, v):
    b, t, h, dk = q.shape
    dv = v.shape[-1]
    c = RET_CHUNK
    log_gamma = jnp.log1p(-jnp.exp2(-5.0 - jnp.arange(h, dtype=jnp.float32)))
    qc, kc, vc = to_chunks(q, c), to_chunks(k * dk ** -0.5, c), to_chunks(v, c)
    idx = jnp.arange(c, dtype=jnp.float32)
    rel = idx[:, None] - idx[None, :]
    causal = rel >= 0
    dmask = jnp.where(causal, jnp.exp(log_gamma[:, None, None] * jnp.where(causal, rel, 0.0)), 0.0)
    scores = jnp.einsum('bhnid,bhnjd->bhnij', qc, kc) * dmask[:, None]
    intra = jnp.einsum('bhnij,bhnjv->bhniv', scores, vc)
    k_tail = kc * jnp.exp(log_gamma[:, None, None] * (c - 1 - idx))[..., None]
    kv = jnp.einsum('bhncd,bhncv->nbhdv', k_tail, vc)
    chunk_decay = jnp.exp(log_gamma * c)[None, :, None, None]

    def step(s, kv_n):
        return s * chunk_decay + kv_n, s

    _, s_prev = lax.scan(step, jnp.zeros((b, h, dk, dv), jnp.float32), kv)
    q_decay = qc * jnp.exp(log_gamma[:, None, None] * (idx + 1.0))[..., None]
    inter = jnp.einsum('bhncd,nbhdv->bhncv', q_decay, s_prev)
    return from_chunks(intra + inter)

def gated_delta_chunkwise(q, k, v, g, beta):
    b, t, h, dk = q.shape
    dv = v.shape[-1]
    c = GDN_CHUNK
    qc = to_chunks(q * dk ** -0.5, c)
    kc = to_chunks(k, c)
    vc = to_chunks(v, c)
    gc = jnp.cumsum(to_chunks(g[..., None], c)[..., 0], axis=-1)
    bc = to_chunks(beta[..., None], c)
    tril = jnp.tril(jnp.ones((c, c), bool))
    strict = jnp.tril(jnp.ones((c, c), bool), -1)
    decay = jnp.exp(jnp.where(tril, gc[..., :, None] - gc[..., None, :], -jnp.inf))
    k_beta = kc * bc
    lmat = jnp.where(strict, jnp.einsum('bhnid,bhnjd->bhnij', k_beta, kc) * decay, 0.0)
    rhs = jnp.concatenate([vc * bc, k_beta * jnp.exp(gc)[..., None]], axis=-1)
    sol = lax.linalg.triangular_solve(lmat + jnp.eye(c, dtype=jnp.float32), rhs,
                                      left_side=True, lower=True)
    u, w = sol[..., :dv], sol[..., dv:]
    attn = jnp.where(tril, jnp.einsum('bhnid,bhnjd->bhnij', qc, kc) * decay, 0.0)
    q_decay = qc * jnp.exp(gc)[..., None]
    g_last = gc[..., -1:]
    k_tail = kc * jnp.exp(g_last - gc)[..., None]
    chunk_decay = jnp.exp(g_last)[..., None]
    xs = tuple(jnp.moveaxis(a, 2, 0) for a in (u, w, attn, q_decay, k_tail, chunk_decay))

    def step(s, inp):
        u_n, w_n, a_n, qd_n, kt_n, cd_n = inp
        v_new = u_n - jnp.einsum('bhcd,bhdv->bhcv', w_n, s)
        o = jnp.einsum('bhcd,bhdv->bhcv', qd_n, s) + jnp.einsum('bhij,bhjv->bhiv', a_n, v_new)
        s = s * cd_n + jnp.einsum('bhcd,bhcv->bhdv', kt_n, v_new)
        return s, o

    _, o = lax.scan(step, jnp.zeros((b, h, dk, dv), jnp.float32), xs)
    return from_chunks(jnp.moveaxis(o, 0, 2))

def retention_deltanet_mixer(hn, pos, w_in, conv_w, a_log, dt_bias, out_gain, w_out):
    b, t, _ = hn.shape
    f32 = jnp.float32
    split_at = np.cumsum(MIX0_SPLITS)[:-1].tolist()
    q_r, k_r, v_r, g_r, q_d, k_d, v_d, g_d, b_d, a_d = jnp.split(hn @ w_in, split_at, axis=-1)
    q_r = rotary(q_r.reshape(b, t, RET_HEADS, RET_DK).astype(f32), pos)
    k_r = rotary(k_r.reshape(b, t, RET_HEADS, RET_DK).astype(f32), pos)
    v_r = v_r.reshape(b, t, RET_HEADS, RET_DV).astype(f32)
    y_r = _rms(retention_chunkwise(q_r, k_r, v_r)).reshape(b, t, RET_WIDTH)
    y_r = y_r * jax.nn.silu(g_r.astype(f32))
    qkv = jax.nn.silu(causal_dwconv(jnp.concatenate([q_d, k_d, v_d], axis=-1), conv_w)).astype(f32)
    q_d, k_d, v_d = jnp.split(qkv, [GDN_HEADS * GDN_DK, 2 * GDN_HEADS * GDN_DK], axis=-1)
    q_d = l2norm(q_d.reshape(b, t, GDN_HEADS, GDN_DK))
    k_d = l2norm(k_d.reshape(b, t, GDN_HEADS, GDN_DK))
    v_d = v_d.reshape(b, t, GDN_HEADS, GDN_DV)
    beta = jax.nn.sigmoid(b_d.astype(f32))
    g = -jnp.exp(a_log.astype(f32)) * jax.nn.softplus(a_d.astype(f32) + dt_bias.astype(f32))
    y_d = gated_delta_chunkwise(q_d, k_d, v_d, g, beta)
    y_d = rms_norm_2(y_d, out_gain) * jax.nn.silu(g_d.astype(f32).reshape(b, t, GDN_HEADS, GDN_DV))
    y = jnp.concatenate([y_r, y_d.reshape(b, t, GDN_WIDTH)], axis=-1).astype(hn.dtype)
    return y @ w_out

def _linear_combine(e1, e2):
    a1, b1 = e1
    a2, b2 = e2
    return a1 * a2, a2 * b1 + b2

def rglru_mixer(hn, w_in, conv_w, conv_b, w_a, b_a, w_x, b_x, lam, w_out):
    b, t, _ = hn.shape
    f32 = jnp.float32
    gate, xr = jnp.split(hn @ w_in, 2, axis=-1)
    xr = (causal_dwconv(xr, conv_w) + conv_b).astype(f32)
    xb = xr.reshape(b, t, LRU_BLOCKS, LRU_BLOCK)
    r = jax.nn.sigmoid(jnp.einsum('btni,nij->btnj', xb, w_a.astype(f32)).reshape(b, t, D_RNN) + b_a)
    i = jax.nn.sigmoid(jnp.einsum('btni,nij->btnj', xb, w_x.astype(f32)).reshape(b, t, D_RNN) + b_x)
    log_a = -LRU_C * r * jax.nn.softplus(-lam.astype(f32))
    a = jnp.exp(log_a)
    u = jnp.sqrt(-jnp.expm1(2.0 * log_a)) * (i * xr)
    _, hs = lax.associative_scan(_linear_combine, (a, u), axis=1)
    y = jax.nn.gelu(gate.astype(f32)) * hs
    return y.astype(hn.dtype) @ w_out

def conv_ffn(hn, w_up, conv_w, conv_b, w_down):
    up = causal_dwconv(hn @ w_up, conv_w) + conv_b
    gate, val = jnp.split(up, 2, axis=-1)
    return (jax.nn.silu(gate) * val) @ w_down

def second_inputs(seed: int = 0) -> dict:
    key = jax.random.key(seed)
    ks = jax.random.split(key, 24)
    nrm = jax.random.normal
    f32 = jnp.float32
    x = nrm(ks[0], (BATCH, SEQ, D_MODEL), f32)
    norm_mix = 1.0 + 0.02 * nrm(ks[1], (DEPTH, D_MODEL), f32)
    norm_ffn = 1.0 + 0.02 * nrm(ks[2], (DEPTH, D_MODEL), f32)
    ret_gdn_w_in = nrm(ks[3], (N_EVEN_2, D_MODEL, MIX0_IN), f32) * D_MODEL ** -0.5
    gdn_conv_w = nrm(ks[4], (N_EVEN_2, SHORT_CONV, 2 * GDN_HEADS * GDN_DK + GDN_WIDTH), f32) * SHORT_CONV ** -0.5
    gdn_a_log = jnp.log(jax.random.uniform(ks[5], (N_EVEN_2, GDN_HEADS), f32, 1.0, 16.0))
    dt = jnp.exp(jax.random.uniform(ks[6], (N_EVEN_2, GDN_HEADS), f32, np.log(1e-3), np.log(1e-1)))
    gdn_dt_bias = dt + jnp.log(-jnp.expm1(-dt))
    gdn_out_gain = 1.0 + 0.02 * nrm(ks[7], (N_EVEN_2, GDN_DV), f32)
    ret_gdn_w_out = nrm(ks[8], (N_EVEN_2, MIX0_OUT, D_MODEL), f32) * MIX0_OUT ** -0.5
    lru_w_in = nrm(ks[9], (N_ODD_2, D_MODEL, 2 * D_RNN), f32) * D_MODEL ** -0.5
    lru_conv_w = nrm(ks[10], (N_ODD_2, LRU_CONV, D_RNN), f32) * LRU_CONV ** -0.5
    lru_conv_b = 0.01 * nrm(ks[11], (N_ODD_2, D_RNN), f32)
    lru_w_a = nrm(ks[12], (N_ODD_2, LRU_BLOCKS, LRU_BLOCK, LRU_BLOCK), f32) * LRU_BLOCK ** -0.5
    lru_b_a = 0.01 * nrm(ks[13], (N_ODD_2, D_RNN), f32)
    lru_w_x = nrm(ks[14], (N_ODD_2, LRU_BLOCKS, LRU_BLOCK, LRU_BLOCK), f32) * LRU_BLOCK ** -0.5
    lru_b_x = 0.01 * nrm(ks[15], (N_ODD_2, D_RNN), f32)
    a_c = jax.random.uniform(ks[16], (N_ODD_2, D_RNN), f32, 0.9, 0.999)
    a0 = a_c ** (1.0 / LRU_C)
    lru_lambda = jnp.log(a0) - jnp.log1p(-a0)
    lru_w_out = nrm(ks[17], (N_ODD_2, D_RNN, D_MODEL), f32) * D_RNN ** -0.5
    ffn_w_up = nrm(ks[18], (DEPTH, D_MODEL, 2 * D_FF), f32) * D_MODEL ** -0.5
    ffn_conv_w = nrm(ks[19], (DEPTH, FFN_CONV, 2 * D_FF), f32) * FFN_CONV ** -0.5
    ffn_conv_b = 0.01 * nrm(ks[20], (DEPTH, 2 * D_FF), f32)
    ffn_w_down = nrm(ks[21], (DEPTH, D_FF, D_MODEL), f32) * D_FF ** -0.5
    norm_final = 1.0 + 0.02 * nrm(ks[22], (D_MODEL,), f32)
    return {"x": x, "norm_mix": norm_mix, "norm_ffn": norm_ffn,
            "ret_gdn_w_in": ret_gdn_w_in, "gdn_conv_w": gdn_conv_w, "gdn_a_log": gdn_a_log,
            "gdn_dt_bias": gdn_dt_bias, "gdn_out_gain": gdn_out_gain, "ret_gdn_w_out": ret_gdn_w_out,
            "lru_w_in": lru_w_in, "lru_conv_w": lru_conv_w, "lru_conv_b": lru_conv_b,
            "lru_w_a": lru_w_a, "lru_b_a": lru_b_a, "lru_w_x": lru_w_x, "lru_b_x": lru_b_x,
            "lru_lambda": lru_lambda, "lru_w_out": lru_w_out,
            "ffn_w_up": ffn_w_up, "ffn_conv_w": ffn_conv_w, "ffn_conv_b": ffn_conv_b,
            "ffn_w_down": ffn_w_down, "norm_final": norm_final}

def second_block(x, norm_mix, norm_ffn, ret_gdn_w_in, gdn_conv_w, gdn_a_log, gdn_dt_bias,
              gdn_out_gain, ret_gdn_w_out, lru_w_in, lru_conv_w, lru_conv_b, lru_w_a, lru_b_a,
              lru_w_x, lru_b_x, lru_lambda, lru_w_out, ffn_w_up, ffn_conv_w, ffn_conv_b,
              ffn_w_down, norm_final):
    pos = jnp.arange(x.shape[1], dtype=jnp.int32)
    h = x
    for layer in range(DEPTH):
        hn = rms_norm_2(h, norm_mix[layer])
        if layer % 2 == 0:
            e = layer // 2
            h = h + retention_deltanet_mixer(hn, pos, ret_gdn_w_in[e], gdn_conv_w[e], gdn_a_log[e],
                                             gdn_dt_bias[e], gdn_out_gain[e], ret_gdn_w_out[e])
        else:
            o = layer // 2
            h = h + rglru_mixer(hn, lru_w_in[o], lru_conv_w[o], lru_conv_b[o], lru_w_a[o], lru_b_a[o],
                                lru_w_x[o], lru_b_x[o], lru_lambda[o], lru_w_out[o])
        h = h + conv_ffn(rms_norm_2(h, norm_ffn[layer]), ffn_w_up[layer], ffn_conv_w[layer],
                         ffn_conv_b[layer], ffn_w_down[layer])
    return rms_norm_2(h, norm_final)


def setup_inputs(seed=0):
    out = dict(first_inputs(seed))
    for name, value in second_inputs(seed + 1).items():
        if name != "x":
            out[name + "_2"] = value
    return out


def reference(
    x, even_w_in, even_lam_q1, even_lam_k1, even_lam_q2, even_lam_k2, even_subln_g,
    even_q_norm_g, even_w_uq, even_kv_norm_g, even_w_ukv, even_w_o, odd_w_qkv, odd_rel_bias,
    odd_w_o, ln1_g, ln1_b, ln2_g, ln2_b, w_router_group, b_router_group, w_router_expert,
    b_router_expert, w_gate, w_up, w_down, norm_mix_2, norm_ffn_2, ret_gdn_w_in_2, gdn_conv_w_2,
    gdn_a_log_2, gdn_dt_bias_2, gdn_out_gain_2, ret_gdn_w_out_2, lru_w_in_2, lru_conv_w_2,
    lru_conv_b_2, lru_w_a_2, lru_b_a_2, lru_w_x_2, lru_b_x_2, lru_lambda_2, lru_w_out_2,
    ffn_w_up_2, ffn_conv_w_2, ffn_conv_b_2, ffn_w_down_2, norm_final_2,
):
    x = first_block(
        x, even_w_in, even_lam_q1, even_lam_k1, even_lam_q2, even_lam_k2, even_subln_g,
        even_q_norm_g, even_w_uq, even_kv_norm_g, even_w_ukv, even_w_o, odd_w_qkv, odd_rel_bias,
        odd_w_o, ln1_g, ln1_b, ln2_g, ln2_b, w_router_group, b_router_group, w_router_expert,
        b_router_expert, w_gate, w_up, w_down,
    )
    return second_block(
        x, norm_mix_2, norm_ffn_2, ret_gdn_w_in_2, gdn_conv_w_2, gdn_a_log_2, gdn_dt_bias_2,
        gdn_out_gain_2, ret_gdn_w_out_2, lru_w_in_2, lru_conv_w_2, lru_conv_b_2, lru_w_a_2,
        lru_b_a_2, lru_w_x_2, lru_b_x_2, lru_lambda_2, lru_w_out_2, ffn_w_up_2, ffn_conv_w_2,
        ffn_conv_b_2, ffn_w_down_2, norm_final_2,
    )


_drawn_inputs = setup_inputs


def setup_inputs(seed=0):
    import zlib

    import numpy as np

    out = dict(_drawn_inputs(seed))
    spreads = {}
    factors = {'even_lam_k2': 3.022,
     'even_subln_g': 4.19,
     'even_q_norm_g': 8.0,
     'even_kv_norm_g': 6.708,
     'odd_rel_bias': 8.0,
     'b_router_group': 7.7,
     'b_router_expert': 4.487,
     'norm_ffn_2': 3.04,
     'gdn_out_gain_2': 6.839,
     'lru_b_a_2': 200.0,
     'lru_b_x_2': 64.0,
     'ffn_conv_b_2': 5.498,
     'norm_final_2': 25.707,
     'lru_conv_b_2': 8.0,
     'lru_w_a_2': 3.055}
    for name, (base, spread) in spreads.items():
        noise = np.random.default_rng([zlib.crc32(name.encode()), seed]).standard_normal(out[name].shape)
        drawn = base * np.exp(spread * noise) if base else spread * noise
        out[name] = __import__('jax').numpy.asarray(drawn.astype(out[name].dtype))
    for name, factor in factors.items():
        out[name] = (out[name] * factor).astype(out[name].dtype)
    return out
```

```python
from contextlib import ExitStack
import math

import concourse.bass as bass
from concourse import mybir

ALU = mybir.AluOpType
ACT = mybir.ActivationFunctionType
F32 = mybir.dt.float32
U32 = mybir.dt.uint32
I32 = mybir.dt.int32
AX_X = mybir.AxisListType.X

P = 128
D = 1024
S = 512
T = S // P
KD = D // P
BANK = 512
N_BANKS = 8

A_HEADS, A_DIM, A_ROT = 4, 64, 16
A_QKV = A_HEADS * 2 * A_DIM
B_HEADS, B_NOPE, B_ROPE, B_V = 8, 64, 32, 64
B_QK = B_NOPE + B_ROPE
B_Q_RANK, B_KV_RANK = 256, 128
EVEN_IN = 3 * A_QKV + B_Q_RANK + B_KV_RANK + B_ROPE
C_HEADS, C_DIM = 16, 64
GRID_W, NA_ROWS, NA_COLS = 64, 8, 16
REL_R, REL_C = 2 * NA_ROWS - 1, 2 * NA_COLS - 1

GROUPS, PER_GROUP, D_EXPERT = 4, 8, 512
EXPERTS = GROUPS * PER_GROUP
ROUTES = GROUPS + EXPERTS
TOP_K = 2
CAP = 96
KE = D_EXPERT // P

RET_HEADS, GDN_HEADS, HEAD = 4, 4, 128
SHORT_CONV, LRU_CONV, FFN_CONV = 4, 4, 3
D_FF = ((8 * D // 3 + 127) // 128) * 128
KF = D_FF // P
FF_COLS = BANK // 2
MIX0_IN = 8 * 512 + 2 * GDN_HEADS
BIG = 16896

ALPHA = 4 ** 0.25
LN_EPS, RMS_EPS = 1e-5, 1e-6
LAMBDA_INIT = 0.8 - 0.6 * math.exp(0.0)
MASKED = -1e30
LEVELS = 7


def shape_constants():
    import numpy as np
    cols, at, n = [], {}, 0

    def put(name, a):
        nonlocal n
        a = np.asarray(a, np.float32).reshape(a.shape[0], -1)
        full = np.zeros((P, a.shape[1]), np.float32)
        full[:a.shape[0]] = a
        cols.append(full)
        at[name] = (n, a.shape[1])
        n += a.shape[1]

    i = np.arange(P)
    put("ident", np.eye(P))
    put("upto", (i[:, None] <= i[None, :]).astype(np.float32))
    put("before", (i[:, None] < i[None, :]).astype(np.float32))
    put("minus_half", np.full((P, 1), -0.5))
    put("eps", np.full((P, 1), RMS_EPS))
    put("iota", np.tile(np.arange(EXPERTS), (P, 1)))

    def rope(theta, rot, name):
        f = np.float32(theta) ** (-np.arange(0, rot, 2, dtype=np.float32) / np.float32(rot))
        ang = np.arange(S, dtype=np.float32)[:, None] * f.astype(np.float32)[None, :]
        for fn, tag in ((np.cos, "cos"), (np.sin, "sin")):
            put(name + tag, fn(ang).reshape(T, P, rot // 2).transpose(1, 0, 2))

    rope(500000.0, A_ROT, "ra_")
    rope(500000.0, B_ROPE, "rb_")
    rope(10000.0, HEAD, "rr_")
    e = np.zeros((64, 2 * GRID_W + GRID_W - 1))
    for r in range(2):
        for m in range(REL_C):
            e[32 * r + m, GRID_W * r + GRID_W - 1 + NA_COLS - 1 - m] = 1.0
    put("hankel", e)
    c = i % GRID_W
    start = np.clip(c - NA_COLS // 2, 0, GRID_W - NA_COLS)
    j = np.arange(GRID_W)[None, :]
    put("window", np.where((j >= start[:, None]) & (j < start[:, None] + NA_COLS), 0.0, MASKED))
    for l in range(LEVELS):
        s = 1 << l
        jj, ii = i[:, None], i[None, :]
        put(f"level{l}", ((jj // (2 * s) == ii // (2 * s)) & (jj // s % 2 == 0) & (ii // s % 2 == 1)).astype(np.float32))
    return np.concatenate(cols, 1), at


def retention_decay():
    import numpy as np
    h = np.arange(RET_HEADS, dtype=np.float32)
    log_gamma = np.log1p(-np.exp2(-5.0 - h)).astype(np.float64)
    rel = np.arange(S)[None, :] - np.arange(P)[:, None]
    d = np.where(rel >= 0, np.exp(log_gamma[:, None, None] * np.maximum(rel, 0)), 0.0) * HEAD ** -0.5
    return np.ascontiguousarray(d.transpose(1, 0, 2).astype(np.float32))


class Signal:

    def __init__(self, sem):
        self.sem, self.seen = sem, {}

    def next(self, eng, k=1):
        self.seen[id(eng)] = self.seen.get(id(eng), 0) + k
        return self.seen[id(eng)]


class Use:

    def __init__(self, bank, n):
        self.bank, self.n = bank, n


class Plan:

    def __init__(self):
        self.uses = [0] * N_BANKS
        self.at = 0
        self.loads = [0] * 6
        self.slot = 0
        self.freed = [None] * 6

    def take(self, n=1):
        out = []
        for _ in range(n):
            out.append(Use(self.at, self.uses[self.at]))
            self.uses[self.at] += 1
            self.at = (self.at + 1) % N_BANKS
        return out

    def chunk(self, dmas=1):
        s = self.slot
        self.slot = (s + 1) % 4
        self.loads[s] += dmas
        return (s, self.loads[s], self.freed[s])


def build(nc, a, out, stages=99):
    table, where = shape_constants()
    ctx = ExitStack()
    with ctx:
        def sb(name, shape, dt=F32):
            return ctx.enter_context(nc.sbuf_tensor(name, shape, dt))

        def sem(name):
            return ctx.enter_context(nc.semaphore(name))

        ring = sb("ring", [P, 4, 8 * BANK])
        big = sb("big", [P, BIG])
        X = sb("X", [P, T, D])
        XH = sb("XH", [P, T, D])
        XT = sb("XT", [P, KD, S])
        const = sb("const", [P, table.shape[1]])
        lnp = sb("lnp", [P, 2, D])
        router = sb("router", [P, 2, KD, ROUTES])
        ba_w = sb("ba_w", [P, KD, 2 * GDN_HEADS])
        chan = sb("chan", [P, 560])
        bc = sb("bc", [P, 976])
        st = sb("st", [P, 640])
        ones = sb("ones", [P, P])
        rel_sb = sb("rel_sb", [64, C_HEADS * 2 * NA_ROWS])

        def k(name):
            o, w = where[name]
            return const[:, o:o + w]

        ident = k("ident")
        slots = [ring[:, i, :] for i in range(4)] + [big[:, 0:4096], big[:, 4096:8192]]

        psum = [ctx.enter_context(nc.psum_tensor(f"bank{i}", [P, BANK], F32)) for i in range(N_BANKS)]
        full = [sem(f"bank{i}_full") for i in range(N_BANKS)]
        drained = [sem(f"bank{i}_drained") for i in range(N_BANKS)]
        loaded = [sem(f"slot{i}_loaded") for i in range(6)]

        dve_done = Signal(sem("dve_done"))
        act_done = Signal(sem("act_done"))
        pool_done = Signal(sem("pool_done"))
        sig = {}

        def signal(name):
            if name not in sig:
                sig[name] = Signal(sem(name))
            return sig[name]

        def late(l, name):
            return signal(f"late{l}_{name}").sem

        def overflow(eng, waits=True):
            if waits:
                eng.wait_ge(signal("slots_ready").sem, signal("slots_ready").next(eng))
            return eng.value_load(n_over[0:1, 0:1], min_val=0, max_val=S)

        def ps(u):
            return psum[u.bank]

        plan = Plan()
        U, W = {}, {}

        def plan_linear(name, chunks, per_chunk=T, dmas=1):
            W[name], U[name] = [], []
            for _ in range(chunks):
                c = plan.chunk(dmas)
                u = plan.take(per_chunk)
                plan.freed[c[0]] = ("bank", u[-1])
                W[name].append(c)
                U[name].append(u)

        def plan_attention(name, groups, maps, outs, bias):
            U[name] = dict(qk=[None] * groups, bias=[None] * groups, s=[], t=[], o=[])
            n = groups * T
            u = U[name]

            def group(g):
                u["qk"][g] = plan.take(2)
                if bias:
                    u["bias"][g] = plan.take(4)

            group(0)
            for i in range(n + 2):
                if i < n:
                    u["s"].append(plan.take(maps))
                    if i % T == 2 and i // T + 1 < groups:
                        group(i // T + 1)
                if 1 <= i <= n:
                    u["t"].append(plan.take(outs))
                if i >= 2:
                    u["o"].append(plan.take(outs))

        def plan_moe(l):
            U[f"route{l}"] = plan.take(T + 1)
            base = list(plan.uses)
            U[f"moe{l}"] = base
            plan.freed[4] = plan.freed[5] = ("bank", U[f"route{l}"][0])
            W[f"moe{l}"] = (list(plan.loads), list(plan.freed))
            for b in range(7):
                plan.uses[b] += EXPERTS
            for s in range(6):
                plan.loads[s] += EXPERTS // 2
            for half in range(2):
                for j, b in enumerate((2, 3, 6)):
                    plan.freed[3 * half + j] = ("bank", Use(b, base[b] + EXPERTS - 2 + half))
            plan.slot = 0

        def plan_ffn(l):
            plan_linear(f"ffn{l}_up", KF // 2, 4, dmas=2)
            W[f"ffn{l}_down"] = [plan.chunk() for _ in range((KF + 3) // 4)]
            U[f"ffn{l}_down"] = plan.take(N_BANKS)
            n = (KF + 3) // 4
            for i, c in enumerate(W[f"ffn{l}_down"]):
                plan.freed[c[0]] = ("bank", U[f"ffn{l}_down"][-1]) if i == n - 1 else ("down", l * (n - 1) + i + 1)
            for i in range(4, n):
                c = W[f"ffn{l}_down"][i]
                W[f"ffn{l}_down"][i] = (c[0], c[1], ("down", l * (n - 1) + i - 3))

        U["x_T"] = plan.take(KD)
        U["chan"] = plan.take(2)
        U["rel"] = plan.take(1)
        plan_linear("even_in", 4)
        U["lat_T"] = plan.take(3)
        plan_linear("uq", 1, 2 * T)
        plan_linear("ukv", 1, 2 * T)
        plan_attention("A", A_HEADS, 2, 1, False)
        plan_attention("B", B_HEADS, 1, 1, False)
        U["o0_T"] = plan.take(KD)
        plan_linear("even_o", 2)
        U["ln10_T"] = plan.take(KD)
        plan_moe(0)
        U["ln20_T"] = plan.take(KD)
        plan_linear("qkv", 6)
        plan_attention("C", C_HEADS // 2, 2, 2, True)
        U["o1_T"] = plan.take(KD)
        plan_linear("odd_o", 2)
        U["ln11_T"] = plan.take(KD)
        plan_moe(1)
        U["rms0_T"] = plan.take(KD)
        plan_linear("mix_in", 8)
        U["ba"] = plan.take(1)
        U["l2"] = plan.take(2 * GDN_HEADS)
        U["ret"] = [dict(qk=plan.take(2), s=plan.take(T), o=plan.take(1)) for _ in range(RET_HEADS)]
        U["gdn"] = [dict(gc=plan.take(2), kk=plan.take(1), kq=plan.take(1), kt=plan.take(1), vt=plan.take(1),
                         inv=[plan.take(3 if l < LEVELS - 1 else 2) for l in range(LEVELS)], u=plan.take(1), w=plan.take(1), ws=plan.take(1),
                         o=plan.take(1), s=plan.take(1)) for _ in range(T)]
        U["y_T"] = plan.take(KD)
        plan_linear("mix_out", 2)
        U["rmsf0_T"] = plan.take(KD)
        plan_ffn(0)
        U["rms1_T"] = plan.take(KD)
        plan_linear("lru_in", 4)
        U["lru"] = [plan.take(2) for _ in range(KD)]
        plan_linear("lru_out", 2)
        U["rmsf1_T"] = plan.take(KD)
        plan_ffn(1)

        def carve(spec, base=0):
            views, o = {}, base
            for name, shape in spec:
                n = math.prod(shape)
                v = big[:, o:o + n]
                dims = [f"d{i}" for i in range(len(shape))]
                if len(shape) > 1:
                    v = v.rearrange(f"p ({' '.join(dims)}) -> p {' '.join(dims)}", **dict(zip(dims, shape)))
                views[name] = v
                o += n
            assert o <= BIG, (o, [s[0] for s in spec])
            return views

        E = carve([("H", (T, EVEN_IN)), ("KC", (T, B_HEADS, B_QK)), ("QKT", (2, 2, S)), ("p", (2, 2, S)), ("WT", (2, 1, T, P))])
        E["QB"] = XT[:, 0:6, :].rearrange("p a b -> p (a b)").rearrange("p (t h d) -> p t h d", t=T, h=B_HEADS)
        E["VB"] = lnp[:, :, :].rearrange("p a b -> p (a b)").rearrange("p (t h d) -> p t h d", t=T, h=B_HEADS)
        E["latT"] = E["p"].rearrange("p a b s -> p (a b) s")
        E["tmp"] = E["QKT"].rearrange("p a b s -> p (a b) s")
        C = carve([("H", (T, 3 * D)), ("QKT", (2, 2, S)), ("p", (2, 2, S))])
        C["WT"] = lnp[:, :, :].rearrange("p b (o t q) -> p b o t q", o=2, t=T)
        C["bias"] = XT[:, :, :].rearrange("p a b -> p (a b)").rearrange("p (b h s j) -> p b h s j", b=2, h=2, j=GRID_W)
        M = carve([("XE", (2, D)), ("XET", (2, KD, CAP)), ("hid", (2, D_EXPERT)), ("HT", (2, KE, CAP)), ("YE", (2, D))], 8192)
        M["lhid"] = big[:, 12288:12288 + D_EXPERT]
        M["lHT"] = big[:, 12800:12800 + KE * P].rearrange("p (k c) -> p k c", k=KE)
        M["YG"] = big[:, 8192:8192 + T * D].rearrange("p (t d) -> p t d", t=T)
        R = carve([("A", (T, TOP_K, EXPERTS)), ("tmp", (T, TOP_K, EXPERTS)), ("M", (T, EXPERTS)), ("L", (T, ROUTES)),
                   ("LP", (T, 8)), ("g8", (T, 8)), ("e8", (T, 8)), ("v8", (T, 8)), ("sel", (T, 8, GROUPS))], 15616)
        N_ = carve([("GR", (T, 512)), ("GD", (T, 512)), ("QKVT", (12, S)), ("VR", (T, 512)), ("RQK", (T, 1024))])
        N_["rt"] = XT[:, 0:4, :].rearrange("p a (h d) -> p a h d", d=HEAD // 2)
        N_["QKT"] = XT[:, 0:4, :].rearrange("p (b a) s -> p b a s", b=2)
        N_["sc"] = XT[:, 4:7, :].rearrange("p a s -> p (a s)")
        N_["dret"] = lnp[:, :, :].rearrange("p a b -> p (a b)").rearrange("p (h s) -> p h s", h=RET_HEADS)
        gdn_names = ("kg", "v", "ktail", "attnT", "InvT", "Inv", "LT", "dec", "eg", "ub", "wT", "qd")
        G = {n: big[:, 10752 + 512 * i:10752 + 512 * (i + 1)].rearrange("p (h c) -> p h c", h=GDN_HEADS)
             for i, n in enumerate(gdn_names)}
        for i, n in enumerate(("CT", "T1", "vn", "S", "sq", "rn", "gm", "t2")):
            G[n] = XT[:, i, :].rearrange("p (h c) -> p h c", h=GDN_HEADS)
        F_ = carve([("act", (KF, S)), ("cg", (2, S)), ("cv", (2, S))])
        L_ = carve([("gate", (KD, S)), ("xr", (KD, S)), ("i", (KD, S)), ("w", (2, KD, P)), ("q", (2, S)), ("a", (S,)), ("u", (S,))])
        xs = nc.dram_tensor("expert_rows", [EXPERTS * CAP, D], F32).ap()
        ys = nc.dram_tensor("expert_out", [EXPERTS * CAP, D], F32).ap()
        idx = sb("idx", [P, 2 * T * TOP_K], U32)
        n_over = sb("n_over", [1, 1], I32)
        chan_at, n_chan = {}, 0
        for name, rows in (("ln1_g", 16), ("ln1_b", 16), ("ln2_g", 16), ("ln2_b", 16), ("norm_mix_2", 16), ("norm_ffn_2", 16),
                           ("lru_conv_b_2", 8), ("lru_b_a_2", 8), ("lru_b_x_2", 8), ("lru_lambda_2", 8),
                           ("lru_conv_w_2", 32), ("gdn_conv_w_2", 48), ("ffn_conv_w_2", 6 * KF * 2), ("ffn_conv_b_2", 2 * KF * 2)):
            chan_at[name] = n_chan
            n_chan += rows
        bc_at, n_bc = {}, 0
        for name, n in (("even_subln_g", 128), ("even_q_norm_g", 256), ("even_kv_norm_g", 128), ("gdn_out_gain_2", 128),
                        ("even_lam_q1", 64), ("even_lam_k1", 64), ("even_lam_q2", 64), ("even_lam_k2", 64),
                        ("b_router_group", 8), ("b_router_expert", 64), ("gdn_a_log_2", 4), ("gdn_dt_bias_2", 4)):
            bc_at[name] = (n_bc, n)
            n_bc += n

        def bcv(name):
            o, n = bc_at[name]
            return bc[:, o:o + n]

        n_stat = [0]

        def stat(*shape):
            n = math.prod(shape)
            v = st[:, n_stat[0]:n_stat[0] + n]
            n_stat[0] += n
            assert n_stat[0] <= 640
            if len(shape) == 2:
                v = v.rearrange("p (a b) -> p a b", a=shape[0])
            if len(shape) == 3:
                v = v.rearrange("p (a b c) -> p a b c", a=shape[0], b=shape[1])
            return v

        def rep(ap, axis, n):
            ap = ap.unsqueeze(axis)
            shape = list(ap.shape)
            shape[axis] = n
            return ap.broadcast_to(shape)

        sums, negmax, rcp = stat(64), stat(64), stat(64)
        bnst, mv, rstd = stat(T, 2, 6), stat(T, 2), stat(32)
        ssq = stat(32)
        lam = stat(8)
        grp, gw, gsum, ediff = stat(T), stat(T), stat(T), stat(T)
        gdiff, ohg = stat(T, GROUPS), stat(T, GROUPS)
        ek, pos2, over, keep, slotf, wts, wtmp = (stat(T, TOP_K) for _ in range(7))
        gb = stat(T, 2 * GDN_HEADS)
        beta, gg = stat(T, GDN_HEADS), stat(T, GDN_HEADS)
        sp1, sp2, sp3, sp4 = (stat(T, GDN_HEADS) for _ in range(4))
        gcol8, ge8 = stat(2, GDN_HEADS), stat(2, GDN_HEADS)
        cvec, sl1, sl2, sl3 = (stat(KD) for _ in range(4))

        scat, gath = idx[:, 0:8], idx[:, 8:16]
        gidx = sums[:, 0:32].bitcast(U32).rearrange("p (t j) -> p t j", t=T)
        eidx = sums[:, 32:64].bitcast(U32).rearrange("p (t j) -> p t j", t=T)

        def col(name, i):
            return chan[:, chan_at[name] + i:chan_at[name] + i + 1]

        def slot_kn(s, nk=KD, n=BANK):
            return slots[s][:, 0:nk * n].rearrange("p (k n) -> p k n", k=nk)

        def on(n):
            return stages >= n

        sc_at = [sum(S - P * i for i in range(kc)) for kc in range(T)]

        att = {
            "A": dict(groups=A_HEADS, maps=2, outs=1, rows=A_DIM, scale=A_DIM ** -0.5, buf=E, dv=128,
                      q=lambda g, t: E["H"][:, t, 128 * g:128 * g + 128],
                      k=lambda g, t: E["H"][:, t, A_QKV + 128 * g:A_QKV + 128 * g + 128], width=128,
                      v=lambda g, o, kt: E["H"][:, kt, 2 * A_QKV + 128 * g:2 * A_QKV + 128 * g + 128],
                      o=lambda g, o, t: XH[:, t, 128 * g:128 * g + 128]),
            "B": dict(groups=B_HEADS, maps=1, outs=1, rows=B_QK, scale=B_QK ** -0.5, buf=E, dv=B_V,
                      q=lambda g, t: E["QB"][:, t, g, :], k=lambda g, t: E["KC"][:, t, g, :], width=B_QK,
                      v=lambda g, o, kt: E["VB"][:, kt, g, :],
                      o=lambda g, o, t: XH[:, t, 512 + B_V * g:512 + B_V * g + B_V]),
            "C": dict(groups=C_HEADS // 2, maps=2, outs=2, rows=C_DIM, scale=C_DIM ** -0.5, buf=C, dv=C_DIM,
                      q=lambda g, t: C["H"][:, t, 128 * g:128 * g + 128],
                      k=lambda g, t: C["H"][:, t, D + 128 * g:D + 128 * g + 128], width=128,
                      v=lambda g, o, kt: C["H"][:, kt, 2 * D + 128 * g + 64 * o:2 * D + 128 * g + 64 * o + 64],
                      o=lambda g, o, t: XH[:, t, 128 * g + 64 * o:128 * g + 64 * o + 64]),
        }

        block = ctx.enter_context(nc.Block())
        chan_dmas = []

        @block.sync
        def _(sp):
            def load(c, dst, src):
                slot, _, freed = c
                if freed is not None:
                    kind, by = freed
                    if kind == "bank":
                        sp.wait_ge(full[by.bank], by.n + 1)
                    else:
                        sp.wait_ge(signal("down_used").sem, by)
                sp.dma_start(dst, src).then_inc(loaded[slot], 16)

            def load_cols(name, w, n, nk=KD, width=BANK):
                v = w.rearrange("(k p) n -> p k n", p=P)
                for i, c in enumerate(W[name]):
                    m = min(width, n - i * width)
                    sp_dst = slot_kn(c[0], nk, width)[:, :, 0:m]
                    load(c, sp_dst, v[:, :, i * width:i * width + m])

            def load_experts(l):
                n0, freed = W[f"moe{l}"]
                base = U[f"moe{l}"]

                def expert(half, e, first):
                    for j, (name, b) in enumerate((("w_gate", 2), ("w_up", 3), ("w_down", 6))):
                        s = 3 * half + j
                        if first:
                            if freed[s] is not None:
                                sp.wait_ge(full[freed[s][1].bank], freed[s][1].n + 1)
                        else:
                            sp.wait_ge(full[b], e + (base[b] - 1))
                        src = a[name][l][e].rearrange("(k p) n -> p k n", p=P)
                        nk, n = (KE, D) if j == 2 else (KD, D_EXPERT)
                        sp.dma_start(slot_kn(s, nk, n), src).then_inc(loaded[s], 16)

                for half in range(2):
                    expert(half, half, True)
                with sp.Fori(1, EXPERTS // 2) as i:
                    for half in range(2):
                        expert(half, i * 2 + half, False)
                with sp.If(overflow(sp) > 0):
                    for b in (2, 3, 6):
                        sp.wait_ge(full[b], base[b] + EXPERTS)

                    def weights(e):
                        for j, name in enumerate(("w_gate", "w_up", "w_down")):
                            nk, n = (KE, D) if j == 2 else (KD, D_EXPERT)
                            sp.dma_start(slot_kn(j, nk, n), a[name][l][e].rearrange("(k p) n -> p k n", p=P)).then_inc(
                                late(l, "loaded"), 16)

                    weights(0)
                    with sp.Fori(1, EXPERTS) as e:
                        sp.wait_ge(late(l, "added"), e * T)
                        weights(e)
                    sp.wait_ge(late(l, "added"), EXPERTS * T)

            def load_ffn(l):
                up = a["ffn_w_up_2"][l].rearrange("(k p) (h n) -> p k h n", p=P, h=2)
                for i, c in enumerate(W[f"ffn{l}_up"]):
                    slot, _, freed = c
                    if freed is not None:
                        sp.wait_ge(full[freed[1].bank], freed[1].n + 1)
                    dst = slot_kn(slot).rearrange("p k (h n) -> p k h n", h=2)
                    for h in range(2):
                        sp.dma_start(dst[:, :, h, :], up[:, :, h, i * FF_COLS:(i + 1) * FF_COLS]).then_inc(loaded[slot], 16)
                down = a["ffn_w_down_2"][l].rearrange("(k p) n -> p k n", p=P)
                for i, c in enumerate(W[f"ffn{l}_down"]):
                    m = min(4, KF - 4 * i)
                    load(c, slot_kn(c[0], 4, D)[:, 0:m, :], down[:, 4 * i:4 * i + m, :])

            sp.dma_start(X[:, :, :], a["x"][0].rearrange("(t p) d -> p t d", p=P)).then_inc(signal("x_loaded").sem, 16)
            load_cols("even_in", a["even_w_in"][0], EVEN_IN)
            load_cols("uq", a["even_w_uq"][0], B_HEADS * B_QK, 2, B_HEADS * B_QK)
            load_cols("ukv", a["even_w_ukv"][0], B_HEADS * 128, 1, B_HEADS * 128)
            load_cols("even_o", a["even_w_o"][0], D)
            if on(4):
                load_experts(0)
            if on(5):
                load_cols("qkv", a["odd_w_qkv"][0], 3 * D)
                load_cols("odd_o", a["odd_w_o"][0], D)
            if on(6):
                load_experts(1)
            if on(7):
                load_cols("mix_in", a["ret_gdn_w_in_2"][0], 8 * BANK)
                load_cols("mix_out", a["ret_gdn_w_out_2"][0], D)
            if on(8):
                load_ffn(0)
            if on(9):
                load_cols("lru_in", a["lru_w_in_2"][0], 2 * D)
                load_cols("lru_out", a["lru_w_out_2"][0], D)
            if on(10):
                load_ffn(1)
            sp.wait_ge(signal("out_ready").sem, signal("out_ready").next(sp, T))
            sp.dma_start(out[0].rearrange("(t p) d -> p t d", p=P), XH[:, :, :]).then_inc(signal("out_stored").sem, 16)
            sp.wait_ge(signal("out_stored").sem, signal("out_stored").next(sp, 16))

        @block.gpsimd
        def _(pool):
            def power(dst, src, mul, add, ready, told):
                pool.wait_ge(signal(ready).sem, signal(ready).next(pool))
                pool.tensor_scalar(dst, src, mul, add, ALU.mult, ALU.add).then_inc(pool_done.sem, 1)
                pool.wait_ge(pool_done.sem, pool_done.next(pool))
                pool.tensor_tensor(dst, dst, k("minus_half").broadcast_to(list(dst.shape)), ALU.pow).then_inc(signal(told).sem, 1)
                pool.wait_ge(signal(told).sem, signal(told).next(pool))

            def layer_norm(g, b):
                power(rstd[:, 0:T], mv[:, :, 1], 1.0, LN_EPS, "ln_stats", "rstd_ready")
                for i, v in enumerate((g, b)):
                    pool.dma_start(lnp[:, i, :], v.partition_broadcast(P)).then_inc(signal("ln_loaded").sem, 16)
                pool.wait_ge(signal("ln_loaded").sem, signal("ln_loaded").next(pool, 32))
                for t in range(T):
                    pool.wait_ge(signal("xh_ready").sem, signal("xh_ready").next(pool))
                    pool.tensor_tensor(X[:, t, :], XH[:, t, :], lnp[:, 0, :], ALU.mult).then_inc(pool_done.sem, 1)
                    pool.wait_ge(pool_done.sem, pool_done.next(pool))
                    pool.tensor_tensor(X[:, t, :], X[:, t, :], lnp[:, 1, :], ALU.add).then_inc(signal("x_applied").sem, 1)
                    pool.wait_ge(signal("x_applied").sem, signal("x_applied").next(pool))

            def to_experts(l):
                pool.wait_ge(signal("slots_ready").sem, signal("slots_ready").next(pool))
                for t in range(T):
                    for j in range(TOP_K):
                        pool.indirect_dma_start(
                            xs, bass.IndirectOffsetOnAxis(ap=scat[:, TOP_K * t + j:TOP_K * t + j + 1], axis=0),
                            X[:, t, :], None, bounds_check=EXPERTS * CAP - 1, oob_is_err=False,
                        ).then_inc(signal("rows_sent").sem, 16)

            def from_experts(l):
                for half in range(2):
                    pool.wait_ge(signal(f"y_stored{half}").sem, 16 * (EXPERTS // 2) * (l + 1))
                for t in range(T):
                    for j, dst in enumerate((XH[:, t, :], M["YG"][:, t, :])):
                        pool.indirect_dma_start(
                            dst, None, ys, bass.IndirectOffsetOnAxis(ap=gath[:, TOP_K * t + j:TOP_K * t + j + 1], axis=0),
                        ).then_inc(signal("rows_back").sem, 16)

            pool.memset(lnp[:, 0, :], 0.0).then_inc(pool_done.sem, 1)
            pool.wait_ge(pool_done.sem, pool_done.next(pool))
            pool.dma_start(xs.rearrange("(n p) d -> p n d", p=P), rep(lnp[:, 0, :], 1, EXPERTS * CAP // P)).then_inc(
                signal("rows_zeroed").sem, 16)
            pool.memset(ones[:, :], 1.0).then_inc(signal("ones_ready").sem, 1)
            pool.wait_ge(signal("ones_ready").sem, signal("ones_ready").next(pool))
            pool.wait_ge(signal("table_loaded").sem, signal("table_loaded").next(pool, 16))
            pool.wait_ge(signal("lat_ssq").sem, signal("lat_ssq").next(pool))
            pool.tensor_scalar(rstd[:, 0:T], ssq[:, 0:T], 1.0 / B_Q_RANK, RMS_EPS, ALU.mult, ALU.add).then_inc(pool_done.sem, 1)
            pool.wait_ge(pool_done.sem, pool_done.next(pool))
            pool.tensor_scalar(rstd[:, T:2 * T], ssq[:, T:2 * T], 1.0 / B_KV_RANK, RMS_EPS, ALU.mult, ALU.add).then_inc(
                pool_done.sem, 1)
            pool.wait_ge(pool_done.sem, pool_done.next(pool))
            pool.tensor_tensor(rstd[:, 0:2 * T], rstd[:, 0:2 * T], k("minus_half").broadcast_to([P, 2 * T]), ALU.pow).then_inc(
                signal("rstd_ready").sem, 1)
            pool.wait_ge(signal("rstd_ready").sem, signal("rstd_ready").next(pool))
            if on(2):
                power(rstd[:, 0:16], ssq[:, 0:16], 1.0 / 128, RMS_EPS, "a_ssq", "rstd_ready")
            if on(3):
                layer_norm(a["ln1_g"][0], a["ln1_b"][0])
            if on(4):
                pool.wait_ge(signal("rows_zeroed").sem, signal("rows_zeroed").next(pool, 16))
                to_experts(0)
                from_experts(0)
                layer_norm(a["ln2_g"][0], a["ln2_b"][0])
            if on(5):
                layer_norm(a["ln1_g"][1], a["ln1_b"][1])
            if on(6):
                to_experts(1)
                from_experts(1)
                layer_norm(a["ln2_g"][1], a["ln2_b"][1])

            def rms():
                power(rstd[:, 0:T], ssq[:, 0:T], 1.0 / D, RMS_EPS, "x_ssq", "rstd_ready")

            if on(7):
                rms()
                power(rstd[:, 0:32], ssq[:, 0:32], 1.0 / 128, RMS_EPS, "y_ssq", "rstd_ready")
            if on(8):
                rms()
            if on(9):
                rms()
            if on(10):
                rms()
            if on(11):
                pool.dma_start(lnp[:, 0, :], a["norm_final_2"].partition_broadcast(P)).then_inc(signal("ln_loaded").sem, 16)
                rms()

        @block.scalar
        def _(act):
            def load(dst, src, name="small_loaded"):
                act.dma_start(dst, src).then_inc(signal(name).sem, 16)

            def transposed(name, dst=XT, gain=None, bias=None, gain_at=0):
                for i, u in enumerate(U[name]):
                    if gain is None:
                        act.wait_ge(full[u.bank], u.n + 1)
                        act.activation(dst[:, i, :], ps(u)[:, :], ACT.Copy).then_inc(drained[u.bank], 1)
                        act.wait_ge(drained[u.bank], u.n + 1)
                    elif bias is None:
                        act.wait_ge(full[u.bank], u.n + 1)
                        act.activation(dst[:, i, :], ps(u)[:, :], ACT.Copy, scale=col(gain, gain_at + i)).then_inc(
                            drained[u.bank], 1)
                        act.wait_ge(drained[u.bank], u.n + 1)
                    else:
                        act.wait_ge(full[u.bank], u.n + 1)
                        act.activation(dst[:, i, :], ps(u)[:, :], ACT.Identity, scale=col(gain, gain_at + i), bias=col(bias, gain_at + i)).then_inc(
                            drained[u.bank], 1)
                        act.wait_ge(drained[u.bank], u.n + 1)

            def linear(name, dst, n, width=BANK):
                for i, us in enumerate(U[name]):
                    m = min(width, n - i * width)
                    for t, u in enumerate(us):
                        act.wait_ge(full[u.bank], u.n + 1)
                        act.activation(dst[:, t, i * width:i * width + m], ps(u)[:, 0:m], ACT.Copy).then_inc(drained[u.bank], 1)
                        act.wait_ge(drained[u.bank], u.n + 1)

            def attention(name):
                c = att[name]
                u, buf, n = U[name], att[name]["buf"], att[name]["groups"] * T

                def group(g):
                    for j in range(2):
                        v = u["qk"][g][j]
                        act.wait_ge(full[v.bank], v.n + 1)
                        act.activation(buf["QKT"][0:c["width"], g % 2, j, :], ps(v)[0:c["width"], :], ACT.Copy).then_inc(
                            drained[v.bank], 1)
                        act.wait_ge(drained[v.bank], v.n + 1)

                group(0)
                for i in range(n + 1):
                    if i < n:
                        for m in range(c["maps"]):
                            s = i * c["maps"] + m
                            act.wait_ge(signal("max_ready").sem, signal("max_ready").next(act))
                            v = u["s"][i][m]
                            j = s % 64
                            if name == "C":
                                p = buf["p"][:, i % 2, m, :]
                                act.activation(p, p, ACT.Exp, bias=negmax[:, j:j + 1], accum_out=sums[:, j:j + 1]).then_inc(
                                    signal("exp_done").sem, 1)
                                act.wait_ge(signal("exp_done").sem, signal("exp_done").next(act))
                            else:
                                act.wait_ge(full[v.bank], v.n + 1)
                                act.activation(buf["p"][:, i % 2, m, :], ps(v)[:, :], ACT.Exp, bias=negmax[:, j:j + 1], scale=c["scale"], accum_out=sums[:, j:j + 1]).then_inc(
                                    drained[v.bank], 1)
                                act.wait_ge(drained[v.bank], v.n + 1)
                        if i % T == 2 and i // T + 1 < c["groups"]:
                            group(i // T + 1)
                    if i >= 1:
                        for o in range(c["outs"]):
                            if i >= 3:
                                act.wait_ge(full[u["o"][i - 3][o].bank], u["o"][i - 3][o].n + 1)
                            v = u["t"][i - 1][o]
                            act.wait_ge(full[v.bank], v.n + 1)
                            act.activation(buf["WT"][:, (i - 1) % 2, o, :, :].rearrange("p t q -> p (t q)"), ps(v)[:, :], ACT.Copy).then_inc(
                                drained[v.bank], 1)
                            act.wait_ge(drained[v.bank], v.n + 1)

            def route(l):
                act.wait_ge(signal("gdiff").sem, signal("gdiff").next(act))
                act.activation(gdiff, gdiff, ACT.Exp).then_inc(signal("gexp").sem, 1)
                act.wait_ge(signal("gexp").sem, signal("gexp").next(act))
                act.wait_ge(signal("ediff").sem, signal("ediff").next(act))
                act.activation(ediff, ediff, ACT.Exp).then_inc(signal("eexp").sem, 1)
                act.wait_ge(signal("eexp").sem, signal("eexp").next(act))

            def experts(l):
                base = U[f"moe{l}"]

                def wait_use(sems, b, e):
                    act.wait_ge(sems[b], e + (base[b] + 1))

                def load_rows(e, half):
                    act.dma_start(M["XE"][0:CAP, half, :], xs.rearrange("(e c) d -> e c d", c=CAP)[e]).then_inc(
                        signal(f"rows_loaded{half}").sem, 16)

                def rows_T(e, half):
                    for b in range(2):
                        wait_use(full, b, e)
                        act.activation(M["XET"][:, half, 4 * b:4 * b + 4, :].rearrange("p k c -> p (k c)"),
                                       psum[b][:, 0:4 * CAP], ACT.Copy).then_inc(drained[b], 1)

                def silu(e, half):
                    wait_use(full, 2, e)
                    act.activation(M["hid"][0:CAP, half, :], psum[2][0:CAP, :], ACT.Silu).then_inc(drained[2], 1)

                def out_rows(e, half, n, checked):
                    if checked:
                        act.wait_ge(signal(f"y_stored{half}").sem, n * 16 + 16 * (EXPERTS // 2) * l)
                    wait_use(full, 5, e)
                    act.activation(M["YE"][0:CAP, half, 0:BANK], psum[5][0:CAP, :], ACT.Copy).then_inc(drained[5], 1)
                    wait_use(drained, 5, e)
                    wait_use(drained, 6, e)
                    act.dma_start(ys.rearrange("(e c) d -> e c d", c=CAP)[e], M["YE"][0:CAP, half, :]).then_inc(
                        signal(f"y_stored{half}").sem, 16)

                def stage(e, half, n, first=False, last=False, load=True, checked=True):
                    silu(e, half)
                    if not last:
                        rows_T(e + 1, 1 - half)
                    if load:
                        load_rows(e + 3, 1 - half)
                    if not first:
                        out_rows(e - 1, 1 - half, n - 1 + half, checked)

                act.wait_ge(signal("rows_sent").sem, signal("rows_sent").next(act, 16 * T * TOP_K))
                load_rows(0, 0)
                load_rows(1, 1)
                rows_T(0, 0)
                load_rows(2, 0)
                stage(0, 0, 0, first=True)
                stage(1, 1, 0, checked=l > 0)
                stage(2, 0, 1, checked=l > 0)
                with act.Fori(1, EXPERTS // 2 - 2) as i:
                    stage(i * 2 + 1, 1, i)
                    stage(i * 2 + 2, 0, i + 1)
                h = EXPERTS // 2 - 2
                stage(2 * h + 1, 1, h, load=False)
                stage(2 * h + 2, 0, h + 1, load=False)
                stage(2 * h + 3, 1, h + 1, load=False, last=True)
                out_rows(EXPERTS - 1, 1, EXPERTS // 2 - 1, True)
                with act.If(overflow(act) > 0):
                    with act.Fori(0, EXPERTS) as i:
                        for t in range(T):
                            act.wait_ge(late(l, "up"), i * T + (t + 1))
                            act.activation(M["lhid"], psum[0][:, :], ACT.Silu).then_inc(late(l, "silu"), 1)
                    act.wait_ge(late(l, "added"), EXPERTS * T)

            def squares(uses):
                for us in uses:
                    for v in us:
                        act.wait_ge(drained[v.bank], v.n + 1)
                for t in range(T):
                    ins = act.activation(XH[:, t, :], X[:, t, :], ACT.Square, accum_out=ssq[:, t:t + 1])
                    if t == T - 1:
                        ins.then_inc(signal("x_ssq").sem, 1)
                        act.wait_ge(signal("x_ssq").sem, signal("x_ssq").next(act))
                    else:
                        ins.then_inc(act_done.sem, 1)
                        act.wait_ge(act_done.sem, act_done.next(act))

            def ffn(l):
                for us in U[f"ffn{l}_up"]:
                    for m in range(2):
                        act.wait_ge(drained[us[2 * m].bank], us[2 * m].n + 1)
                        cg = F_["cg"][:, m, :]
                        act.activation(cg, cg, ACT.Silu).then_inc(signal("ff_silu").sem, 1)
                        act.wait_ge(signal("ff_silu").sem, signal("ff_silu").next(act))

            load(const[:, :], a["shape_table"], "table_loaded")
            n = n_dma = 0
            for name in chan_at:
                v = a[name]
                v = v.rearrange("(r c) -> r c", c=P) if len(v.shape) == 1 else (
                    v.rearrange("l (r c) -> (l r) c", c=P) if len(v.shape) == 2 else v.rearrange("l w (r c) -> (l w r) c", c=P))
                done = 0
                while done < v.shape[0]:
                    r = min(v.shape[0] - done, P - n % P)
                    load(XH[n % P:n % P + r, 0, (n // P) * P:(n // P + 1) * P], v[done:done + r, :], "chan_loaded")
                    done += r
                    n += r
                    n_dma += 1
            rel_rows = a["odd_rel_bias"][0].rearrange("(q h) r c -> q (h r) c", q=2)
            for q in range(2):
                load(XH[0:C_HEADS * REL_R // 2, 1, q * REL_C:(q + 1) * REL_C], rel_rows[q], "chan_loaded")
            chan_dmas.append(n_dma + 2)
            for name in bc_at:
                v = a[name]
                if len(v.shape) == 2:
                    v = v.rearrange("a b -> (a b)")
                load(bcv(name), v.partition_broadcast(P))
            for l in range(2):
                load(router[:, l, :, 0:GROUPS], a["w_router_group"][l].rearrange("(k p) n -> p k n", p=P))
                load(router[:, l, :, GROUPS:ROUTES], a["w_router_expert"][l].rearrange("(k p) n -> p k n", p=P))
            load(ba_w[:, :, :], a["ret_gdn_w_in_2"][0].rearrange("(k p) n -> p k n", p=P)[:, :, 8 * BANK:MIX0_IN])
            transposed("x_T")
            act.wait_ge(full[U["chan"][0].bank], U["chan"][0].n + 1)
            act.activation(chan[:, 0:512], ps(U["chan"][0])[:, :], ACT.Copy).then_inc(drained[U["chan"][0].bank], 1)
            act.wait_ge(drained[U["chan"][0].bank], U["chan"][0].n + 1)
            act.wait_ge(full[U["chan"][1].bank], U["chan"][1].n + 1)
            act.activation(chan[:, 512:n_chan], ps(U["chan"][1])[:, 0:n_chan - 512], ACT.Copy).then_inc(
                drained[U["chan"][1].bank], 1)
            act.wait_ge(drained[U["chan"][1].bank], U["chan"][1].n + 1)
            linear("even_in", E["H"], EVEN_IN)
            act.wait_ge(signal("small_loaded").sem, signal("small_loaded").next(act, 16 * (len(bc_at) + 5)))
            for j, (o, w) in enumerate(((3 * A_QKV, B_Q_RANK), (3 * A_QKV + B_Q_RANK, B_KV_RANK))):
                for t in range(T):
                    ins = act.activation(E["tmp"][:, 0, 0:w], E["H"][:, t, o:o + w], ACT.Square,
                                         accum_out=ssq[:, j * T + t:j * T + t + 1])
                    if j == 1 and t == T - 1:
                        ins.then_inc(signal("lat_ssq").sem, 1)
                        act.wait_ge(signal("lat_ssq").sem, signal("lat_ssq").next(act))
                    else:
                        ins.then_inc(act_done.sem, 1)
                        act.wait_ge(act_done.sem, act_done.next(act))
            act.wait_ge(signal("lam_dots").sem, signal("lam_dots").next(act))
            act.activation(lam[:, 0:2], lam[:, 0:2], ACT.Exp).then_inc(signal("lam_exp").sem, 1)
            act.wait_ge(signal("lam_exp").sem, signal("lam_exp").next(act))
            transposed("lat_T", E["latT"])
            act.wait_ge(signal("rows_zeroed").sem, signal("rows_zeroed").next(act, 16))
            for t in range(T):
                for j in range(2):
                    u = U["uq"][0][2 * t + j]
                    act.wait_ge(full[u.bank], u.n + 1)
                    act.activation(E["QB"][:, t, 4 * j:4 * j + 4, :], ps(u)[:, 0:4 * B_QK].rearrange("p (h d) -> p h d", h=4), ACT.Copy).then_inc(
                        drained[u.bank], 1)
                    act.wait_ge(drained[u.bank], u.n + 1)
            for t in range(T):
                for j in range(2):
                    u = U["ukv"][0][2 * t + j]
                    kv = ps(u)[:, :].rearrange("p (h d) -> p h d", h=4)
                    act.wait_ge(full[u.bank], u.n + 1)
                    act.activation(E["KC"][:, t, 4 * j:4 * j + 4, 0:B_NOPE], kv[:, :, 0:B_NOPE], ACT.Copy).then_inc(act_done.sem, 1)
                    act.wait_ge(act_done.sem, act_done.next(act))
                    act.activation(E["VB"][:, t, 4 * j:4 * j + 4, :], kv[:, :, B_NOPE:], ACT.Copy).then_inc(drained[u.bank], 1)
                    act.wait_ge(drained[u.bank], u.n + 1)
            if on(2):
                attention("A")
                attention("B")
                transposed("o0_T")
            if on(3):
                transposed("ln10_T", gain="ln1_g", bias="ln1_b")
            if on(4):
                route(0)
                experts(0)
                transposed("ln20_T", gain="ln2_g", bias="ln2_b")
            if on(5):
                linear("qkv", C["H"], 3 * D)
                act.wait_ge(signal("x_applied").sem, signal("x_applied").next(act, 2 * T))
                attention("C")
                transposed("o1_T")
                transposed("ln11_T", gain="ln1_g", bias="ln1_b", gain_at=KD)
            if on(6):
                route(1)
                experts(1)
            if on(7):
                act.wait_ge(signal("x_applied").sem, signal("x_applied").next(act, 2 * T))
                load(N_["dret"], a["retention_decay"], "decay_loaded")
                squares([])
                transposed("rms0_T", gain="norm_mix_2")
                for i in range(8):
                    us = U["mix_in"][i]
                    if i in (4, 5, 6):
                        for m, u in enumerate(us):
                            act.wait_ge(drained[u.bank], u.n + 1)
                            v = N_["QKVT"][:, 4 * (i - 4) + m, :]
                            act.activation(v, v, ACT.Silu).then_inc(signal("conv_silu").sem, 1)
                            act.wait_ge(signal("conv_silu").sem, signal("conv_silu").next(act))
                        continue
                    dst = {0: N_["RQK"][:, :, 0:512], 1: N_["RQK"][:, :, 512:1024], 2: N_["VR"], 3: N_["GR"], 7: N_["GD"]}[i]
                    for t, u in enumerate(us):
                        act.wait_ge(full[u.bank], u.n + 1)
                        act.activation(dst[:, t, :], ps(u)[:, :], ACT.Silu if i in (3, 7) else ACT.Copy).then_inc(
                            drained[u.bank], 1)
                        act.wait_ge(drained[u.bank], u.n + 1)
                act.wait_ge(signal("ab_ready").sem, signal("ab_ready").next(act))
                act.activation(beta, gb[:, :, 0:GDN_HEADS], ACT.Tanh, scale=0.5).then_inc(act_done.sem, 1)
                act.wait_ge(act_done.sem, act_done.next(act))
                act.activation(sp1, sp1, ACT.Exp, scale=-1.0).then_inc(act_done.sem, 1)
                act.wait_ge(act_done.sem, act_done.next(act))
                act.activation(lam[:, 4:8], bcv("gdn_a_log_2"), ACT.Exp).then_inc(signal("ab_exp").sem, 1)
                act.wait_ge(signal("ab_exp").sem, signal("ab_exp").next(act))
                act.wait_ge(signal("ln_arg").sem, signal("ln_arg").next(act))
                act.activation(sp3, sp2, ACT.Ln).then_inc(signal("ln_done").sem, 1)
                act.wait_ge(signal("ln_done").sem, signal("ln_done").next(act))
                for i in range(2 * GDN_HEADS):
                    if i >= 2:
                        act.wait_ge(full[U["l2"][i - 2].bank], U["l2"][i - 2].n + 1)
                    else:
                        act.wait_ge(full[U["ba"][0].bank], U["ba"][0].n + 1)
                    act.activation(G[("sq", "gm")[i % 2]].rearrange("p h c -> p (h c)"), N_["QKVT"][:, i, :], ACT.Square).then_inc(
                        signal("l2_square").sem, 1)
                    act.wait_ge(signal("l2_square").sem, signal("l2_square").next(act))
                for i, u in enumerate(U["l2"]):
                    if i >= 2:
                        act.wait_ge(signal("l2_normed").sem, signal("l2_normed").next(act))
                    act.wait_ge(full[u.bank], u.n + 1)
                    act.activation(G[("rn", "t2")[i % 2]].rearrange("p h c -> p (h c)"), ps(u)[:, :], ACT.Sqrt, bias=k("eps")).then_inc(
                        drained[u.bank], 1)
                    act.wait_ge(drained[u.bank], u.n + 1)
                for h in range(RET_HEADS):
                    for j in range(2):
                        u = U["ret"][h]["qk"][j]
                        act.wait_ge(full[u.bank], u.n + 1)
                        act.activation(N_["QKT"][:, h % 2, j, :], ps(u)[:, :], ACT.Copy).then_inc(drained[u.bank], 1)
                        act.wait_ge(drained[u.bank], u.n + 1)
                for t in range(T):
                    g = U["gdn"][t]
                    act.wait_ge(signal("dec_raw").sem, signal("dec_raw").next(act))
                    act.activation(G["eg"], ps(g["gc"][0])[:, :].rearrange("p (h c) -> p h c", h=GDN_HEADS), ACT.Exp).then_inc(
                        drained[g["gc"][0].bank], 1)
                    act.wait_ge(drained[g["gc"][0].bank], g["gc"][0].n + 1)
                    act.activation(ge8, gcol8, ACT.Exp).then_inc(act_done.sem, 1)
                    act.wait_ge(act_done.sem, act_done.next(act))
                    act.activation(G["dec"], G["dec"], ACT.Exp).then_inc(signal("dec_exp").sem, 1)
                    act.wait_ge(signal("dec_exp").sem, signal("dec_exp").next(act))
                    act.wait_ge(full[g["vt"][0].bank], g["vt"][0].n + 1)
                    act.activation(G["v"], ps(g["vt"][0])[:, :].rearrange("p (h c) -> p h c", h=GDN_HEADS), ACT.Copy).then_inc(
                        drained[g["vt"][0].bank], 1)
                    act.wait_ge(drained[g["vt"][0].bank], g["vt"][0].n + 1)
                    for l in range(LEVELS):
                        u = g["inv"][l][0]
                        act.wait_ge(full[u.bank], u.n + 1)
                        act.activation(G["T1"], ps(u)[:, :].rearrange("p (h c) -> p h c", h=GDN_HEADS), ACT.Copy).then_inc(
                            drained[u.bank], 1)
                        act.wait_ge(drained[u.bank], u.n + 1)
                    u = g["w"][0]
                    act.wait_ge(full[u.bank], u.n + 1)
                    act.activation(G["wT"], ps(u)[:, :].rearrange("p (h c) -> p h c", h=GDN_HEADS), ACT.Copy).then_inc(
                        drained[u.bank], 1)
                    act.wait_ge(drained[u.bank], u.n + 1)
                    u = g["o"][0]
                    act.wait_ge(full[u.bank], u.n + 1)
                    act.activation(XH[:, t, 512:1024], ps(u)[:, :], ACT.Copy).then_inc(drained[u.bank], 1)
                    act.wait_ge(drained[u.bank], u.n + 1)
                transposed("y_T")
            if on(8):
                squares(U["mix_out"])
                transposed("rmsf0_T", gain="norm_ffn_2")
                ffn(0)
            if on(9):
                squares([U["ffn0_down"]])
                act.wait_ge(signal("lam_arg").sem, signal("lam_arg").next(act))
                act.activation(sl1, sl1, ACT.Exp, scale=-1.0).then_inc(signal("lam_e").sem, 1)
                act.wait_ge(signal("lam_e").sem, signal("lam_e").next(act))
                act.wait_ge(signal("lam_w").sem, signal("lam_w").next(act))
                act.activation(sl3, sl2, ACT.Ln).then_inc(signal("lam_ln").sem, 1)
                act.wait_ge(signal("lam_ln").sem, signal("lam_ln").next(act))
                transposed("rms1_T", gain="norm_mix_2", gain_at=KD)
                for i in range(2):
                    for m, u in enumerate(U["lru_in"][i]):
                        act.wait_ge(full[u.bank], u.n + 1)
                        act.activation(L_["gate"][:, 4 * i + m, :], ps(u)[:, :], ACT.Gelu_apprx_tanh).then_inc(drained[u.bank], 1)
                        act.wait_ge(drained[u.bank], u.n + 1)
                for i, v in enumerate((a["lru_w_a_2"], a["lru_w_x_2"])):
                    load(L_["w"][:, i, :, :], v[0].rearrange("n i j -> i n j"), "gates_loaded")
                for m in range(KD):
                    ur, ui = U["lru"][m]
                    r = XT[:, m, :]
                    act.wait_ge(full[ur.bank], ur.n + 1)
                    act.activation(r, ps(ur)[:, :], ACT.Sigmoid, bias=col("lru_b_a_2", m)).then_inc(drained[ur.bank], 1)
                    act.wait_ge(drained[ur.bank], ur.n + 1)
                    act.wait_ge(full[ui.bank], ui.n + 1)
                    act.activation(L_["i"][:, m, :], ps(ui)[:, :], ACT.Sigmoid, bias=col("lru_b_x_2", m)).then_inc(
                        drained[ui.bank], 1)
                    act.wait_ge(drained[ui.bank], ui.n + 1)
                    if m == 0:
                        act.wait_ge(signal("cvec_ready").sem, signal("cvec_ready").next(act))
                    act.activation(r, r, ACT.Tanh, scale=cvec[:, m:m + 1]).then_inc(signal("lru_tanh").sem, 1)
                    act.wait_ge(signal("lru_tanh").sem, signal("lru_tanh").next(act))
                for m in range(KD):
                    if m >= 2:
                        act.wait_ge(signal("lru_y").sem, signal("lru_y").next(act))
                    act.activation(L_["q"][:, m % 2, :], XT[:, m, :], ACT.Sqrt, scale=-1.0).then_inc(signal("lru_root").sem, 1)
                    act.wait_ge(signal("lru_root").sem, signal("lru_root").next(act))
            if on(10):
                squares(U["lru_out"])
                transposed("rmsf1_T", gain="norm_ffn_2", gain_at=KD)
                ffn(1)
            if on(11):
                squares([U["ffn1_down"]])

        @block.tensor
        def _(pe):
            def turn(name, src, told, per_tile=True):
                if told is not None:
                    pe.wait_ge(signal(told).sem, signal(told).next(pe, T))
                for i, u in enumerate(U[name]):
                    if u.n:
                        pe.wait_ge(drained[u.bank], u.n)
                    for t in range(T):
                        ins = pe.transpose(ps(u)[:, t * P:(t + 1) * P], src[:, t, i * P:(i + 1) * P], ident)
                    ins.then_inc(full[u.bank], 1)

            def ready(name):
                for u in U[name]:
                    pe.wait_ge(drained[u.bank], u.n + 1)

            def arrived(c):
                slot, n, _ = c
                pe.wait_ge(loaded[slot], 16 * n)
                return slot

            def linear(name, n, nk=KD, width=BANK, split=1, src=XT):
                for i, (c, us) in enumerate(zip(W[name], U[name])):
                    w = slot_kn(arrived(c), nk, width)
                    m = min(width, n - i * width) // split
                    for q, u in enumerate(us):
                        t, h = divmod(q, split)
                        if u.n:
                            pe.wait_ge(drained[u.bank], u.n)
                        for kk in range(nk):
                            ins = pe.matmul(ps(u)[:, 0:m], src[:, kk, t * P:(t + 1) * P], w[:, kk, h * m:h * m + m],
                                            start=(kk == 0), stop=(kk == nk - 1))
                        ins.then_inc(full[u.bank], 1)

            def linear_T(c, us, tiles):
                w = slot_kn(arrived(c))
                for u, m in zip(us, tiles):
                    if u.n:
                        pe.wait_ge(drained[u.bank], u.n)
                    for kk in range(KD):
                        ins = pe.matmul(ps(u)[:, :], w[:, kk, m * P:(m + 1) * P], XT[:, kk, :], start=(kk == 0), stop=(kk == KD - 1))
                    ins.then_inc(full[u.bank], 1)

            def attention(name):
                c = att[name]
                u, buf, n, w = U[name], c["buf"], c["groups"] * T, c["width"]

                def group(g):
                    for j, src in enumerate((c["q"], c["k"])):
                        v = u["qk"][g][j]
                        if v.n:
                            pe.wait_ge(drained[v.bank], v.n)
                        for t in range(T):
                            ins = pe.transpose(ps(v)[0:w, t * P:(t + 1) * P], src(g, t), ident)
                        ins.then_inc(full[v.bank], 1)
                    if name == "C":
                        for j4, v in enumerate(u["bias"][g]):
                            if v.n:
                                pe.wait_ge(drained[v.bank], v.n)
                            for jj in range(16):
                                j = 16 * j4 + jj
                                sel = k("hankel")[0:64, GRID_W - 1 - j:GRID_W - 1 - j + P]
                                ins = pe.matmul(ps(v)[:, 32 * jj:32 * jj + 32], sel, rel_sb[0:64, 32 * g:32 * g + 32],
                                                start=True, stop=True)
                            ins.then_inc(full[v.bank], 1)

                group(0)
                for i in range(n + 2):
                    g, t = divmod(i, T)
                    if i < n:
                        if t == 0:
                            for v in u["qk"][g]:
                                pe.wait_ge(drained[v.bank], v.n + 1)
                        for m in range(c["maps"]):
                            v = u["s"][i][m]
                            if v.n:
                                pe.wait_ge(drained[v.bank], v.n)
                            r = slice(c["rows"] * m, c["rows"] * (m + 1))
                            ins = pe.matmul(ps(v)[:, :], buf["QKT"][r, g % 2, 0, t * P:(t + 1) * P], buf["QKT"][r, g % 2, 1, :],
                                            start=True, stop=True)
                            ins.then_inc(full[v.bank], 1)
                        if t == 2 and g + 1 < c["groups"]:
                            group(g + 1)
                    if 1 <= i <= n:
                        for o in range(c["outs"]):
                            v = u["t"][i - 1][o]
                            if name == "A":
                                pe.wait_ge(signal("mixed").sem, signal("mixed").next(pe))
                            elif name == "B":
                                pe.wait_ge(drained[u["s"][i - 1][o].bank], u["s"][i - 1][o].n + 1)
                            else:
                                pe.wait_ge(signal("exp_done").sem, signal("exp_done").next(pe))
                            if v.n:
                                pe.wait_ge(drained[v.bank], v.n)
                            for kt in range(T):
                                ins = pe.transpose(ps(v)[:, kt * P:(kt + 1) * P], buf["p"][:, (i - 1) % 2, o, kt * P:(kt + 1) * P], ident)
                            ins.then_inc(full[v.bank], 1)
                    if i >= 2:
                        for o in range(c["outs"]):
                            pe.wait_ge(drained[u["t"][i - 2][o].bank], u["t"][i - 2][o].n + 1)
                            v = u["o"][i - 2][o]
                            if v.n:
                                pe.wait_ge(drained[v.bank], v.n)
                            for kt in range(T):
                                ins = pe.matmul(ps(v)[:, 0:c["dv"]], buf["WT"][:, (i - 2) % 2, o, kt, :], c["v"]((i - 2) // T, o, kt),
                                                start=(kt == 0), stop=(kt == T - 1))
                            ins.then_inc(full[v.bank], 1)

            def experts(l):
                base = U[f"moe{l}"]
                n0 = W[f"moe{l}"][0]
                us = U[f"route{l}"]
                for t in range(T):
                    if us[t].n:
                        pe.wait_ge(drained[us[t].bank], us[t].n)
                    for kk in range(KD):
                        ins = pe.matmul(ps(us[t])[:, 0:ROUTES], XT[:, kk, t * P:(t + 1) * P], router[:, l, kk, :],
                                        start=(kk == 0), stop=(kk == KD - 1))
                    ins.then_inc(full[us[t].bank], 1)
                u = us[T]
                if u.n:
                    pe.wait_ge(drained[u.bank], u.n)
                pe.wait_ge(signal("chosen").sem, signal("chosen").next(pe))
                for t in range(T):
                    for b in range(t):
                        pe.matmul(ps(u)[:, t * EXPERTS:(t + 1) * EXPERTS], ones[:, :], R["M"][:, b, :], start=(b == 0), stop=False)
                    pe.matmul(ps(u)[:, t * EXPERTS:(t + 1) * EXPERTS], k("before"), R["M"][:, t, :], start=(t == 0), stop=True)
                for t in range(T):
                    ins = pe.matmul(ps(u)[:, T * EXPERTS:(T + 1) * EXPERTS], ones[:, :], R["M"][:, t, :], start=(t == 0), stop=(t == T - 1))
                ins.then_inc(full[u.bank], 1)

                def wait_use(sems, b, e, more=0):
                    pe.wait_ge(sems[b], e + (base[b] + more))

                def rows_T(e, half, n):
                    pe.wait_ge(signal(f"rows_loaded{half}").sem, n * 16 + 16 * (1 + EXPERTS // 2 * l))
                    for b in range(2):
                        wait_use(drained, b, e)
                        for j in range(4):
                            kk = 4 * b + j
                            ins = pe.transpose(psum[b][:, j * CAP:(j + 1) * CAP], M["XE"][0:CAP, half, kk * P:(kk + 1) * P], ident[0:CAP, 0:CAP])
                        ins.then_inc(full[b], 1)

                def up(e, half, n):
                    for b in range(2):
                        wait_use(drained, b, e, 1)
                    for j, b in enumerate((2, 3)):
                        s = 3 * half + j
                        pe.wait_ge(loaded[s], n * 16 + 16 * (n0[s] + 1))
                        wait_use(drained, b, e)
                        w = slot_kn(s)
                        for kk in range(KD):
                            ins = pe.matmul(psum[b][0:CAP, :], M["XET"][:, half, kk, :], w[:, kk, :], start=(kk == 0), stop=(kk == KD - 1))
                        ins.then_inc(full[b], 1)

                def hidden_T(e, half):
                    wait_use(drained, 3, e, 1)
                    wait_use(drained, 4, e)
                    for kk in range(KE):
                        ins = pe.transpose(psum[4][:, kk * CAP:(kk + 1) * CAP], M["hid"][0:CAP, half, kk * P:(kk + 1) * P], ident[0:CAP, 0:CAP])
                    ins.then_inc(full[4], 1)

                def down(e, half, n):
                    s = 3 * half + 2
                    pe.wait_ge(loaded[s], n * 16 + 16 * (n0[s] + 1))
                    wait_use(drained, 4, e, 1)
                    w = slot_kn(s, KE, D)
                    for j, b in enumerate((5, 6)):
                        wait_use(drained, b, e)
                        for kk in range(KE):
                            ins = pe.matmul(psum[b][0:CAP, :], M["HT"][:, half, kk, :], w[:, kk, j * BANK:(j + 1) * BANK],
                                            start=(kk == 0), stop=(kk == KE - 1))
                        ins.then_inc(full[b], 1)

                def stage(e, half, n, first=False, last=False):
                    up(e, half, n)
                    if not last:
                        rows_T(e + 1, 1 - half, n + half)
                    if not first:
                        down(e - 1, 1 - half, n - 1 + half)
                    hidden_T(e, half)

                rows_T(0, 0, 0)
                stage(0, 0, 0, first=True)
                with pe.Fori(0, EXPERTS // 2 - 1) as i:
                    stage(i * 2 + 1, 1, i)
                    stage(i * 2 + 2, 0, i + 1)
                stage(EXPERTS - 1, 1, EXPERTS // 2 - 1, last=True)
                down(EXPERTS - 1, 1, EXPERTS // 2 - 1)
                with pe.If(overflow(pe) > 0):
                    for b in range(7):
                        pe.wait_ge(drained[b], base[b] + EXPERTS)

                    def late_tile(e, t, first=False):
                        if not first:
                            pe.wait_ge(late(l, "added"), e * T + t)
                        for j in range(2):
                            w = slot_kn(j)
                            for kk in range(KD):
                                ins = pe.matmul(psum[j][:, :], XT[:, kk, t * P:(t + 1) * P], w[:, kk, :], start=(kk == 0), stop=(kk == KD - 1))
                        ins.then_inc(late(l, "up"), 1)
                        pe.wait_ge(late(l, "hidden"), e * T + (t + 1))
                        for kk in range(KE):
                            ins = pe.transpose(psum[2][:, kk * P:(kk + 1) * P], M["lhid"][:, kk * P:(kk + 1) * P], ident)
                        ins.then_inc(late(l, "turned"), 1)
                        pe.wait_ge(late(l, "hidden_T"), e * T + (t + 1))
                        w = slot_kn(2, KE, D)
                        for j in range(2):
                            for kk in range(KE):
                                ins = pe.matmul(psum[3 + j][:, :], M["lHT"][:, kk, :], w[:, kk, j * BANK:(j + 1) * BANK],
                                                start=(kk == 0), stop=(kk == KE - 1))
                        ins.then_inc(late(l, "down"), 1)

                    pe.wait_ge(late(l, "loaded"), 16 * 3)
                    for t in range(T):
                        late_tile(0, t, first=(t == 0))
                    with pe.Fori(1, EXPERTS) as e:
                        pe.wait_ge(late(l, "loaded"), e * 48 + 48)
                        for t in range(T):
                            late_tile(e, t)
                    pe.wait_ge(late(l, "added"), EXPERTS * T)

            def ffn(l):
                for i, (c, us) in enumerate(zip(W[f"ffn{l}_up"], U[f"ffn{l}_up"])):
                    linear_T(c, us, (0, 2, 1, 3))
                pe.wait_ge(signal("ff_act").sem, signal("ff_act").next(pe, KF))
                us = U[f"ffn{l}_down"]
                for i, c in enumerate(W[f"ffn{l}_down"]):
                    w = slot_kn(arrived(c), 4, D)
                    m = min(4, KF - 4 * i)
                    for q, u in enumerate(us):
                        t, h = divmod(q, 2)
                        if i == 0:
                            if u.n:
                                pe.wait_ge(drained[u.bank], u.n)
                        for kk in range(m):
                            f = 4 * i + kk
                            ins = pe.matmul(ps(u)[:, :], F_["act"][:, f, t * P:(t + 1) * P], w[:, kk, h * BANK:(h + 1) * BANK],
                                            start=(f == 0), stop=(f == KF - 1))
                        if f == KF - 1:
                            ins.then_inc(full[u.bank], 1)
                    if f < KF - 1:
                        ins.then_inc(signal("down_used").sem, 1)

            pe.wait_ge(signal("table_loaded").sem, signal("table_loaded").next(pe, 16))
            pe.wait_ge(signal("x_loaded").sem, signal("x_loaded").next(pe, 16))
            turn("x_T", X, None)
            pe.wait_ge(signal("chan_loaded").sem, signal("chan_loaded").next(pe, 16 * chan_dmas[0]))
            for i, u in enumerate(U["chan"]):
                if u.n:
                    pe.wait_ge(drained[u.bank], u.n)
                for q in range(4 * i, min(4 * i + 4, -(-n_chan // P))):
                    r = min(P, n_chan - q * P)
                    ins = pe.transpose(ps(u)[:, (q - 4 * i) * P:(q - 4 * i) * P + r], XH[0:r, 0, q * P:(q + 1) * P], ident[0:r, 0:r])
                ins.then_inc(full[u.bank], 1)
            u = U["rel"][0]
            if u.n:
                pe.wait_ge(drained[u.bank], u.n)
            for q in range(2):
                r = C_HEADS * REL_R // 2
                ins = pe.transpose(ps(u)[0:REL_C, q * r:(q + 1) * r], XH[0:r, 1, q * REL_C:(q + 1) * REL_C], ident[0:r, 0:r])
            ins.then_inc(full[u.bank], 1)
            ready("x_T")
            linear("even_in", EVEN_IN)
            pe.wait_ge(signal("lat_ready").sem, signal("lat_ready").next(pe, 2 * T))
            for j, u in enumerate(U["lat_T"]):
                if u.n:
                    pe.wait_ge(drained[u.bank], u.n)
                for t in range(T):
                    ins = pe.transpose(ps(u)[:, t * P:(t + 1) * P], E["H"][:, t, 3 * A_QKV + j * P:3 * A_QKV + (j + 1) * P], ident)
                ins.then_inc(full[u.bank], 1)
            ready("lat_T")
            linear("uq", B_HEADS * B_QK, 2, B_HEADS * B_QK, 2, src=E["latT"])
            linear("ukv", B_HEADS * 128, 1, B_HEADS * 128, 2, src=E["latT"][:, 2:3, :])
            if on(2):
                pe.wait_ge(signal("rope_a").sem, signal("rope_a").next(pe))
                pe.wait_ge(signal("rope_b").sem, signal("rope_b").next(pe, 2))
                attention("A")
                attention("B")
                pe.wait_ge(signal("a_normed").sem, signal("a_normed").next(pe))
                for v in U["B"]["o"][-2:]:
                    pe.wait_ge(drained[v[0].bank], v[0].n + 1)
                turn("o0_T", XH, None)
                ready("o0_T")
                linear("even_o", D)
            if on(3):
                turn("ln10_T", XH, "xh_ready")
                ready("ln10_T")
            if on(4):
                experts(0)
                turn("ln20_T", XH, "xh_ready")
                ready("ln20_T")
            if on(5):
                linear("qkv", 3 * D)
                for us in U["qkv"]:
                    for v in us:
                        pe.wait_ge(drained[v.bank], v.n + 1)
                pe.wait_ge(drained[U["rel"][0].bank], U["rel"][0].n + 1)
                attention("C")
                for v in U["C"]["o"][-2:]:
                    for w in v:
                        pe.wait_ge(drained[w.bank], w.n + 1)
                turn("o1_T", XH, None)
                ready("o1_T")
                linear("odd_o", D)
                turn("ln11_T", XH, "xh_ready")
                ready("ln11_T")
            if on(6):
                experts(1)
                pe.wait_ge(signal("xh_ready").sem, signal("xh_ready").next(pe, T))
            if on(7):
                turn("rms0_T", XH, "xh_ready")
                ready("rms0_T")
                for i, (c, us) in enumerate(zip(W["mix_in"], U["mix_in"])):
                    if i in (4, 5, 6):
                        linear_T(c, us, range(4))
                    else:
                        w = slot_kn(arrived(c))
                        for t, u in enumerate(us):
                            if u.n:
                                pe.wait_ge(drained[u.bank], u.n)
                            for kk in range(KD):
                                ins = pe.matmul(ps(u)[:, :], XT[:, kk, t * P:(t + 1) * P], w[:, kk, :], start=(kk == 0), stop=(kk == KD - 1))
                            ins.then_inc(full[u.bank], 1)
                u = U["ba"][0]
                if u.n:
                    pe.wait_ge(drained[u.bank], u.n)
                for t in range(T):
                    for kk in range(KD):
                        ins = pe.matmul(ps(u)[:, t * 8:t * 8 + 8], XT[:, kk, t * P:(t + 1) * P], ba_w[:, kk, :], start=(kk == 0), stop=(kk == KD - 1))
                ins.then_inc(full[u.bank], 1)
                for i, u in enumerate(U["l2"]):
                    pe.wait_ge(signal("l2_square").sem, signal("l2_square").next(pe))
                    if u.n:
                        pe.wait_ge(drained[u.bank], u.n)
                    pe.matmul(ps(u)[:, :], ones[:, :], G[("sq", "gm")[i % 2]].rearrange("p h c -> p (h c)"), start=True, stop=True).then_inc(
                        full[u.bank], 1)
                pe.wait_ge(signal("rotated").sem, signal("rotated").next(pe))
                for h, r in enumerate(U["ret"]):
                    for j, u in enumerate(r["qk"]):
                        if u.n:
                            pe.wait_ge(drained[u.bank], u.n)
                        for t in range(T):
                            ins = pe.transpose(ps(u)[:, t * P:(t + 1) * P], N_["RQK"][:, t, 512 * j + 128 * h:512 * j + 128 * h + 128], ident)
                        ins.then_inc(full[u.bank], 1)
                    for u in r["qk"]:
                        pe.wait_ge(drained[u.bank], u.n + 1)
                    for kc, u in enumerate(r["s"]):
                        if u.n:
                            pe.wait_ge(drained[u.bank], u.n)
                        pe.matmul(ps(u)[:, 0:S - kc * P], N_["QKT"][:, h % 2, 1, kc * P:(kc + 1) * P], N_["QKT"][:, h % 2, 0, kc * P:S], start=True, stop=True).then_inc(
                            full[u.bank], 1)
                    u = r["o"][0]
                    for v in r["s"]:
                        pe.wait_ge(drained[v.bank], v.n + 1)
                    if u.n:
                        pe.wait_ge(drained[u.bank], u.n)
                    for t in range(T):
                        for kc in range(t + 1):
                            at = sc_at[kc] + (t - kc) * P
                            ins = pe.matmul(ps(u)[:, t * P:(t + 1) * P], N_["sc"][:, at:at + P], N_["VR"][:, kc, 128 * h:128 * h + 128],
                                            start=(kc == 0), stop=(kc == t))
                    ins.then_inc(full[u.bank], 1)

                def heads(u, lhsT, rhs, start=True, stop=True):
                    for h in range(GDN_HEADS):
                        ins = pe.matmul(ps(u)[:, h * P:(h + 1) * P], lhsT(h), rhs(h), start=start, stop=stop)
                    ins.then_inc(full[u.bank], 1)

                for t in range(T):
                    g = U["gdn"][t]
                    tok = slice(t * P, (t + 1) * P)
                    pe.wait_ge(signal("gm_ready").sem, signal("gm_ready").next(pe))
                    if g["gc"][0].n:
                        pe.wait_ge(drained[g["gc"][0].bank], g["gc"][0].n)
                    pe.matmul(ps(g["gc"][0])[:, :], ones[:, :], G["gm"].rearrange("p h c -> p (h c)"), start=True, stop=True).then_inc(
                        full[g["gc"][0].bank], 1)
                    if g["gc"][1].n:
                        pe.wait_ge(drained[g["gc"][1].bank], g["gc"][1].n)
                    pe.matmul(ps(g["gc"][1])[:, 0:GDN_HEADS], k("upto"), gg[:, t, :], start=True, stop=True).then_inc(
                        full[g["gc"][1].bank], 1)
                    QT = lambda h: N_["QKVT"][:, h, tok]
                    KT = lambda h: N_["QKVT"][:, 4 + h, tok]
                    VT = lambda h: N_["QKVT"][:, 8 + h, tok]
                    if g["kk"][0].n:
                        pe.wait_ge(drained[g["kk"][0].bank], g["kk"][0].n)
                    heads(g["kk"][0], KT, KT)
                    if g["kq"][0].n:
                        pe.wait_ge(drained[g["kq"][0].bank], g["kq"][0].n)
                    heads(g["kq"][0], KT, QT)
                    for name, src in (("kt", KT), ("vt", VT)):
                        u = g[name][0]
                        if u.n:
                            pe.wait_ge(drained[u.bank], u.n)
                        for h in range(GDN_HEADS):
                            ins = pe.transpose(ps(u)[:, h * P:(h + 1) * P], src(h), ident)
                        ins.then_inc(full[u.bank], 1)
                    for l in range(LEVELS):
                        u1, *u2, u3 = g["inv"][l]
                        pe.wait_ge(signal("level_ready").sem, signal("level_ready").next(pe))
                        if u1.n:
                            pe.wait_ge(drained[u1.bank], u1.n)
                        heads(u1, lambda h: G["CT"][:, h, :], lambda h: G["Inv"][:, h, :])
                        pe.wait_ge(drained[u1.bank], u1.n + 1)
                        for u in u2:
                            if u.n:
                                pe.wait_ge(drained[u.bank], u.n)
                            heads(u, lambda h: G["InvT"][:, h, :], lambda h: G["T1"][:, h, :])
                        if u3.n:
                            pe.wait_ge(drained[u3.bank], u3.n)
                        heads(u3, lambda h: G["T1"][:, h, :], lambda h: G["InvT"][:, h, :])
                    u = g["u"][0]
                    pe.wait_ge(drained[g["inv"][-1][1].bank], g["inv"][-1][1].n + 1)
                    pe.wait_ge(drained[g["vt"][0].bank], g["vt"][0].n + 1)
                    if u.n:
                        pe.wait_ge(drained[u.bank], u.n)
                    heads(u, lambda h: G["InvT"][:, h, :], lambda h: G["v"][:, h, :])
                    u = g["w"][0]
                    if u.n:
                        pe.wait_ge(drained[u.bank], u.n)
                    heads(u, lambda h: G["kg"][:, h, :], lambda h: G["InvT"][:, h, :])
                    pe.wait_ge(drained[u.bank], u.n + 1)
                    u = g["ws"][0]
                    if t == 0:
                        pe.wait_ge(signal("state_ready").sem, signal("state_ready").next(pe))
                    else:
                        pe.wait_ge(drained[U["gdn"][t - 1]["s"][0].bank], U["gdn"][t - 1]["s"][0].n + 1)
                    if u.n:
                        pe.wait_ge(drained[u.bank], u.n)
                    heads(u, lambda h: G["wT"][:, h, :], lambda h: G["S"][:, h, :])
                    u = g["o"][0]
                    pe.wait_ge(signal("v_new").sem, signal("v_new").next(pe))
                    if u.n:
                        pe.wait_ge(drained[u.bank], u.n)
                    for h in range(GDN_HEADS):
                        pe.matmul(ps(u)[:, h * P:(h + 1) * P], G["qd"][:, h, :], G["S"][:, h, :], start=True, stop=False)
                        ins = pe.matmul(ps(u)[:, h * P:(h + 1) * P], G["attnT"][:, h, :], G["vn"][:, h, :], start=False, stop=True)
                    ins.then_inc(full[u.bank], 1)
                    u = g["s"][0]
                    if u.n:
                        pe.wait_ge(drained[u.bank], u.n)
                    heads(u, lambda h: G["ktail"][:, h, :], lambda h: G["vn"][:, h, :])
                turn("y_T", XH, "y_ready")
                ready("y_T")
                linear("mix_out", D)
            if on(8):
                turn("rmsf0_T", XH, "xh_ready")
                ready("rmsf0_T")
                ffn(0)
            if on(9):
                turn("rms1_T", XH, "xh_ready")
                ready("rms1_T")
                for c, us in zip(W["lru_in"], U["lru_in"]):
                    linear_T(c, us, range(4))
                pe.wait_ge(signal("gates_loaded").sem, signal("gates_loaded").next(pe, 32))
                for m in range(KD):
                    pe.wait_ge(drained[U["lru_in"][2 + m // 4][m % 4].bank], U["lru_in"][2 + m // 4][m % 4].n + 1)
                    for j, u in enumerate(U["lru"][m]):
                        if u.n:
                            pe.wait_ge(drained[u.bank], u.n)
                        pe.matmul(ps(u)[:, :], L_["w"][:, j, m, :], L_["xr"][:, m, :], start=True, stop=True).then_inc(
                            full[u.bank], 1)
                pe.wait_ge(signal("lru_y").sem, signal("lru_y").next(pe, KD))
                linear("lru_out", D, src=L_["gate"])
            if on(10):
                turn("rmsf1_T", XH, "xh_ready")
                ready("rmsf1_T")
                ffn(1)

        @block.vector
        def _(dve):
            def rope(x1, x2, cos, sin, tmp, told):
                dve.tensor_tensor(tmp[0], x1, cos, ALU.mult).then_inc(dve_done.sem, 1)
                dve.wait_ge(dve_done.sem, dve_done.next(dve))
                dve.tensor_tensor(tmp[1], x2, sin, ALU.mult).then_inc(dve_done.sem, 1)
                dve.wait_ge(dve_done.sem, dve_done.next(dve))
                dve.tensor_tensor(tmp[2], x2, cos, ALU.mult).then_inc(dve_done.sem, 1)
                dve.wait_ge(dve_done.sem, dve_done.next(dve))
                dve.tensor_tensor(tmp[3], x1, sin, ALU.mult).then_inc(dve_done.sem, 1)
                dve.wait_ge(dve_done.sem, dve_done.next(dve))
                dve.tensor_tensor(x1, tmp[0], tmp[1], ALU.subtract).then_inc(dve_done.sem, 1)
                dve.wait_ge(dve_done.sem, dve_done.next(dve))
                ins = dve.tensor_tensor(x2, tmp[2], tmp[3], ALU.add)
                if told:
                    ins.then_inc(signal(told).sem, 1)
                    dve.wait_ge(signal(told).sem, signal(told).next(dve))
                else:
                    ins.then_inc(dve_done.sem, 1)
                    dve.wait_ge(dve_done.sem, dve_done.next(dve))

            def residual(uses, scale):
                for i, us in enumerate(uses):
                    for q, u in enumerate(us):
                        t, c = (q, i) if len(us) == T else divmod(q, 2)
                        dve.wait_ge(full[u.bank], u.n + 1)
                        x = X[:, t, c * BANK:(c + 1) * BANK]
                        dve.scalar_tensor_tensor(x, x, scale, ps(u)[:, :], ALU.mult, ALU.add).then_inc(drained[u.bank], 1)
                        dve.wait_ge(drained[u.bank], u.n + 1)

            def layer_norm():
                for t in range(T):
                    for h in range(2):
                        dve.bn_stats(bnst[:, t, h, :], X[:, t, h * BANK:(h + 1) * BANK]).then_inc(dve_done.sem, 1)
                        dve.wait_ge(dve_done.sem, dve_done.next(dve))
                    ins = dve.bn_aggr(mv[:, t, :], bnst[:, t, :, :].rearrange("p a b -> p (a b)"))
                    if t == T - 1:
                        ins.then_inc(signal("ln_stats").sem, 1)
                        dve.wait_ge(signal("ln_stats").sem, signal("ln_stats").next(dve))
                    else:
                        ins.then_inc(dve_done.sem, 1)
                        dve.wait_ge(dve_done.sem, dve_done.next(dve))
                dve.wait_ge(signal("rstd_ready").sem, signal("rstd_ready").next(dve))
                for t in range(T):
                    dve.tensor_scalar(XH[:, t, :], X[:, t, :], mv[:, t, 0:1], rstd[:, t:t + 1], ALU.subtract, ALU.mult).then_inc(
                        signal("xh_ready").sem, 1)
                    dve.wait_ge(signal("xh_ready").sem, signal("xh_ready").next(dve))

            def rms():
                dve.wait_ge(signal("rstd_ready").sem, signal("rstd_ready").next(dve))
                for t in range(T):
                    dve.tensor_scalar(XH[:, t, :], X[:, t, :], rstd[:, t:t + 1], None, ALU.mult).then_inc(signal("xh_ready").sem, 1)
                    dve.wait_ge(signal("xh_ready").sem, signal("xh_ready").next(dve))

            def attention(name):
                c = att[name]
                u, buf, n = U[name], c["buf"], c["groups"] * T

                def bias(g):
                    for j4, v in enumerate(u["bias"][g]):
                        dve.wait_ge(full[v.bank], v.n + 1)
                        dst = buf["bias"][:, g % 2, :, :, 16 * j4:16 * j4 + 16].rearrange("p h s j -> p (h s) j")
                        src = ps(v)[:, :].rearrange("p (j q) -> p q j", j=16)
                        dve.tensor_tensor(dst, src, rep(k("window")[:, 16 * j4:16 * j4 + 16], 1, 32), ALU.add).then_inc(
                            drained[v.bank], 1)
                        dve.wait_ge(drained[v.bank], v.n + 1)

                if name == "C":
                    bias(0)
                for i in range(n + 2):
                    g, t = divmod(i, T)
                    if i < n:
                        for m in range(c["maps"]):
                            s = (i * c["maps"] + m) % 64
                            v = u["s"][i][m]
                            dve.wait_ge(full[v.bank], v.n + 1)
                            if name == "C":
                                if i >= 2:
                                    dve.wait_ge(full[u["t"][i - 2][m].bank], u["t"][i - 2][m].n + 1)
                                p = buf["p"][:, i % 2, m, :]
                                b = buf["bias"][:, g % 2, m, 7 - 2 * t:15 - 2 * t, :].rearrange("p s j -> p (s j)")
                                dve.scalar_tensor_tensor(p, ps(v)[:, :], c["scale"], b, ALU.mult, ALU.add).then_inc(
                                    drained[v.bank], 1)
                                dve.wait_ge(drained[v.bank], v.n + 1)
                                dve.tensor_reduce(negmax[:, s:s + 1], p, AX_X, ALU.max).then_inc(dve_done.sem, 1)
                                dve.wait_ge(dve_done.sem, dve_done.next(dve))
                            else:
                                dve.tensor_reduce(negmax[:, s:s + 1], ps(v)[:, :], AX_X, ALU.max).then_inc(dve_done.sem, 1)
                                dve.wait_ge(dve_done.sem, dve_done.next(dve))
                            dve.tensor_scalar(negmax[:, s:s + 1], negmax[:, s:s + 1], -1.0 if name == "C" else -c["scale"], None, ALU.mult).then_inc(
                                signal("max_ready").sem, 1)
                            dve.wait_ge(signal("max_ready").sem, signal("max_ready").next(dve))
                        if name == "C" and t == 2 and g + 1 < c["groups"]:
                            bias(g + 1)
                    if 1 <= i <= n:
                        s = ((i - 1) * c["maps"]) % 64
                        for m in range(c["maps"]):
                            if name == "C":
                                dve.wait_ge(signal("exp_done").sem, signal("exp_done").next(dve))
                            else:
                                dve.wait_ge(drained[u["s"][i - 1][m].bank], u["s"][i - 1][m].n + 1)
                        dve.reciprocal(rcp[:, s:s + c["maps"]], sums[:, s:s + c["maps"]]).then_inc(dve_done.sem, 1)
                        dve.wait_ge(dve_done.sem, dve_done.next(dve))
                        if name == "A":
                            p0, p1 = (buf["p"][:, (i - 1) % 2, m, :] for m in range(2))
                            dve.tensor_scalar(p1, p1, rcp[:, s + 1:s + 2], lam[:, 2:3], ALU.mult, ALU.mult).then_inc(
                                dve_done.sem, 1)
                            dve.wait_ge(dve_done.sem, dve_done.next(dve))
                            dve.scalar_tensor_tensor(p0, p0, rcp[:, s:s + 1], p1, ALU.mult, ALU.add).then_inc(
                                signal("mixed").sem, 1)
                            dve.wait_ge(signal("mixed").sem, signal("mixed").next(dve))
                    if i >= 2:
                        g2, t2 = divmod(i - 2, T)
                        for o in range(c["outs"]):
                            v = u["o"][i - 2][o]
                            s = ((i - 2) * c["maps"] + o) % 64
                            dve.wait_ge(full[v.bank], v.n + 1)
                            if name == "A":
                                dve.tensor_copy(c["o"](g2, o, t2), ps(v)[:, 0:c["dv"]]).then_inc(drained[v.bank], 1)
                                dve.wait_ge(drained[v.bank], v.n + 1)
                            else:
                                dve.tensor_scalar(c["o"](g2, o, t2), ps(v)[:, 0:c["dv"]], rcp[:, s:s + 1], None, ALU.mult).then_inc(
                                    drained[v.bank], 1)
                                dve.wait_ge(drained[v.bank], v.n + 1)

            def route(l):
                bg, be = bcv("b_router_group")[:, 4 * l:4 * l + 4], bcv("b_router_expert")[:, 32 * l:32 * l + 32]
                for t in range(T):
                    u = U[f"route{l}"][t]
                    dve.wait_ge(full[u.bank], u.n + 1)
                    dve.tensor_tensor(R["L"][:, t, 0:GROUPS], ps(u)[:, 0:GROUPS], bg, ALU.add).then_inc(dve_done.sem, 1)
                    dve.wait_ge(dve_done.sem, dve_done.next(dve))
                    dve.tensor_tensor(R["L"][:, t, GROUPS:], ps(u)[:, GROUPS:ROUTES], be, ALU.add).then_inc(drained[u.bank], 1)
                    dve.wait_ge(drained[u.bank], u.n + 1)
                dve.memset(R["LP"], -3e38).then_inc(dve_done.sem, 1)
                dve.wait_ge(dve_done.sem, dve_done.next(dve))
                dve.tensor_copy(R["LP"][:, :, 0:GROUPS], R["L"][:, :, 0:GROUPS]).then_inc(dve_done.sem, 1)
                dve.wait_ge(dve_done.sem, dve_done.next(dve))
                for t in range(T):
                    dve.max(R["g8"][:, t, :], R["LP"][:, t, :]).then_inc(dve_done.sem, 1)
                    dve.wait_ge(dve_done.sem, dve_done.next(dve))
                    dve.max_index(gidx[:, t, :], R["g8"][:, t, :], R["LP"][:, t, :]).then_inc(dve_done.sem, 1)
                    dve.wait_ge(dve_done.sem, dve_done.next(dve))
                dve.tensor_tensor(gdiff, R["L"][:, :, 0:GROUPS], rep(R["g8"][:, :, 0], 2, GROUPS), ALU.subtract).then_inc(
                    signal("gdiff").sem, 1)
                dve.wait_ge(signal("gdiff").sem, signal("gdiff").next(dve))
                dve.tensor_copy(grp, gidx[:, :, 0]).then_inc(dve_done.sem, 1)
                dve.wait_ge(dve_done.sem, dve_done.next(dve))
                dve.tensor_tensor(ohg, rep(k("iota")[:, 0:GROUPS], 1, T), rep(grp, 2, GROUPS), ALU.is_equal).then_inc(
                    dve_done.sem, 1)
                dve.wait_ge(dve_done.sem, dve_done.next(dve))
                dve.tensor_tensor(R["sel"], R["L"][:, :, GROUPS:].rearrange("p t (g j) -> p t j g", g=GROUPS), rep(ohg, 2, PER_GROUP), ALU.mult).then_inc(
                    dve_done.sem, 1)
                dve.wait_ge(dve_done.sem, dve_done.next(dve))
                dve.tensor_reduce(R["e8"], R["sel"], AX_X, ALU.add).then_inc(dve_done.sem, 1)
                dve.wait_ge(dve_done.sem, dve_done.next(dve))
                for t in range(T):
                    dve.max(R["v8"][:, t, :], R["e8"][:, t, :]).then_inc(dve_done.sem, 1)
                    dve.wait_ge(dve_done.sem, dve_done.next(dve))
                    dve.max_index(eidx[:, t, :], R["v8"][:, t, :], R["e8"][:, t, :]).then_inc(dve_done.sem, 1)
                    dve.wait_ge(dve_done.sem, dve_done.next(dve))
                dve.tensor_tensor(ediff, R["v8"][:, :, 1], R["v8"][:, :, 0], ALU.subtract).then_inc(signal("ediff").sem, 1)
                dve.wait_ge(signal("ediff").sem, signal("ediff").next(dve))
                dve.tensor_copy(pos2, eidx[:, :, 0:TOP_K]).then_inc(dve_done.sem, 1)
                dve.wait_ge(dve_done.sem, dve_done.next(dve))
                dve.scalar_tensor_tensor(ek, rep(grp, 2, TOP_K), float(PER_GROUP), pos2, ALU.mult, ALU.add).then_inc(
                    dve_done.sem, 1)
                dve.wait_ge(dve_done.sem, dve_done.next(dve))
                dve.tensor_tensor(R["A"], rep(rep(k("iota"), 1, TOP_K), 1, T), rep(ek, 3, EXPERTS), ALU.is_equal).then_inc(
                    dve_done.sem, 1)
                dve.wait_ge(dve_done.sem, dve_done.next(dve))
                dve.tensor_tensor(R["M"], R["A"][:, :, 0, :], R["A"][:, :, 1, :], ALU.add).then_inc(signal("chosen").sem, 1)
                dve.wait_ge(signal("chosen").sem, signal("chosen").next(dve))
                dve.wait_ge(signal("gexp").sem, signal("gexp").next(dve))
                dve.tensor_reduce(gsum, gdiff, AX_X, ALU.add).then_inc(dve_done.sem, 1)
                dve.wait_ge(dve_done.sem, dve_done.next(dve))
                dve.reciprocal(gw, gsum).then_inc(dve_done.sem, 1)
                dve.wait_ge(dve_done.sem, dve_done.next(dve))
                dve.wait_ge(signal("eexp").sem, signal("eexp").next(dve))
                dve.tensor_scalar(gsum, ediff, 1.0, None, ALU.add).then_inc(dve_done.sem, 1)
                dve.wait_ge(dve_done.sem, dve_done.next(dve))
                dve.reciprocal(gsum, gsum).then_inc(dve_done.sem, 1)
                dve.wait_ge(dve_done.sem, dve_done.next(dve))
                dve.tensor_tensor(wts[:, :, 0], gw, gsum, ALU.mult).then_inc(dve_done.sem, 1)
                dve.wait_ge(dve_done.sem, dve_done.next(dve))
                dve.tensor_tensor(wts[:, :, 1], wts[:, :, 0], ediff, ALU.mult).then_inc(dve_done.sem, 1)
                dve.wait_ge(dve_done.sem, dve_done.next(dve))
                u = U[f"route{l}"][T]
                dve.wait_ge(full[u.bank], u.n + 1)
                pos = ps(u)[:, 0:T * EXPERTS].rearrange("p (t e) -> p t e", t=T)
                dve.tensor_reduce(gsum[:, 0:1], ps(u)[:, T * EXPERTS:(T + 1) * EXPERTS], AX_X, ALU.max).then_inc(dve_done.sem, 1)
                dve.wait_ge(dve_done.sem, dve_done.next(dve))
                dve.tensor_scalar(gsum[:, 0:1], gsum[:, 0:1], -float(CAP), 0.0, ALU.add, ALU.max).then_inc(dve_done.sem, 1)
                dve.wait_ge(dve_done.sem, dve_done.next(dve))
                dve.tensor_copy(n_over[0:1, 0:1], gsum[0:1, 0:1]).then_inc(dve_done.sem, 1)
                dve.wait_ge(dve_done.sem, dve_done.next(dve))
                dve.tensor_tensor(R["tmp"], R["A"], rep(pos, 2, TOP_K), ALU.mult).then_inc(drained[u.bank], 1)
                dve.wait_ge(drained[u.bank], u.n + 1)
                dve.tensor_reduce(pos2, R["tmp"], AX_X, ALU.add).then_inc(dve_done.sem, 1)
                dve.wait_ge(dve_done.sem, dve_done.next(dve))
                dve.tensor_scalar(over, pos2, float(CAP), None, ALU.is_ge).then_inc(dve_done.sem, 1)
                dve.wait_ge(dve_done.sem, dve_done.next(dve))
                dve.tensor_scalar(keep, over, -1.0, 1.0, ALU.mult, ALU.add).then_inc(dve_done.sem, 1)
                dve.wait_ge(dve_done.sem, dve_done.next(dve))
                dve.scalar_tensor_tensor(slotf, ek, float(CAP), pos2, ALU.mult, ALU.add).then_inc(dve_done.sem, 1)
                dve.wait_ge(dve_done.sem, dve_done.next(dve))
                dve.scalar_tensor_tensor(wtmp, over, 1e6, slotf, ALU.mult, ALU.add).then_inc(dve_done.sem, 1)
                dve.wait_ge(dve_done.sem, dve_done.next(dve))
                dve.tensor_copy(scat.rearrange("p (t j) -> p t j", t=T), wtmp).then_inc(dve_done.sem, 1)
                dve.wait_ge(dve_done.sem, dve_done.next(dve))
                dve.tensor_tensor(wtmp, slotf, keep, ALU.mult).then_inc(dve_done.sem, 1)
                dve.wait_ge(dve_done.sem, dve_done.next(dve))
                dve.tensor_tensor(slotf, wts, over, ALU.mult).then_inc(
                    dve_done.sem, 1)
                dve.wait_ge(dve_done.sem, dve_done.next(dve))
                dve.tensor_tensor(wts, wts, keep, ALU.mult).then_inc(dve_done.sem, 1)
                dve.wait_ge(dve_done.sem, dve_done.next(dve))
                dve.tensor_copy(gath.rearrange("p (t j) -> p t j", t=T), wtmp).then_inc(signal("slots_ready").sem, 1)
                dve.wait_ge(signal("slots_ready").sem, signal("slots_ready").next(dve))

            def experts(l):
                base = U[f"moe{l}"]

                def wait_use(sems, b, e):
                    dve.wait_ge(sems[b], e + (base[b] + 1))

                def hidden(e, half):
                    wait_use(full, 3, e)
                    wait_use(drained, 2, e)
                    h = M["hid"][0:CAP, half, :]
                    dve.tensor_tensor(h, h, psum[3][0:CAP, :], ALU.mult).then_inc(drained[3], 1)

                def hidden_T(e, half):
                    wait_use(full, 4, e)
                    dve.tensor_copy(M["HT"][:, half, :, :].rearrange("p k c -> p (k c)"), psum[4][:, 0:KE * CAP]).then_inc(drained[4], 1)

                def out_rows(e, half, n, checked):
                    if checked:
                        dve.wait_ge(signal(f"y_stored{half}").sem, n * 16 + 16 * (EXPERTS // 2) * l)
                    wait_use(full, 6, e)
                    dve.tensor_copy(M["YE"][0:CAP, half, BANK:D], psum[6][0:CAP, :]).then_inc(drained[6], 1)

                def stage(e, half, n, first=False, checked=True):
                    hidden(e, half)
                    if not first:
                        out_rows(e - 1, 1 - half, n - 1 + half, checked)
                    hidden_T(e, half)

                stage(0, 0, 0, first=True)
                stage(1, 1, 0, checked=l > 0)
                stage(2, 0, 1, checked=l > 0)
                with dve.Fori(1, EXPERTS // 2 - 1) as i:
                    stage(i * 2 + 1, 1, i)
                    stage(i * 2 + 2, 0, i + 1)
                stage(EXPERTS - 1, 1, EXPERTS // 2 - 1)
                out_rows(EXPERTS - 1, 1, EXPERTS // 2 - 1, True)
                dve.wait_ge(signal("rows_back").sem, signal("rows_back").next(dve, 16 * T * TOP_K))
                for t in range(T):
                    dve.tensor_scalar(X[:, t, :], X[:, t, :], ALPHA, None, ALU.mult).then_inc(dve_done.sem, 1)
                    dve.wait_ge(dve_done.sem, dve_done.next(dve))
                    for j, y in enumerate((XH[:, t, :], M["YG"][:, t, :])):
                        dve.scalar_tensor_tensor(X[:, t, :], y, wts[:, t, j:j + 1], X[:, t, :], ALU.mult, ALU.add).then_inc(
                            dve_done.sem, 1)
                        dve.wait_ge(dve_done.sem, dve_done.next(dve))
                with dve.If(overflow(dve, waits=False) > 0):
                    late_n = Signal(late(l, "steps"))

                    dve.tensor_tensor(R["tmp"], R["A"], rep(slotf, 3, EXPERTS), ALU.mult).then_inc(late_n.sem, 1)
                    dve.wait_ge(late_n.sem, late_n.next(dve))
                    dve.tensor_tensor(R["M"], R["tmp"][:, :, 0, :], R["tmp"][:, :, 1, :], ALU.add).then_inc(late_n.sem, 1)
                    dve.wait_ge(late_n.sem, late_n.next(dve))
                    with dve.Fori(0, EXPERTS) as e:
                        for t in range(T):
                            n = e * T + (t + 1)
                            dve.wait_ge(late(l, "silu"), n)
                            dve.tensor_tensor(M["lhid"], M["lhid"], psum[1][:, :], ALU.mult).then_inc(late(l, "hidden"), 1)
                            dve.wait_ge(late(l, "turned"), n)
                            dve.tensor_copy(M["lHT"].rearrange("p k c -> p (k c)"), psum[2][:, :]).then_inc(late(l, "hidden_T"), 1)
                            dve.wait_ge(late(l, "down"), n)
                            for j in range(2):
                                x = X[:, t, j * BANK:(j + 1) * BANK]
                                dve.scalar_tensor_tensor(x, psum[3 + j][:, :], R["M"][:, t, bass.ds(e, 1)], x, ALU.mult, ALU.add).then_inc(
                                    late(l, "added" if j else "half"), 1)
                    dve.wait_ge(late(l, "added"), EXPERTS * T)
                    dve.wait_ge(late(l, "half"), EXPERTS * T)

            def conv(dst, u, taps, bias=None, told=None):
                dve.wait_ge(full[u.bank], u.n + 1)
                n = len(taps)
                if bias is None:
                    dve.tensor_scalar(dst, ps(u)[:, :], taps[-1], None, ALU.mult).then_inc(dve_done.sem, 1)
                    dve.wait_ge(dve_done.sem, dve_done.next(dve))
                else:
                    dve.tensor_scalar(dst, ps(u)[:, :], taps[-1], bias, ALU.mult, ALU.add).then_inc(dve_done.sem, 1)
                    dve.wait_ge(dve_done.sem, dve_done.next(dve))
                for d in range(1, n):
                    ins = dve.scalar_tensor_tensor(dst[:, d:S], ps(u)[:, 0:S - d], taps[n - 1 - d], dst[:, d:S], ALU.mult, ALU.add)
                    if d < n - 1:
                        ins.then_inc(dve_done.sem, 1)
                        dve.wait_ge(dve_done.sem, dve_done.next(dve))
                ins.then_inc(drained[u.bank], 1)
                dve.wait_ge(drained[u.bank], u.n + 1)

            def log1p_arg(dst, e):
                dve.tensor_scalar(dst, e, 1.0, None, ALU.add).then_inc(dve_done.sem, 1)
                dve.wait_ge(dve_done.sem, dve_done.next(dve))

            def log1p(dst, e, w, ln, tmp):
                dve.tensor_scalar(tmp, w, 1.0, 1e-30, ALU.subtract, ALU.max).then_inc(dve_done.sem, 1)
                dve.wait_ge(dve_done.sem, dve_done.next(dve))
                dve.reciprocal(tmp, tmp).then_inc(dve_done.sem, 1)
                dve.wait_ge(dve_done.sem, dve_done.next(dve))
                dve.tensor_tensor(tmp, tmp, ln, ALU.mult).then_inc(dve_done.sem, 1)
                dve.wait_ge(dve_done.sem, dve_done.next(dve))
                dve.tensor_tensor(tmp, tmp, e, ALU.mult).then_inc(dve_done.sem, 1)
                dve.wait_ge(dve_done.sem, dve_done.next(dve))
                dve.tensor_scalar(dst, w, 1.0, None, ALU.is_equal).then_inc(dve_done.sem, 1)
                dve.wait_ge(dve_done.sem, dve_done.next(dve))
                dve.tensor_tensor(dst, dst, e, ALU.mult).then_inc(dve_done.sem, 1)
                dve.wait_ge(dve_done.sem, dve_done.next(dve))
                dve.tensor_tensor(dst, dst, tmp, ALU.add).then_inc(dve_done.sem, 1)
                dve.wait_ge(dve_done.sem, dve_done.next(dve))

            def delta_rule():
                dve.memset(G["S"], 0.0).then_inc(signal("state_ready").sem, 1)
                dve.wait_ge(signal("state_ready").sem, signal("state_ready").next(dve))
                for t in range(T):
                    g = U["gdn"][t]
                    tok = slice(t * P, (t + 1) * P)

                    def heads(u):
                        return ps(u)[:, :].rearrange("p (h c) -> p h c", h=GDN_HEADS)

                    bt = rep(beta[:, t, :], 2, P)
                    dve.tensor_tensor(G["gm"], rep(k("upto"), 1, GDN_HEADS), rep(gg[:, t, :], 2, P), ALU.mult).then_inc(
                        signal("gm_ready").sem, 1)
                    dve.wait_ge(signal("gm_ready").sem, signal("gm_ready").next(dve))
                    u = g["gc"][1]
                    dve.wait_ge(full[u.bank], u.n + 1)
                    dve.tensor_copy(gcol8[:, 0, :], ps(u)[:, 0:GDN_HEADS]).then_inc(drained[u.bank], 1)
                    dve.wait_ge(drained[u.bank], u.n + 1)
                    u = g["gc"][0]
                    dve.wait_ge(full[u.bank], u.n + 1)
                    dve.tensor_tensor(gcol8[:, 1, :], heads(u)[:, :, P - 1], gcol8[:, 0, :], ALU.subtract).then_inc(dve_done.sem, 1)
                    dve.wait_ge(dve_done.sem, dve_done.next(dve))
                    dve.tensor_tensor(G["dec"], heads(u), rep(gcol8[:, 0, :], 2, P), ALU.subtract).then_inc(dve_done.sem, 1)
                    dve.wait_ge(dve_done.sem, dve_done.next(dve))
                    dve.tensor_scalar(G["dec"], G["dec"], 0.0, None, ALU.min).then_inc(signal("dec_raw").sem, 1)
                    dve.wait_ge(signal("dec_raw").sem, signal("dec_raw").next(dve))
                    dve.wait_ge(signal("dec_exp").sem, signal("dec_exp").next(dve))
                    dve.tensor_tensor(G["dec"], G["dec"], rep(k("upto"), 1, GDN_HEADS), ALU.mult).then_inc(dve_done.sem, 1)
                    dve.wait_ge(dve_done.sem, dve_done.next(dve))
                    u = g["kq"][0]
                    dve.wait_ge(full[u.bank], u.n + 1)
                    dve.tensor_tensor(G["attnT"], heads(u), G["dec"], ALU.mult).then_inc(drained[u.bank], 1)
                    dve.wait_ge(drained[u.bank], u.n + 1)
                    dve.tensor_tensor(G["dec"], G["dec"], rep(k("before"), 1, GDN_HEADS), ALU.mult).then_inc(dve_done.sem, 1)
                    dve.wait_ge(dve_done.sem, dve_done.next(dve))
                    dve.tensor_tensor(G["dec"], G["dec"], bt, ALU.mult).then_inc(dve_done.sem, 1)
                    dve.wait_ge(dve_done.sem, dve_done.next(dve))
                    u = g["kk"][0]
                    dve.wait_ge(full[u.bank], u.n + 1)
                    dve.tensor_tensor(G["LT"], heads(u), G["dec"], ALU.mult).then_inc(drained[u.bank], 1)
                    dve.wait_ge(drained[u.bank], u.n + 1)
                    u = g["kt"][0]
                    dve.wait_ge(full[u.bank], u.n + 1)
                    dve.tensor_tensor(G["kg"], heads(u), rep(ge8[:, 0, :], 2, P), ALU.mult).then_inc(dve_done.sem, 1)
                    dve.wait_ge(dve_done.sem, dve_done.next(dve))
                    dve.tensor_tensor(G["ktail"], heads(u), rep(ge8[:, 1, :], 2, P), ALU.mult).then_inc(drained[u.bank], 1)
                    dve.wait_ge(drained[u.bank], u.n + 1)
                    dve.tensor_tensor(G["qd"], N_["QKVT"][:, 0:GDN_HEADS, tok], G["eg"], ALU.mult).then_inc(dve_done.sem, 1)
                    dve.wait_ge(dve_done.sem, dve_done.next(dve))
                    dve.tensor_copy(G["Inv"], rep(ident, 1, GDN_HEADS)).then_inc(dve_done.sem, 1)
                    dve.wait_ge(dve_done.sem, dve_done.next(dve))
                    dve.tensor_copy(G["InvT"], rep(ident, 1, GDN_HEADS)).then_inc(dve_done.sem, 1)
                    dve.wait_ge(dve_done.sem, dve_done.next(dve))
                    for l in range(LEVELS):
                        dve.tensor_tensor(G["CT"], G["LT"], rep(k(f"level{l}"), 1, GDN_HEADS), ALU.mult).then_inc(
                            signal("level_ready").sem, 1)
                        dve.wait_ge(signal("level_ready").sem, signal("level_ready").next(dve))
                        _, *u2, u3 = g["inv"][l]
                        for u, dst in [(u, "Inv") for u in u2] + [(u3, "InvT")]:
                            dve.wait_ge(full[u.bank], u.n + 1)
                            dve.tensor_tensor(G[dst], G[dst], heads(u), ALU.subtract).then_inc(drained[u.bank], 1)
                            dve.wait_ge(drained[u.bank], u.n + 1)
                    u = g["u"][0]
                    dve.wait_ge(full[u.bank], u.n + 1)
                    dve.tensor_tensor(G["ub"], heads(u), bt, ALU.mult).then_inc(drained[u.bank], 1)
                    dve.wait_ge(drained[u.bank], u.n + 1)
                    u = g["ws"][0]
                    dve.wait_ge(full[u.bank], u.n + 1)
                    dve.tensor_tensor(G["t2"], heads(u), bt, ALU.mult).then_inc(drained[u.bank], 1)
                    dve.wait_ge(drained[u.bank], u.n + 1)
                    dve.tensor_tensor(G["vn"], G["ub"], G["t2"], ALU.subtract).then_inc(signal("v_new").sem, 1)
                    dve.wait_ge(signal("v_new").sem, signal("v_new").next(dve))
                    u = g["s"][0]
                    dve.wait_ge(full[u.bank], u.n + 1)
                    dve.tensor_tensor(G["S"], G["S"], rep(G["eg"][:, :, P - 1], 2, P), ALU.mult).then_inc(dve_done.sem, 1)
                    dve.wait_ge(dve_done.sem, dve_done.next(dve))
                    dve.tensor_tensor(G["S"], G["S"], heads(u), ALU.add).then_inc(drained[u.bank], 1)
                    dve.wait_ge(drained[u.bank], u.n + 1)

            def ffn(l):
                n = 0
                for us in U[f"ffn{l}_up"]:
                    for m in range(2):
                        taps = lambda tile: [col("ffn_conv_w_2", (l * FFN_CONV + w) * 2 * KF + tile) for w in range(FFN_CONV)]
                        off = lambda tile: col("ffn_conv_b_2", l * 2 * KF + tile)
                        conv(F_["cg"][:, m, :], us[2 * m], taps(n), off(n))
                        conv(F_["cv"][:, m, :], us[2 * m + 1], taps(KF + n), off(KF + n))
                        dve.wait_ge(signal("ff_silu").sem, signal("ff_silu").next(dve))
                        dve.tensor_tensor(F_["act"][:, n, :], F_["cg"][:, m, :], F_["cv"][:, m, :], ALU.mult).then_inc(
                            signal("ff_act").sem, 1)
                        dve.wait_ge(signal("ff_act").sem, signal("ff_act").next(dve))
                        n += 1

            dve.memset(rel_sb[:, :], 0.0).then_inc(dve_done.sem, 1)
            dve.wait_ge(dve_done.sem, dve_done.next(dve))
            u = U["rel"][0]
            dve.wait_ge(full[u.bank], u.n + 1)
            rel_v = rel_sb[:, :].rearrange("p (h s) -> p h s", s=2 * NA_ROWS)
            rel_u = ps(u)[0:REL_C, 0:C_HEADS * REL_R].rearrange("p (h s) -> p h s", s=REL_R)
            dve.tensor_copy(rel_v[0:REL_C, :, 0:REL_R], rel_u).then_inc(dve_done.sem, 1)
            dve.wait_ge(dve_done.sem, dve_done.next(dve))
            dve.tensor_copy(rel_v[32:32 + REL_C, :, 1:1 + REL_R], rel_u).then_inc(drained[u.bank], 1)
            dve.wait_ge(drained[u.bank], u.n + 1)
            for us in U["even_in"]:
                for u in us:
                    dve.wait_ge(drained[u.bank], u.n + 1)
            dve.wait_ge(signal("table_loaded").sem, signal("table_loaded").next(dve, 16))
            dve.wait_ge(signal("small_loaded").sem, signal("small_loaded").next(dve, 16 * (len(bc_at) + 5)))
            lv = bc[:, bc_at["even_lam_q1"][0]:bc_at["even_lam_q1"][0] + 256].rearrange("p (m a d) -> p m a d", m=2, a=2)
            lt = E["tmp"][:, 3, 0:128].rearrange("p (m d) -> p m d", m=2)
            dve.tensor_tensor(lt, lv[:, :, 0, :], lv[:, :, 1, :], ALU.mult).then_inc(dve_done.sem, 1)
            dve.wait_ge(dve_done.sem, dve_done.next(dve))
            dve.tensor_reduce(lam[:, 0:2], lt, AX_X, ALU.add).then_inc(signal("lam_dots").sem, 1)
            dve.wait_ge(signal("lam_dots").sem, signal("lam_dots").next(dve))
            tmp = [E["p"][:, i // 2, i % 2, :].rearrange("p (t g d) -> p t g d", t=T, g=16) for i in range(4)]
            qk = E["H"][:, :, 0:2 * A_QKV].rearrange("p t (g d) -> p t g d", d=A_DIM)
            h = A_ROT // 2
            cs = [rep(k(f"ra_{f}").rearrange("p (t d) -> p t d", t=T), 2, 16) for f in ("cos", "sin")]
            rope(qk[:, :, :, 0:h], qk[:, :, :, h:2 * h], cs[0], cs[1], tmp, "rope_a")
            dve.wait_ge(signal("rstd_ready").sem, signal("rstd_ready").next(dve))
            for j, (o, n, name) in enumerate(((3 * A_QKV, B_Q_RANK, "even_q_norm_g"), (3 * A_QKV + B_Q_RANK, B_KV_RANK, "even_kv_norm_g"))):
                for t in range(T):
                    x = E["H"][:, t, o:o + n]
                    dve.scalar_tensor_tensor(x, x, rstd[:, j * T + t:j * T + t + 1], bcv(name), ALU.mult, ALU.mult).then_inc(
                        signal("lat_ready").sem, 1)
                    dve.wait_ge(signal("lat_ready").sem, signal("lat_ready").next(dve))
            dve.wait_ge(signal("lam_exp").sem, signal("lam_exp").next(dve))
            dve.tensor_tensor(lam[:, 2:3], lam[:, 1:2], lam[:, 0:1], ALU.subtract).then_inc(dve_done.sem, 1)
            dve.wait_ge(dve_done.sem, dve_done.next(dve))
            dve.tensor_scalar(lam[:, 2:3], lam[:, 2:3], -LAMBDA_INIT, None, ALU.add).then_inc(dve_done.sem, 1)
            dve.wait_ge(dve_done.sem, dve_done.next(dve))
            for name in ("uq", "ukv"):
                for u in U[name][0]:
                    dve.wait_ge(drained[u.bank], u.n + 1)
            h = B_ROPE // 2
            cs = [k(f"rb_{f}").rearrange("p (t d) -> p t d", t=T) for f in ("cos", "sin")]
            tmp = [E["tmp"][:, i, :].rearrange("p (t g d) -> p t g d", t=T, g=B_HEADS) for i in range(4)]
            rope(E["QB"][:, :, :, B_NOPE:B_NOPE + h], E["QB"][:, :, :, B_NOPE + h:], rep(cs[0], 2, B_HEADS), rep(cs[1], 2, B_HEADS), tmp, "rope_b")
            kr = E["H"][:, :, EVEN_IN - B_ROPE:EVEN_IN]
            tmp = [E["tmp"][:, i, 0:T * h].rearrange("p (t d) -> p t d", t=T) for i in range(4)]
            rope(kr[:, :, 0:h], kr[:, :, h:], cs[0], cs[1], tmp, None)
            dve.tensor_copy(E["KC"][:, :, :, B_NOPE:], rep(kr, 2, B_HEADS)).then_inc(signal("rope_b").sem, 1)
            dve.wait_ge(signal("rope_b").sem, signal("rope_b").next(dve))
            if on(2):
                attention("A")
                attention("B")
                o = XH[:, :, 0:512]
                sq = E["H"][:, :, 0:512]
                dve.tensor_tensor(sq, o, o, ALU.mult).then_inc(dve_done.sem, 1)
                dve.wait_ge(dve_done.sem, dve_done.next(dve))
                dve.tensor_reduce(ssq[:, 0:16].rearrange("p (t h) -> p t h", t=T), sq.rearrange("p t (h d) -> p t h d", d=128), AX_X, ALU.add).then_inc(
                    signal("a_ssq").sem, 1)
                dve.wait_ge(signal("a_ssq").sem, signal("a_ssq").next(dve))
                dve.wait_ge(signal("rstd_ready").sem, signal("rstd_ready").next(dve))
                dve.tensor_scalar(rstd[:, 0:16], rstd[:, 0:16], 1.0 - LAMBDA_INIT, None, ALU.mult).then_inc(dve_done.sem, 1)
                dve.wait_ge(dve_done.sem, dve_done.next(dve))
                for t in range(T):
                    ov = XH[:, t, 0:512].rearrange("p (h d) -> p h d", d=128)
                    dve.tensor_tensor(ov, ov, rep(rstd[:, 4 * t:4 * t + 4], 2, 128), ALU.mult).then_inc(dve_done.sem, 1)
                    dve.wait_ge(dve_done.sem, dve_done.next(dve))
                    ins = dve.tensor_tensor(ov, ov, rep(bcv("even_subln_g"), 1, A_HEADS), ALU.mult)
                    if t == T - 1:
                        ins.then_inc(signal("a_normed").sem, 1)
                        dve.wait_ge(signal("a_normed").sem, signal("a_normed").next(dve))
                    else:
                        ins.then_inc(dve_done.sem, 1)
                        dve.wait_ge(dve_done.sem, dve_done.next(dve))
                residual(U["even_o"], ALPHA)
            if on(3):
                layer_norm()
            if on(4):
                route(0)
                dve.wait_ge(signal("x_applied").sem, signal("x_applied").next(dve, T))
                experts(0)
                layer_norm()
            if on(5):
                dve.wait_ge(signal("x_applied").sem, signal("x_applied").next(dve, T))
                attention("C")
                residual(U["odd_o"], ALPHA)
                layer_norm()
            if on(6):
                route(1)
                dve.wait_ge(signal("x_applied").sem, signal("x_applied").next(dve, T))
                experts(1)
                layer_norm()
            if on(7):
                dve.wait_ge(signal("x_applied").sem, signal("x_applied").next(dve, T))
                rms()
                for i in (4, 5, 6):
                    for m, u in enumerate(U["mix_in"][i]):
                        tile = 4 * (i - 4) + m
                        conv(N_["QKVT"][:, tile, :], u, [col("gdn_conv_w_2", w * 12 + tile) for w in range(SHORT_CONV)])
                u = U["ba"][0]
                dve.wait_ge(full[u.bank], u.n + 1)
                dve.tensor_copy(gb, ps(u)[:, 0:T * 8].rearrange("p (t c) -> p t c", t=T)).then_inc(drained[u.bank], 1)
                dve.wait_ge(drained[u.bank], u.n + 1)
                ad = gb[:, :, GDN_HEADS:]
                dve.tensor_tensor(ad, ad, rep(bcv("gdn_dt_bias_2"), 1, T), ALU.add).then_inc(dve_done.sem, 1)
                dve.wait_ge(dve_done.sem, dve_done.next(dve))
                dve.tensor_scalar(sp4, ad, -1.0, None, ALU.mult).then_inc(dve_done.sem, 1)
                dve.wait_ge(dve_done.sem, dve_done.next(dve))
                dve.tensor_tensor(sp1, sp4, ad, ALU.max).then_inc(signal("ab_ready").sem, 1)
                dve.wait_ge(signal("ab_ready").sem, signal("ab_ready").next(dve))
                dve.wait_ge(signal("ab_exp").sem, signal("ab_exp").next(dve))
                dve.tensor_scalar(sp2, sp1, 1.0, None, ALU.add).then_inc(signal("ln_arg").sem, 1)
                dve.wait_ge(signal("ln_arg").sem, signal("ln_arg").next(dve))
                dve.tensor_scalar(beta, beta, 0.5, 0.5, ALU.mult, ALU.add).then_inc(dve_done.sem, 1)
                dve.wait_ge(dve_done.sem, dve_done.next(dve))
                dve.wait_ge(signal("ln_done").sem, signal("ln_done").next(dve))
                log1p(sp4, sp1, sp2, sp3, gg)
                dve.scalar_tensor_tensor(sp4, ad, 0.0, sp4, ALU.max, ALU.add).then_inc(dve_done.sem, 1)
                dve.wait_ge(dve_done.sem, dve_done.next(dve))
                dve.tensor_tensor(sp4, sp4, rep(lam[:, 4:8], 1, T), ALU.mult).then_inc(dve_done.sem, 1)
                dve.wait_ge(dve_done.sem, dve_done.next(dve))
                dve.tensor_scalar(gg, sp4, -1.0, None, ALU.mult).then_inc(dve_done.sem, 1)
                dve.wait_ge(dve_done.sem, dve_done.next(dve))
                for i, u in enumerate(U["l2"]):
                    rn = G[("rn", "t2")[i % 2]].rearrange("p h c -> p (h c)")
                    dve.wait_ge(drained[u.bank], u.n + 1)
                    dve.reciprocal(rn, rn).then_inc(dve_done.sem, 1)
                    dve.wait_ge(dve_done.sem, dve_done.next(dve))
                    x = N_["QKVT"][:, i, :]
                    dve.scalar_tensor_tensor(x, x, HEAD ** -0.5 if i < GDN_HEADS else 1.0, rn, ALU.mult, ALU.mult).then_inc(
                        signal("l2_normed").sem, 1)
                    dve.wait_ge(signal("l2_normed").sem, signal("l2_normed").next(dve))
                for i in (0, 1, 2, 3, 7):
                    for u in U["mix_in"][i]:
                        dve.wait_ge(drained[u.bank], u.n + 1)
                h = HEAD // 2
                for t in range(T):
                    x = N_["RQK"][:, t, :].rearrange("p (g d) -> p g d", d=HEAD)
                    cs = [rep(k(f"rr_{f}")[:, t * h:(t + 1) * h], 1, 8) for f in ("cos", "sin")]
                    tmp = [N_["rt"][:, i, :, :] for i in range(4)]
                    rope(x[:, :, 0:h], x[:, :, h:], cs[0], cs[1], tmp, "rotated" if t == T - 1 else None)
                dve.wait_ge(signal("decay_loaded").sem, signal("decay_loaded").next(dve, 16))
                for hd, r in enumerate(U["ret"]):
                    for kc, u in enumerate(r["s"]):
                        dve.wait_ge(full[u.bank], u.n + 1)
                        n = S - kc * P
                        dve.tensor_tensor(N_["sc"][:, sc_at[kc]:sc_at[kc] + n], ps(u)[:, 0:n], N_["dret"][:, hd, 0:n], ALU.mult).then_inc(
                            drained[u.bank], 1)
                        dve.wait_ge(drained[u.bank], u.n + 1)
                    u = r["o"][0]
                    dve.wait_ge(full[u.bank], u.n + 1)
                    dve.tensor_copy(XH[:, :, 128 * hd:128 * hd + 128], ps(u)[:, :].rearrange("p (t d) -> p t d", t=T)).then_inc(
                        drained[u.bank], 1)
                    dve.wait_ge(drained[u.bank], u.n + 1)
                delta_rule()
                sq = big[:, 10752:10752 + 4096].rearrange("p (t d) -> p t d", t=T)
                for u in (U["gdn"][t]["o"][0] for t in range(T)):
                    dve.wait_ge(drained[u.bank], u.n + 1)
                dve.tensor_tensor(sq, XH[:, :, :], XH[:, :, :], ALU.mult).then_inc(dve_done.sem, 1)
                dve.wait_ge(dve_done.sem, dve_done.next(dve))
                dve.tensor_reduce(ssq[:, 0:32].rearrange("p (t h) -> p t h", t=T), sq.rearrange("p t (h d) -> p t h d", d=128), AX_X, ALU.add).then_inc(
                    signal("y_ssq").sem, 1)
                dve.wait_ge(signal("y_ssq").sem, signal("y_ssq").next(dve))
                for t in range(T):
                    gd = N_["GD"][:, t, :].rearrange("p (h d) -> p h d", d=128)
                    dve.tensor_tensor(gd, gd, rep(bcv("gdn_out_gain_2"), 1, GDN_HEADS), ALU.mult).then_inc(dve_done.sem, 1)
                    dve.wait_ge(dve_done.sem, dve_done.next(dve))
                dve.wait_ge(signal("rstd_ready").sem, signal("rstd_ready").next(dve))
                for t in range(T):
                    y = XH[:, t, :].rearrange("p (h d) -> p h d", d=128)
                    dve.tensor_tensor(y, y, rep(rstd[:, 8 * t:8 * t + 8], 2, 128), ALU.mult).then_inc(dve_done.sem, 1)
                    dve.wait_ge(dve_done.sem, dve_done.next(dve))
                    dve.tensor_tensor(XH[:, t, 0:512], XH[:, t, 0:512], N_["GR"][:, t, :], ALU.mult).then_inc(dve_done.sem, 1)
                    dve.wait_ge(dve_done.sem, dve_done.next(dve))
                    dve.tensor_tensor(XH[:, t, 512:1024], XH[:, t, 512:1024], N_["GD"][:, t, :], ALU.mult).then_inc(
                        signal("y_ready").sem, 1)
                    dve.wait_ge(signal("y_ready").sem, signal("y_ready").next(dve))
                residual(U["mix_out"], 1.0)
            if on(8):
                rms()
                ffn(0)
                residual([U["ffn0_down"]], 1.0)
            if on(9):
                lm = chan[:, chan_at["lru_lambda_2"]:chan_at["lru_lambda_2"] + KD]
                dve.tensor_scalar(sl2, lm, -1.0, None, ALU.mult).then_inc(dve_done.sem, 1)
                dve.wait_ge(dve_done.sem, dve_done.next(dve))
                dve.tensor_tensor(sl1, sl2, lm, ALU.max).then_inc(signal("lam_arg").sem, 1)
                dve.wait_ge(signal("lam_arg").sem, signal("lam_arg").next(dve))
                dve.wait_ge(signal("lam_e").sem, signal("lam_e").next(dve))
                dve.tensor_scalar(sl2, sl1, 1.0, None, ALU.add).then_inc(signal("lam_w").sem, 1)
                dve.wait_ge(signal("lam_w").sem, signal("lam_w").next(dve))
                dve.wait_ge(signal("lam_ln").sem, signal("lam_ln").next(dve))
                log1p(cvec, sl1, sl2, sl3, bnst.rearrange("p a b c -> p (a b c)")[:, 0:KD])
                dve.tensor_scalar(sl2, lm, -1.0, 0.0, ALU.mult, ALU.max).then_inc(dve_done.sem, 1)
                dve.wait_ge(dve_done.sem, dve_done.next(dve))
                dve.tensor_tensor(cvec, cvec, sl2, ALU.add).then_inc(dve_done.sem, 1)
                dve.wait_ge(dve_done.sem, dve_done.next(dve))
                dve.tensor_scalar(cvec, cvec, -4.0, None, ALU.mult).then_inc(signal("cvec_ready").sem, 1)
                dve.wait_ge(signal("cvec_ready").sem, signal("cvec_ready").next(dve))
                rms()
                for i in range(2):
                    for m, u in enumerate(U["lru_in"][2 + i]):
                        tile = 4 * i + m
                        conv(L_["xr"][:, tile, :], u, [col("lru_conv_w_2", w * KD + tile) for w in range(LRU_CONV)], col("lru_conv_b_2", tile))
                for m in range(KD):
                    dve.wait_ge(signal("lru_tanh").sem, signal("lru_tanh").next(dve))
                    s = XT[:, m, :]
                    x = L_["i"][:, m, :]
                    dve.tensor_scalar(L_["u"], s, -1.0, 1.0, ALU.mult, ALU.add).then_inc(dve_done.sem, 1)
                    dve.wait_ge(dve_done.sem, dve_done.next(dve))
                    dve.reciprocal(L_["u"], L_["u"]).then_inc(dve_done.sem, 1)
                    dve.wait_ge(dve_done.sem, dve_done.next(dve))
                    dve.scalar_tensor_tensor(L_["a"], s, 1.0, L_["u"], ALU.add, ALU.mult).then_inc(dve_done.sem, 1)
                    dve.wait_ge(dve_done.sem, dve_done.next(dve))
                    dve.wait_ge(signal("lru_root").sem, signal("lru_root").next(dve))
                    dve.scalar_tensor_tensor(L_["u"], L_["q"][:, m % 2, :], 2.0, L_["u"], ALU.mult, ALU.mult).then_inc(
                        dve_done.sem, 1)
                    dve.wait_ge(dve_done.sem, dve_done.next(dve))
                    dve.tensor_tensor(x, x, L_["xr"][:, m, :], ALU.mult).then_inc(dve_done.sem, 1)
                    dve.wait_ge(dve_done.sem, dve_done.next(dve))
                    dve.tensor_tensor(L_["u"], L_["u"], x, ALU.mult).then_inc(dve_done.sem, 1)
                    dve.wait_ge(dve_done.sem, dve_done.next(dve))
                    dve.tensor_tensor_scan(x, L_["a"], L_["u"], 0.0, ALU.mult, ALU.add).then_inc(dve_done.sem, 1)
                    dve.wait_ge(dve_done.sem, dve_done.next(dve))
                    dve.tensor_tensor(L_["gate"][:, m, :], L_["gate"][:, m, :], x, ALU.mult).then_inc(signal("lru_y").sem, 1)
                    dve.wait_ge(signal("lru_y").sem, signal("lru_y").next(dve))
                residual(U["lru_out"], 1.0)
            if on(10):
                rms()
                ffn(1)
                residual([U["ffn1_down"]], 1.0)
            if on(11):
                dve.wait_ge(signal("rstd_ready").sem, signal("rstd_ready").next(dve))
                dve.wait_ge(signal("ln_loaded").sem, signal("ln_loaded").next(dve, 16 * 9))
                for t in range(T):
                    dve.scalar_tensor_tensor(XH[:, t, :], X[:, t, :], rstd[:, t:t + 1], lnp[:, 0, :], ALU.mult, ALU.mult).then_inc(
                        signal("out_ready").sem, 1)
                    dve.wait_ge(signal("out_ready").sem, signal("out_ready").next(dve))
            else:
                if stages in (3, 4, 5):
                    dve.wait_ge(full[U[{3: "ln10_T", 4: "ln20_T", 5: "ln11_T"}[stages]][-1].bank], U[{3: "ln10_T", 4: "ln20_T", 5: "ln11_T"}[stages]][-1].n + 1)
                for t in range(T):
                    if stages in (3, 4, 5, 6):
                        dve.wait_ge(signal("x_applied").sem, signal("x_applied").next(dve))
                    dve.tensor_copy(XH[:, t, :], X[:, t, :]).then_inc(signal("out_ready").sem, 1)
                    dve.wait_ge(signal("out_ready").sem, signal("out_ready").next(dve))


def kernel(**inputs):
    import numpy as np
    import concourse.bacc as bacc
    from concourse.bass_utils import run_bass_kernel_spmd

    nc = bacc.Bacc("TRN2", target_bir_lowering=False, num_devices=1)
    arrays = {n: np.ascontiguousarray(v) for n, v in inputs.items()}
    arrays["shape_table"] = shape_constants()[0]
    arrays["retention_decay"] = retention_decay()
    aps = {n: nc.dram_tensor(n, v.shape, mybir.dt.from_np(v.dtype), kind="ExternalInput").ap() for n, v in arrays.items()}
    out = nc.dram_tensor("out", (1, S, D), F32, kind="ExternalOutput").ap()
    build(nc, aps, out)
    return run_bass_kernel_spmd(nc, [arrays], core_ids=[0]).results[0]["out"]
```

```python
from contextlib import ExitStack
import math

import concourse.bass as bass
from concourse import mybir

ALU = mybir.AluOpType
ACT = mybir.ActivationFunctionType
F32 = mybir.dt.float32
F32R = mybir.dt.float32r
U32 = mybir.dt.uint32
I32 = mybir.dt.int32
AX_X = mybir.AxisListType.X

P = 128
D = 1024
S = 512
T = S // P
KD = D // P
BANK = 512
N_BANKS = 8

A_HEADS, A_DIM, A_ROT = 4, 64, 16
A_QKV = A_HEADS * 2 * A_DIM
B_HEADS, B_NOPE, B_ROPE, B_V = 8, 64, 32, 64
B_QK = B_NOPE + B_ROPE
B_Q_RANK, B_KV_RANK = 256, 128
EVEN_IN = 3 * A_QKV + B_Q_RANK + B_KV_RANK + B_ROPE
C_HEADS, C_DIM = 16, 64
GRID_W, NA_ROWS, NA_COLS = 64, 8, 16
REL_R, REL_C = 2 * NA_ROWS - 1, 2 * NA_COLS - 1

GROUPS, PER_GROUP, D_EXPERT = 4, 8, 512
EXPERTS = GROUPS * PER_GROUP
ROUTES = GROUPS + EXPERTS
TOP_K = 2
CAP = 96
KE = D_EXPERT // P

RET_HEADS, GDN_HEADS, HEAD = 4, 4, 128
SHORT_CONV, LRU_CONV, FFN_CONV = 4, 4, 3
D_FF = ((8 * D // 3 + 127) // 128) * 128
KF = D_FF // P
FF_COLS = BANK // 2
MIX0_IN = 8 * 512 + 2 * GDN_HEADS
BIG = 16896

ALPHA = 4 ** 0.25
LN_EPS, RMS_EPS = 1e-5, 1e-6
LAMBDA_INIT = 0.8 - 0.6 * math.exp(0.0)
MASKED = -1e30
LEVELS = 7


def shape_constants():
    import numpy as np
    cols, at, n = [], {}, 0

    def put(name, a):
        nonlocal n
        a = np.asarray(a, np.float32).reshape(a.shape[0], -1)
        full = np.zeros((P, a.shape[1]), np.float32)
        full[:a.shape[0]] = a
        cols.append(full)
        at[name] = (n, a.shape[1])
        n += a.shape[1]

    i = np.arange(P)
    put("ident", np.eye(P))
    put("upto", (i[:, None] <= i[None, :]).astype(np.float32))
    put("before", (i[:, None] < i[None, :]).astype(np.float32))
    put("minus_half", np.full((P, 1), -0.5))
    put("eps", np.full((P, 1), RMS_EPS))
    put("iota", np.tile(np.arange(EXPERTS), (P, 1)))

    def rope(theta, rot, name):
        f = np.float32(theta) ** (-np.arange(0, rot, 2, dtype=np.float32) / np.float32(rot))
        ang = np.arange(S, dtype=np.float32)[:, None] * f.astype(np.float32)[None, :]
        for fn, tag in ((np.cos, "cos"), (np.sin, "sin")):
            put(name + tag, fn(ang).reshape(T, P, rot // 2).transpose(1, 0, 2))

    rope(500000.0, A_ROT, "ra_")
    rope(500000.0, B_ROPE, "rb_")
    rope(10000.0, HEAD, "rr_")
    e = np.zeros((64, 2 * GRID_W + GRID_W - 1))
    for r in range(2):
        for m in range(REL_C):
            e[32 * r + m, GRID_W * r + GRID_W - 1 + NA_COLS - 1 - m] = 1.0
    put("hankel", np.concatenate([e, e]))
    c = i % GRID_W
    start = np.clip(c - NA_COLS // 2, 0, GRID_W - NA_COLS)
    j = np.arange(GRID_W)[None, :]
    put("window", np.where((j >= start[:, None]) & (j < start[:, None] + NA_COLS), 0.0, MASKED))
    for l in range(LEVELS):
        s = 1 << l
        jj, ii = i[:, None], i[None, :]
        put(f"level{l}", ((jj // (2 * s) == ii // (2 * s)) & (jj // s % 2 == 0) & (ii // s % 2 == 1)).astype(np.float32))
    return np.concatenate(cols, 1), at


def retention_decay():
    import numpy as np
    h = np.arange(RET_HEADS, dtype=np.float32)
    log_gamma = np.log1p(-np.exp2(-5.0 - h)).astype(np.float64)
    rel = np.arange(S)[None, :] - np.arange(P)[:, None]
    d = np.where(rel >= 0, np.exp(log_gamma[:, None, None] * np.maximum(rel, 0)), 0.0) * HEAD ** -0.5
    return np.ascontiguousarray(d.transpose(1, 0, 2).astype(np.float32))


class Signal:

    def __init__(self, sem):
        self.sem, self.seen = sem, {}

    def next(self, eng, k=1):
        self.seen[id(eng)] = self.seen.get(id(eng), 0) + k
        return self.seen[id(eng)]


class Use:

    def __init__(self, bank, n):
        self.bank, self.n = bank, n


class Plan:

    def __init__(self):
        self.uses = [0] * N_BANKS
        self.at = 0
        self.loads = [0] * 6
        self.splits = [0] * 2
        self.slot = 0
        self.freed = [None] * 6

    def take(self, n=1):
        out = []
        for _ in range(n):
            out.append(Use(self.at, self.uses[self.at]))
            self.uses[self.at] += 1
            self.at = (self.at + 1) % N_BANKS
        return out

    def chunk(self, nk, width, cols, dmas=1, split=True):
        s = self.slot
        self.slot = 2 - s
        self.loads[s] += dmas
        self.splits[s // 2] += split
        return Chunk(s, self.loads[s], self.freed[s], self.splits[s // 2], nk, width, cols)


class Chunk:

    def __init__(self, slot, loads, freed, nth, nk, width, cols):
        self.slot, self.loads, self.freed, self.nth = slot, loads, freed, nth
        self.nk, self.width, self.cols = nk, width, cols
        self.pair = slot // 2


def build(nc, a, out, stages=99):
    table, where = shape_constants()
    ctx = ExitStack()
    with ctx:
        def sb(name, shape, dt=F32):
            return ctx.enter_context(nc.sbuf_tensor(name, shape, dt))

        rounded_view = {}

        def sb_and_rounded(name, shape):
            offset = -(-nc.sbuf_base // 32) * 32
            t = sb(name, shape)
            rounded_view[t.name] = nc.alloc_sbuf_tensor_at(name + "_rounded", shape, F32R, offset=offset)
            return t

        def sem(name):
            return ctx.enter_context(nc.semaphore(name))

        ring = sb_and_rounded("ring", [P, 4, 8 * BANK])
        big = sb_and_rounded("big", [P, BIG])
        X = sb("X", [P, T, D])
        XH = sb_and_rounded("XH", [P, T, D])
        XT = sb_and_rounded("XT", [P, KD, S])
        const = sb_and_rounded("const", [P, table.shape[1]])
        lnp = sb("lnp", [P, 2, D])
        router = sb_and_rounded("router", [P, 2, KD, ROUTES])
        ba_w = sb_and_rounded("ba_w", [P, KD, 2 * GDN_HEADS])
        chan = sb("chan", [P, 560])
        bc = sb("bc", [P, 976])
        st = sb("st", [P, 640])
        ones = sb("ones", [P, P])
        rel_sb = sb_and_rounded("rel_sb", [P, C_HEADS * 2 * NA_ROWS])

        def k(name):
            o, w = where[name]
            return const[:, o:o + w]

        ident = k("ident")
        ba_hi = router[:, 0, :, 0:2 * GDN_HEADS]
        slots = [ring[:, i, :] for i in range(4)] + [big[:, 0:4096], big[:, 4096:8192]]

        psum = [ctx.enter_context(nc.psum_tensor(f"bank{i}", [P, BANK], F32)) for i in range(N_BANKS)]
        full = [sem(f"bank{i}_full") for i in range(N_BANKS)]
        drained = [sem(f"bank{i}_drained") for i in range(N_BANKS)]
        loaded = [sem(f"slot{i}_loaded") for i in range(6)]
        rounded = [sem(f"pair{i}_rounded") for i in range(2)]
        split = [sem(f"pair{i}_split") for i in range(2)]

        dve_done = Signal(sem("dve_done"))
        act_done = Signal(sem("act_done"))
        pool_done = Signal(sem("pool_done"))
        sig = {}

        def signal(name):
            if name not in sig:
                sig[name] = Signal(sem(name))
            return sig[name]

        def late(l, name):
            return signal(f"late{l}_{name}").sem

        def overflow(eng, waits=True):
            if waits:
                eng.wait_ge(signal("slots_ready").sem, signal("slots_ready").next(eng))
            return eng.value_load(n_over[0:1, 0:1], min_val=0, max_val=S)

        def ps(u):
            return psum[u.bank]

        plan = Plan()
        U, W = {}, {}

        def plan_linear(name, n, nk=KD, width=BANK, per_chunk=T, dmas=1, split=True):
            W[name], U[name] = [], []
            for o in range(0, n, width):
                c = plan.chunk(nk, width, min(width, n - o), dmas, split)
                u = plan.take(per_chunk)
                plan.freed[c.slot] = ("bank", u[-1])
                W[name].append(c)
                U[name].append(u)

        def bias_blocks(g, groups):
            n = GRID_W // 4
            if g == 0:
                return [(0, b) for b in range(n)]
            share = n // (groups // 2)
            return [(1, share * (g - 1) + b) for b in range(share)] if g <= groups // 2 else []

        def plan_attention(name, groups, maps, outs, bias):
            U[name] = dict(qk=[None] * groups, bias=[None] * groups, s=[], t=[], o=[])
            n = groups * T
            u = U[name]

            def group(g):
                u["qk"][g] = plan.take(2)
                if bias:
                    u["bias"][g] = list(zip(bias_blocks(g, groups), plan.take(len(bias_blocks(g, groups)))))

            group(0)
            for i in range(n + 3):
                if i < n:
                    u["s"].append(plan.take(maps))
                    if i % T == 2 and i // T + 1 < groups:
                        group(i // T + 1)
                if 2 <= i < n + 2:
                    u["t"].append(plan.take(outs))
                if i >= 3:
                    u["o"].append(plan.take(outs))

        def plan_moe(l):
            U[f"route{l}"] = plan.take(T + 1)
            base = list(plan.uses)
            U[f"moe{l}"] = base
            plan.freed[4] = plan.freed[5] = ("bank", U[f"route{l}"][0])
            plan.freed[1], plan.freed[3] = plan.freed[0], plan.freed[2]
            W[f"moe{l}"] = (list(plan.loads), list(plan.freed))
            for b in range(7):
                plan.uses[b] += EXPERTS
            for s in range(6):
                plan.loads[s] += EXPERTS
            plan.freed[0] = ("bank", Use(3, base[3] + EXPERTS - 1))
            plan.freed[2] = ("bank", Use(6, base[6] + EXPERTS - 1))
            plan.slot = 0

        def plan_ffn(l):
            plan_linear(f"ffn{l}_up", KF * FF_COLS, per_chunk=4, dmas=2)
            n = (KF + 3) // 4
            W[f"ffn{l}_down"] = [plan.chunk(min(4, KF - 4 * i), D, D) for i in range(n)]
            U[f"ffn{l}_down"] = plan.take(N_BANKS)
            for i, c in enumerate(W[f"ffn{l}_down"]):
                if i >= 2:
                    c.freed = ("down", l * (n - 1) + i - 1)
                plan.freed[c.slot] = ("bank", U[f"ffn{l}_down"][-1]) if i == n - 1 else ("down", l * (n - 1) + i + 1)

        U["x_T"] = plan.take(KD)
        plan_linear("even_in", EVEN_IN)
        U["chan"] = plan.take(2)
        U["rel"] = plan.take(1)
        U["lat_T"] = plan.take(3)
        plan_linear("uq", B_HEADS * B_QK, 2, B_HEADS * B_QK, 2 * T, split=False)
        plan_linear("ukv", B_HEADS * 128, 1, B_HEADS * 128, 2 * T, split=False)
        plan_attention("A", A_HEADS, 2, 1, False)
        plan_attention("B", B_HEADS, 1, 1, False)
        U["o0_T"] = plan.take(KD)
        plan_linear("even_o", D)
        U["ln10_T"] = plan.take(KD)
        plan_moe(0)
        U["ln20_T"] = plan.take(KD)
        plan_linear("qkv", 3 * D)
        plan_attention("C", C_HEADS // 2, 2, 2, True)
        U["o1_T"] = plan.take(KD)
        plan_linear("odd_o", D)
        scores = U["C"]["s"]
        for c, v in zip(W["odd_o"], (scores[len(scores) // 2 - 1], scores[-1])):
            c.freed = ("scores", v[1])
        U["ln11_T"] = plan.take(KD)
        plan_moe(1)
        U["rms0_T"] = plan.take(KD)
        plan_linear("mix_in", 8 * BANK)
        U["ba"] = plan.take(1)
        U["l2"], U["ret"] = [], []
        for _ in range(RET_HEADS):
            U["l2"] += plan.take(2)
            U["ret"].append(dict(qk=plan.take(2), s=plan.take(T), o=plan.take(1)))

        def plan_level(l):
            first = plan.take(2)
            return [(t1, plan.take(1)[0] if l < LEVELS - 1 else None, plan.take(1)[0]) for t1 in first]

        U["gdn"] = [dict(gc=plan.take(2), kk=plan.take(1), kq=plan.take(1), kt=plan.take(1), vt=plan.take(1),
                         inv=[plan_level(l) for l in range(LEVELS)], u=plan.take(1), w=plan.take(1), ws=plan.take(1),
                         o=plan.take(1), s=plan.take(1)) for _ in range(T)]
        U["y_T"] = plan.take(KD)
        plan_linear("mix_out", D)
        U["rmsf0_T"] = plan.take(KD)
        plan_ffn(0)
        U["rms1_T"] = plan.take(KD)
        plan_linear("lru_in", 2 * D)
        U["lru"] = [plan.take(2) for _ in range(KD)]
        plan_linear("lru_out", D)
        U["rmsf1_T"] = plan.take(KD)
        plan_ffn(1)

        def carve(spec, base=0):
            views, o = {}, base
            for name, shape in spec:
                n = math.prod(shape)
                v = big[:, o:o + n]
                dims = [f"d{i}" for i in range(len(shape))]
                if len(shape) > 1:
                    v = v.rearrange(f"p ({' '.join(dims)}) -> p {' '.join(dims)}", **dict(zip(dims, shape)))
                views[name] = v
                o += n
            assert o <= BIG, (o, [s[0] for s in spec])
            return views

        E = carve([("H", (T, EVEN_IN)), ("KC", (T, B_HEADS, B_QK)), ("QKT", (2, 2, S)), ("p", (2, 2, S)), ("WT", (2, 1, T, P))])
        E["QB"] = XT[:, 0:6, :].rearrange("p a b -> p (a b)").rearrange("p (t h d) -> p t h d", t=T, h=B_HEADS)
        E["VB"] = lnp[:, :, :].rearrange("p a b -> p (a b)").rearrange("p (t h d) -> p t h d", t=T, h=B_HEADS)
        E["latT"] = E["p"].rearrange("p a b s -> p (a b) s")
        E["tmp"] = E["QKT"].rearrange("p a b s -> p (a b) s")
        C = carve([("H", (T, 3 * D)), ("QKT", (2, 2, S)), ("p", (2, 2, S))])
        for b, third in ((E, ring[:, 3, 0:2 * S].rearrange("p (m s) -> p m s", m=2)), (C, XT[:, 0:2, :])):
            b["p"] = [b["p"][:, 0, :, :], b["p"][:, 1, :, :], third]
        C["WT"] = lnp[:, :, :].rearrange("p b (o t q) -> p b o t q", o=2, t=T)
        C["bias"] = [ring[:, 2 * i:2 * i + 2, :].rearrange("p a c -> p (a c)").rearrange("p (b h s j) -> p b h s j", h=2, s=16, j=GRID_W)
                     for i in range(2)]
        M = carve([("XE", (2, D)), ("XET", (2, KD, CAP)), ("hid", (2, D_EXPERT)), ("HT", (2, KE, CAP)), ("YE", (2, D))], 8192)
        M["XET_lo"] = XH[:, 0:2, 0:KD * CAP].rearrange("p b (k c) -> p b k c", k=KD)
        M["HT_lo"] = XH[:, 2:4, 0:KE * CAP].rearrange("p b (k c) -> p b k c", k=KE)
        M["lhid"] = big[:, 12288:12288 + D_EXPERT]
        M["lHT"] = big[:, 12800:12800 + KE * P].rearrange("p (k c) -> p k c", k=KE)
        M["YG"] = big[:, 8192:8192 + T * D].rearrange("p (t d) -> p t d", t=T)
        R = carve([("A", (T, TOP_K, EXPERTS)), ("tmp", (T, TOP_K, EXPERTS)), ("M", (T, EXPERTS)), ("L", (T, ROUTES)),
                   ("LP", (T, 8)), ("g8", (T, 8)), ("e8", (T, 8)), ("v8", (T, 8)), ("sel", (T, 8, GROUPS)), ("Mc", (T + 1, EXPERTS))], 15616)
        N_ = carve([("GR", (T, 512)), ("GD", (T, 512)), ("QKVT", (12, S)), ("VR", (T, 512)), ("RQK", (T, 1024))])
        N_["rt"] = lnp[:, :, :].rearrange("p a b -> p (a b)").rearrange("p (a h d) -> p a h d", a=4, d=HEAD // 2)
        N_["QKT"] = XT[:, 0:4, :].rearrange("p (b a) s -> p b a s", b=2)
        N_["sc"] = XT[:, 4:7, :].rearrange("p a s -> p (a s)")
        N_["dret"] = lnp[:, :, :].rearrange("p a b -> p (a b)").rearrange("p (h s) -> p h s", h=RET_HEADS)
        gdn_names = ("kg", "v", "ktail", "attnT", "InvT", "Inv", "LT", "dec", "eg", "ub", "wT", "qd")
        l2_buf = [XH[:, i, 512:1024] for i in range(4)]
        G = {n: big[:, 10752 + 512 * i:10752 + 512 * (i + 1)].rearrange("p (h c) -> p h c", h=GDN_HEADS)
             for i, n in enumerate(gdn_names)}
        for i, n in enumerate(("CT", "T1", "vn", "S", "sq", "rn", "gm", "t2")):
            G[n] = XT[:, i, :].rearrange("p (h c) -> p h c", h=GDN_HEADS)
        CT = (G["CT"], lnp[:, 0, 0:512].rearrange("p (h c) -> p h c", h=GDN_HEADS))

        y_sq = lnp[:, 1, :]

        def pair(q):
            return slice(2 * q, 2 * q + 2)

        F_ = carve([("act", (KF, S)), ("cg", (2, S)), ("cv", (2, S)), ("hi", (7, S))])

        def act_hi(f):
            if f < 7:
                return F_["hi"][:, f, :]
            if f < 7 + KD:
                return XT[:, f - 7, :]
            return XH[:, :, :].rearrange("p t d -> p (t d)")[:, (f - 7 - KD) * S:(f - 6 - KD) * S]

        x_lo = big[:, 3 * T * D:4 * T * D].rearrange("p (t d) -> p t d", t=T)
        L_ = carve([("gate", (KD, S)), ("xr", (KD, S)), ("i", (KD, S)), ("w", (2, KD, P)), ("q", (2, S)), ("u", (S,))])
        xs = nc.dram_tensor("expert_rows", [EXPERTS * CAP, D], F32).ap()
        ys = nc.dram_tensor("expert_out", [EXPERTS * CAP, D], F32).ap()
        idx = sb("idx", [P, 2 * T * TOP_K], U32)
        n_over = sb("n_over", [1, 1], I32)
        chan_at, n_chan = {}, 0
        for name, rows in (("ln1_g", 16), ("ln1_b", 16), ("ln2_g", 16), ("ln2_b", 16), ("norm_mix_2", 16), ("norm_ffn_2", 16),
                           ("lru_conv_b_2", 8), ("lru_b_a_2", 8), ("lru_b_x_2", 8), ("lru_lambda_2", 8),
                           ("lru_conv_w_2", 32), ("gdn_conv_w_2", 48), ("ffn_conv_w_2", 6 * KF * 2), ("ffn_conv_b_2", 2 * KF * 2)):
            chan_at[name] = n_chan
            n_chan += rows
        bc_at, n_bc = {}, 0
        for name, n in (("even_subln_g", 128), ("even_q_norm_g", 256), ("even_kv_norm_g", 128), ("gdn_out_gain_2", 128),
                        ("even_lam_q1", 64), ("even_lam_k1", 64), ("even_lam_q2", 64), ("even_lam_k2", 64),
                        ("b_router_group", 8), ("b_router_expert", 64), ("gdn_a_log_2", 4), ("gdn_dt_bias_2", 4)):
            bc_at[name] = (n_bc, n)
            n_bc += n

        def bcv(name):
            o, n = bc_at[name]
            return bc[:, o:o + n]

        n_stat = [0]

        def stat(*shape):
            n = math.prod(shape)
            v = st[:, n_stat[0]:n_stat[0] + n]
            n_stat[0] += n
            assert n_stat[0] <= 640
            if len(shape) == 2:
                v = v.rearrange("p (a b) -> p a b", a=shape[0])
            if len(shape) == 3:
                v = v.rearrange("p (a b c) -> p a b c", a=shape[0], b=shape[1])
            return v

        def rep(ap, axis, n):
            ap = ap.unsqueeze(axis)
            shape = list(ap.shape)
            shape[axis] = n
            return ap.broadcast_to(shape)

        sums, negmax, rcp = stat(64), stat(64), stat(64)
        bnst, mv, rstd = stat(T, 2, 6), stat(T, 2), stat(32)
        ssq = stat(32)
        lam = stat(8)
        grp, gw, gsum, ediff = stat(T), stat(T), stat(T), stat(T)
        gdiff, ohg = stat(T, GROUPS), stat(T, GROUPS)
        ek, pos2, over, keep, slotf, wts, wtmp = (stat(T, TOP_K) for _ in range(7))
        gb = stat(T, 2 * GDN_HEADS)
        beta, gg = stat(T, GDN_HEADS), stat(T, GDN_HEADS)
        sp1, sp2, sp3, sp4 = (stat(T, GDN_HEADS) for _ in range(4))
        gcol8, ge8 = stat(2, GDN_HEADS), stat(2, GDN_HEADS)
        cvec, sl1, sl2, sl3 = (stat(KD) for _ in range(4))

        scat, gath = idx[:, 0:8], idx[:, 8:16]
        gidx = sums[:, 0:32].bitcast(U32).rearrange("p (t j) -> p t j", t=T)
        eidx = sums[:, 32:64].bitcast(U32).rearrange("p (t j) -> p t j", t=T)

        def col(name, i):
            return chan[:, chan_at[name] + i:chan_at[name] + i + 1]

        def slot_kn(s, nk=KD, n=BANK):
            return slots[s][:, 0:nk * n].rearrange("p (k n) -> p k n", k=nk)

        def raw(c):
            return slot_kn(c.slot, c.nk, c.width)[:, :, 0:c.cols]

        def hi(c):
            return slot_kn(c.slot + 1, c.nk, c.width)[:, :, 0:c.cols]

        def expert_raw(j):
            return half_slot(j // 2, j)

        def expert_hi(j):
            return half_slot(3 + j // 2, j)

        def half_slot(s, j):
            n = 4 * BANK
            return slots[s][:, j % 2 * n:(j % 2 + 1) * n].rearrange("p (k n) -> p k n", k=4)

        GATE, UP, DOWN = (0, 1), (2, 3), (4, 5)

        def nth_split(l, e, j, first=False, last=False):
            before = EXPERTS * 6 * l
            if j in DOWN:
                return e * 6 + (before + j + (1 if last else 5))
            return e * 6 + (before + j + (1 if first else -1))

        def one_pass(ap):
            return bass.AP(rounded_view[ap.tensor.name], ap.offset, ap.ap)

        def parts(ap):
            return one_pass(ap).bitcast(F32)

        def pieces(c):
            return [slice(0, c.nk // 2), slice(c.nk // 2, c.nk)]

        def on(n):
            return stages >= n

        sc_at = [sum(S - P * i for i in range(kc)) for kc in range(T)]

        att = {
            "A": dict(groups=A_HEADS, maps=2, outs=1, rows=A_DIM, scale=A_DIM ** -0.5, buf=E, dv=128,
                      q=lambda g, t: E["H"][:, t, 128 * g:128 * g + 128],
                      k=lambda g, t: E["H"][:, t, A_QKV + 128 * g:A_QKV + 128 * g + 128], width=128,
                      v=lambda g, o, kt: E["H"][:, kt, 2 * A_QKV + 128 * g:2 * A_QKV + 128 * g + 128],
                      o=lambda g, o, t: XH[:, t, 128 * g:128 * g + 128]),
            "B": dict(groups=B_HEADS, maps=1, outs=1, rows=B_QK, scale=B_QK ** -0.5, buf=E, dv=B_V,
                      q=lambda g, t: E["QB"][:, t, g, :], k=lambda g, t: E["KC"][:, t, g, :], width=B_QK,
                      v=lambda g, o, kt: E["VB"][:, kt, g, :],
                      o=lambda g, o, t: XH[:, t, 512 + B_V * g:512 + B_V * g + B_V]),
            "C": dict(groups=C_HEADS // 2, maps=2, outs=2, rows=C_DIM, scale=C_DIM ** -0.5, buf=C, dv=C_DIM,
                      q=lambda g, t: C["H"][:, t, 128 * g:128 * g + 128],
                      k=lambda g, t: C["H"][:, t, D + 128 * g:D + 128 * g + 128], width=128,
                      v=lambda g, o, kt: C["H"][:, kt, 2 * D + 128 * g + 64 * o:2 * D + 128 * g + 64 * o + 64],
                      o=lambda g, o, t: XH[:, t, 128 * g + 64 * o:128 * g + 64 * o + 64]),
        }

        block = ctx.enter_context(nc.Block())
        chan_dmas = []

        @block.sync
        def _(sp):
            def load(c, dst, src):
                slot = c.slot
                if c.freed is not None:
                    kind, by = c.freed
                    if kind == "bank":
                        sp.wait_ge(full[by.bank], by.n + 1)
                    elif kind == "scores":
                        sp.wait_ge(drained[by.bank], by.n + 1)
                    else:
                        sp.wait_ge(signal("down_used").sem, by)
                sp.dma_start(dst, src).then_inc(loaded[slot], 16)

            def load_cols(name, w, n, nk=KD, width=BANK):
                v = w.rearrange("(k p) n -> p k n", p=P)
                for i, c in enumerate(W[name]):
                    m = min(width, n - i * width)
                    load(c, raw(c), v[:, :, i * width:i * width + m])

            def load_experts(l):
                n0, freed = W[f"moe{l}"]
                base = U[f"moe{l}"]

                def expert_half(e, j):
                    w = a[("w_gate", "w_up", "w_down")[j // 2]][l][e]
                    if j in DOWN:
                        v = w.rearrange("(k p) (h n) -> h p k n", p=P, h=2)
                    else:
                        v = w.rearrange("(h k p) n -> h p k n", p=P, h=2)
                    sp.dma_start(expert_raw(j), v[j % 2]).then_inc(loaded[j], 16)

                def next_gate_up(e):
                    for b, js in ((2, GATE), (3, UP)):
                        sp.wait_ge(full[b], e + (base[b] + 1))
                        for j in js:
                            expert_half(e + 1, j)

                def next_down(e):
                    for b, j in ((5, DOWN[0]), (6, DOWN[1])):
                        sp.wait_ge(full[b], e + base[b])
                        expert_half(e, j)

                sp.wait_ge(full[freed[2][1].bank], freed[2][1].n + 1)
                for j in GATE + UP + DOWN:
                    expert_half(0, j)
                next_gate_up(0)
                with sp.Fori(1, EXPERTS - 1) as e:
                    next_gate_up(e)
                    next_down(e)
                next_down(EXPERTS - 1)
                with sp.If(overflow(sp) > 0):
                    for b in (2, 3, 6):
                        sp.wait_ge(full[b], base[b] + EXPERTS)

                    def weights(e):
                        for j, name in enumerate(("w_gate", "w_up", "w_down")):
                            nk, n = (KE, D) if j == 2 else (KD, D_EXPERT)
                            sp.dma_start(slot_kn(j, nk, n), a[name][l][e].rearrange("(k p) n -> p k n", p=P)).then_inc(
                                late(l, "loaded"), 16)

                    weights(0)
                    with sp.Fori(1, EXPERTS) as e:
                        sp.wait_ge(late(l, "added"), e * T)
                        weights(e)
                    sp.wait_ge(late(l, "added"), EXPERTS * T)
                for t in range(T):
                    sp.wait_ge(signal(f"rows_back{t}").sem, 16 * TOP_K * (l + 1))

            def load_ffn(l):
                up = a["ffn_w_up_2"][l].rearrange("(k p) (h n) -> p k h n", p=P, h=2)
                for i, c in enumerate(W[f"ffn{l}_up"]):
                    if c.freed is not None:
                        sp.wait_ge(full[c.freed[1].bank], c.freed[1].n + 1)
                    dst = slot_kn(c.slot).rearrange("p k (h n) -> p k h n", h=2)
                    for h in range(2):
                        sp.dma_start(dst[:, :, h, :], up[:, :, h, i * FF_COLS:(i + 1) * FF_COLS]).then_inc(loaded[c.slot], 16)
                down = a["ffn_w_down_2"][l].rearrange("(k p) n -> p k n", p=P)
                for i, c in enumerate(W[f"ffn{l}_down"]):
                    load(c, raw(c), down[:, 4 * i:4 * i + c.nk, :])

            sp.dma_start(X[:, :, :], a["x"][0].rearrange("(t p) d -> p t d", p=P)).then_inc(signal("x_loaded").sem, 16)
            load_cols("even_in", a["even_w_in"][0], EVEN_IN)
            load_cols("uq", a["even_w_uq"][0], B_HEADS * B_QK, 2, B_HEADS * B_QK)
            load_cols("ukv", a["even_w_ukv"][0], B_HEADS * 128, 1, B_HEADS * 128)
            load_cols("even_o", a["even_w_o"][0], D)
            if on(4):
                load_experts(0)
            if on(5):
                load_cols("qkv", a["odd_w_qkv"][0], 3 * D)
                load_cols("odd_o", a["odd_w_o"][0], D)
            if on(6):
                load_experts(1)
            if on(7):
                load_cols("mix_in", a["ret_gdn_w_in_2"][0], 8 * BANK)
                load_cols("mix_out", a["ret_gdn_w_out_2"][0], D)
            if on(8):
                load_ffn(0)
            if on(9):
                load_cols("lru_in", a["lru_w_in_2"][0], 2 * D)
                load_cols("lru_out", a["lru_w_out_2"][0], D)
            if on(10):
                load_ffn(1)
            sp.wait_ge(signal("out_ready").sem, signal("out_ready").next(sp, T))
            sp.dma_start(out[0].rearrange("(t p) d -> p t d", p=P), XH[:, :, :]).then_inc(signal("out_stored").sem, 16)
            sp.wait_ge(signal("out_stored").sem, signal("out_stored").next(sp, 16))

        @block.gpsimd
        def _(pool):
            def power(dst, src, mul, add, ready, told):
                pool.wait_ge(signal(ready).sem, signal(ready).next(pool))
                pool.tensor_scalar(dst, src, mul, add, ALU.mult, ALU.add).then_inc(pool_done.sem, 1)
                pool.wait_ge(pool_done.sem, pool_done.next(pool))
                pool.tensor_tensor(dst, dst, k("minus_half").broadcast_to(list(dst.shape)), ALU.pow).then_inc(signal(told).sem, 1)
                pool.wait_ge(signal(told).sem, signal(told).next(pool))

            def norm_params(g, b):
                for i, v in enumerate((g, b)):
                    pool.dma_start(lnp[:, i, :], v.partition_broadcast(P)).then_inc(signal("ln_loaded").sem, 16)

            def layer_norm():
                power(rstd[:, 0:T], mv[:, :, 1], 1.0, LN_EPS, "ln_stats", "rstd_ready")
                pool.wait_ge(signal("ln_loaded").sem, signal("ln_loaded").next(pool, 32))
                for t in range(T):
                    pool.wait_ge(signal("xh_ready").sem, signal("xh_ready").next(pool))
                    pool.tensor_tensor(X[:, t, :], XH[:, t, :], lnp[:, 0, :], ALU.mult).then_inc(pool_done.sem, 1)
                    pool.wait_ge(pool_done.sem, pool_done.next(pool))
                    pool.tensor_tensor(X[:, t, :], X[:, t, :], lnp[:, 1, :], ALU.add).then_inc(signal("x_applied").sem, 1)
                    pool.wait_ge(signal("x_applied").sem, signal("x_applied").next(pool))

            def to_experts(l):
                pool.wait_ge(signal("slots_ready").sem, signal("slots_ready").next(pool))
                for t in range(T):
                    for j in range(TOP_K):
                        pool.indirect_dma_start(
                            xs, bass.IndirectOffsetOnAxis(ap=scat[:, TOP_K * t + j:TOP_K * t + j + 1], axis=0),
                            X[:, t, :], None, bounds_check=EXPERTS * CAP - 1, oob_is_err=False,
                        ).then_inc(signal("rows_sent").sem, 16)

            def from_experts(l):
                for half in range(2):
                    pool.wait_ge(signal(f"y_stored{half}").sem, 16 * (EXPERTS // 2) * (l + 1))
                for t in range(T):
                    for j, dst in enumerate((XH[:, t, :], M["YG"][:, t, :])):
                        pool.indirect_dma_start(
                            dst, None, ys, bass.IndirectOffsetOnAxis(ap=gath[:, TOP_K * t + j:TOP_K * t + j + 1], axis=0),
                        ).then_inc(signal(f"rows_back{t}").sem, 16)

            pool.memset(ones[:, :], 1.0).then_inc(signal("ones_ready").sem, 1)
            pool.wait_ge(signal("ones_ready").sem, signal("ones_ready").next(pool))
            pool.memset(lnp[:, 0, :], 0.0).then_inc(pool_done.sem, 1)
            pool.wait_ge(pool_done.sem, pool_done.next(pool))
            pool.wait_ge(loaded[0], 16 * W["even_in"][2].loads)
            pool.dma_start(xs.rearrange("(n p) d -> p n d", p=P), rep(lnp[:, 0, :], 1, EXPERTS * CAP // P)).then_inc(
                signal("rows_zeroed").sem, 16)
            pool.wait_ge(signal("table_loaded").sem, signal("table_loaded").next(pool, 16))
            pool.wait_ge(signal("lat_ssq").sem, signal("lat_ssq").next(pool))
            pool.tensor_scalar(rstd[:, 0:T], ssq[:, 0:T], 1.0 / B_Q_RANK, RMS_EPS, ALU.mult, ALU.add).then_inc(pool_done.sem, 1)
            pool.wait_ge(pool_done.sem, pool_done.next(pool))
            pool.tensor_scalar(rstd[:, T:2 * T], ssq[:, T:2 * T], 1.0 / B_KV_RANK, RMS_EPS, ALU.mult, ALU.add).then_inc(
                pool_done.sem, 1)
            pool.wait_ge(pool_done.sem, pool_done.next(pool))
            pool.tensor_tensor(rstd[:, 0:2 * T], rstd[:, 0:2 * T], k("minus_half").broadcast_to([P, 2 * T]), ALU.pow).then_inc(
                signal("rstd_ready").sem, 1)
            pool.wait_ge(signal("rstd_ready").sem, signal("rstd_ready").next(pool))
            if on(2):
                power(rstd[:, 0:16], ssq[:, 0:16], 1.0 / 128, RMS_EPS, "a_ssq", "rstd_ready")
            if on(3):
                pool.wait_ge(full[U["o0_T"][0].bank], U["o0_T"][0].n + 1)
                norm_params(a["ln1_g"][0], a["ln1_b"][0])
                layer_norm()
            if on(4):
                pool.wait_ge(signal("rows_zeroed").sem, signal("rows_zeroed").next(pool, 16))
                norm_params(a["ln2_g"][0], a["ln2_b"][0])
                to_experts(0)
                from_experts(0)
                layer_norm()
            if on(5):
                pool.wait_ge(full[U["o1_T"][0].bank], U["o1_T"][0].n + 1)
                norm_params(a["ln1_g"][1], a["ln1_b"][1])
                layer_norm()
            if on(6):
                norm_params(a["ln2_g"][1], a["ln2_b"][1])
                to_experts(1)
                from_experts(1)
                power(rstd[:, 0:T], mv[:, :, 1], 1.0, LN_EPS, "ln_stats", "rstd_ready")

            def rms():
                for t in range(T):
                    power(rstd[:, t:t + 1], ssq[:, t:t + 1], 1.0 / D, RMS_EPS, "x_ssq", "rstd_ready")

            if on(7):
                rms()
                for us in [r["o"] for r in U["ret"]] + [U["mix_in"][7]]:
                    for u in us:
                        pool.wait_ge(drained[u.bank], u.n + 1)
                for t in range(T):
                    gd = N_["GD"][:, t, :].rearrange("p (h d) -> p h d", d=128)
                    ins = pool.tensor_tensor(gd, gd, rep(bcv("gdn_out_gain_2"), 1, GDN_HEADS), ALU.mult)
                    if t == T - 1:
                        ins.then_inc(signal("gate_gained").sem, 1)
                        pool.wait_ge(signal("gate_gained").sem, signal("gate_gained").next(pool))
                    else:
                        ins.then_inc(pool_done.sem, 1)
                        pool.wait_ge(pool_done.sem, pool_done.next(pool))
                for t in range(T):
                    heads8 = slice(8 * t, 8 * t + 8)
                    if t < T - 1:
                        pool.wait_ge(drained[U["gdn"][t]["o"][0].bank], U["gdn"][t]["o"][0].n + 1)
                        pool.tensor_tensor(y_sq, XH[:, t, :], XH[:, t, :], ALU.mult).then_inc(signal("y_squared").sem, 1)
                        pool.wait_ge(signal("y_squared").sem, signal("y_squared").next(pool))
                    power(rstd[:, heads8], ssq[:, heads8], 1.0 / 128, RMS_EPS, "y_ssq", "rstd_ready")
                    if t < T - 1:
                        y = XH[:, t, :].rearrange("p (h d) -> p h d", d=128)
                        pool.tensor_tensor(y, y, rep(rstd[:, heads8], 2, 128), ALU.mult).then_inc(pool_done.sem, 1)
                        pool.wait_ge(pool_done.sem, pool_done.next(pool))
                        pool.tensor_tensor(XH[:, t, 0:512], XH[:, t, 0:512], N_["GR"][:, t, :], ALU.mult).then_inc(pool_done.sem, 1)
                        pool.wait_ge(pool_done.sem, pool_done.next(pool))
                        pool.tensor_tensor(XH[:, t, 512:1024], XH[:, t, 512:1024], N_["GD"][:, t, :], ALU.mult).then_inc(
                            signal("y_ready").sem, 1)
                        pool.wait_ge(signal("y_ready").sem, signal("y_ready").next(pool))
            if on(8):
                rms()
            if on(9):
                rms()
                for m in range(KD):
                    pool.wait_ge(signal("lru_root").sem, signal("lru_root").next(pool))
                    pool.tensor_tensor(XT[:, m, :], XT[:, m, :], L_["i"][:, m, :], ALU.mult).then_inc(signal("lru_in").sem, 1)
                    pool.wait_ge(signal("lru_in").sem, signal("lru_in").next(pool))
            if on(10):
                rms()
            if on(11):
                pool.dma_start(lnp[:, 0, :], a["norm_final_2"].partition_broadcast(P)).then_inc(signal("ln_loaded").sem, 16)
                rms()

        @block.scalar
        def _(act):
            def load(dst, src, name="small_loaded"):
                act.dma_start(dst, src).then_inc(signal(name).sem, 16)

            def transposed(name, dst=XT, gain=None, bias=None, gain_at=0):
                for i, u in enumerate(U[name]):
                    if gain is None:
                        act.wait_ge(full[u.bank], u.n + 1)
                        act.activation(dst[:, i, :], ps(u)[:, :], ACT.Copy).then_inc(drained[u.bank], 1)
                        act.wait_ge(drained[u.bank], u.n + 1)
                    elif bias is None:
                        act.wait_ge(full[u.bank], u.n + 1)
                        act.activation(dst[:, i, :], ps(u)[:, :], ACT.Copy, scale=col(gain, gain_at + i)).then_inc(
                            drained[u.bank], 1)
                        act.wait_ge(drained[u.bank], u.n + 1)
                    else:
                        act.wait_ge(full[u.bank], u.n + 1)
                        act.activation(dst[:, i, :], ps(u)[:, :], ACT.Identity, scale=col(gain, gain_at + i), bias=col(bias, gain_at + i)).then_inc(
                            drained[u.bank], 1)
                        act.wait_ge(drained[u.bank], u.n + 1)

            def round_chunk(c):
                act.wait_ge(loaded[c.slot], 16 * c.loads)
                for ks in pieces(c):
                    act.activation(one_pass(hi(c)[:, ks, :]), raw(c)[:, ks, :], ACT.Copy).then_inc(rounded[c.pair], 1)

            def round_next(name, i):
                if i + 1 < len(W[name]):
                    round_chunk(W[name][i + 1])

            def rounded_T(name, gain=None, bias=None, gain_at=0):
                for i, u in enumerate(U[name]):
                    act.wait_ge(full[u.bank], u.n + 1)
                    dst = one_pass(XT[:, i, :])
                    if gain is None:
                        act.activation(dst, ps(u)[:, :], ACT.Copy).then_inc(signal("xt_rounded").sem, 1)
                    elif bias is None:
                        act.activation(dst, ps(u)[:, :], ACT.Copy, scale=col(gain, gain_at + i)).then_inc(signal("xt_rounded").sem, 1)
                    else:
                        act.activation(dst, ps(u)[:, :], ACT.Identity, scale=col(gain, gain_at + i), bias=col(bias, gain_at + i)).then_inc(signal("xt_rounded").sem, 1)

            def linear(name, dst, n, width=BANK, ahead=1):
                for i, us in enumerate(U[name]):
                    if i + 1 >= ahead:
                        round_next(name, i)
                    m = min(width, n - i * width)
                    for t, u in enumerate(us):
                        act.wait_ge(full[u.bank], u.n + 1)
                        act.activation(dst[:, t, i * width:i * width + m], ps(u)[:, 0:m], ACT.Copy).then_inc(drained[u.bank], 1)
                        act.wait_ge(drained[u.bank], u.n + 1)

            def attention(name, then=None):
                c = att[name]
                u, buf, n = U[name], att[name]["buf"], att[name]["groups"] * T

                def group(g):
                    for j in range(2):
                        v = u["qk"][g][j]
                        act.wait_ge(full[v.bank], v.n + 1)
                        act.activation(buf["QKT"][0:c["width"], g % 2, j, :], ps(v)[0:c["width"], :], ACT.Copy).then_inc(
                            drained[v.bank], 1)
                        act.wait_ge(drained[v.bank], v.n + 1)

                group(0)
                for i in range(n + 2):
                    if then and i == (n // 2 + 6 if name == "C" else 6):
                        round_chunk(W[then][0])
                    if i < n:
                        for m in range(c["maps"]):
                            s = i * c["maps"] + m
                            act.wait_ge(signal("max_ready").sem, signal("max_ready").next(act))
                            v = u["s"][i][m]
                            j = s % 64
                            if name == "C":
                                p = buf["p"][i % 3][:, m, :]
                                act.activation(p, p, ACT.Exp, bias=negmax[:, j:j + 1], accum_out=sums[:, j:j + 1]).then_inc(
                                    signal("exp_done").sem, 1)
                                act.wait_ge(signal("exp_done").sem, signal("exp_done").next(act))
                            else:
                                act.wait_ge(full[v.bank], v.n + 1)
                                act.activation(buf["p"][i % 3][:, m, :], ps(v)[:, :], ACT.Exp, bias=negmax[:, j:j + 1], scale=c["scale"], accum_out=sums[:, j:j + 1]).then_inc(
                                    drained[v.bank], 1)
                                act.wait_ge(drained[v.bank], v.n + 1)
                        if i % T == 2 and i // T + 1 < c["groups"]:
                            group(i // T + 1)
                    if i >= 2:
                        for o in range(c["outs"]):
                            if i >= 4:
                                act.wait_ge(full[u["o"][i - 4][o].bank], u["o"][i - 4][o].n + 1)
                            v = u["t"][i - 2][o]
                            act.wait_ge(full[v.bank], v.n + 1)
                            act.activation(buf["WT"][:, (i - 2) % 2, o, :, :].rearrange("p t q -> p (t q)"), ps(v)[:, :], ACT.Copy).then_inc(
                                drained[v.bank], 1)
                            act.wait_ge(drained[v.bank], v.n + 1)

            def route(l):
                act.wait_ge(signal("gdiff").sem, signal("gdiff").next(act))
                act.activation(gdiff, gdiff, ACT.Exp).then_inc(signal("gexp").sem, 1)
                act.wait_ge(signal("gexp").sem, signal("gexp").next(act))
                act.wait_ge(signal("ediff").sem, signal("ediff").next(act))
                act.activation(ediff, ediff, ACT.Exp).then_inc(signal("eexp").sem, 1)
                act.wait_ge(signal("eexp").sem, signal("eexp").next(act))

            def experts(l):
                base, us = U[f"moe{l}"], U[f"route{l}"]
                n0, freed = W[f"moe{l}"]

                def wait_use(sems, b, e):
                    act.wait_ge(sems[b], e + (base[b] + 1))

                def load_rows(e, half):
                    act.dma_start(M["XE"][0:CAP, half, :], xs.rearrange("(e c) d -> e c d", c=CAP)[e]).then_inc(
                        signal(f"rows_loaded{half}").sem, 16)

                def round_half(e, j):
                    act.wait_ge(loaded[j], e * 16 + 16 * (n0[j] + 1))
                    act.activation(one_pass(expert_hi(j)), expert_raw(j), ACT.Copy).then_inc(signal("half_rounded").sem, 1)

                def rows_T(e, half):
                    for b in range(2):
                        wait_use(full, b, e)
                        act.activation(one_pass(M["XET"][:, half, 4 * b:4 * b + 4, :].rearrange("p k c -> p (k c)")),
                                       psum[b][:, 0:4 * CAP], ACT.Copy).then_inc(signal("rows_rounded").sem, 1)

                def silu(e, half):
                    wait_use(full, 2, e)
                    act.activation(M["hid"][0:CAP, half, :], psum[2][0:CAP, :], ACT.Silu).then_inc(drained[2], 1)

                def hidden_T(e, half):
                    wait_use(full, 4, e)
                    act.activation(one_pass(M["HT"][:, half, :, :].rearrange("p k c -> p (k c)")), psum[4][:, 0:KE * CAP], ACT.Copy).then_inc(signal("hidden_rounded").sem, 1)

                def out_rows(e, half, n, checked):
                    if checked:
                        act.wait_ge(signal(f"y_stored{half}").sem, n * 16 + 16 * (EXPERTS // 2) * l)
                    for h, b in enumerate((5, 6)):
                        wait_use(full, b, e)
                        act.activation(M["YE"][0:CAP, half, h * BANK:(h + 1) * BANK], psum[b][0:CAP, :], ACT.Copy).then_inc(drained[b], 1)
                    for b in (5, 6):
                        wait_use(drained, b, e)
                    act.dma_start(ys.rearrange("(e c) d -> e c d", c=CAP)[e], M["YE"][0:CAP, half, :]).then_inc(
                        signal(f"y_stored{half}").sem, 16)

                def stage(e, half, n, first=False, last=False, load=True, checked=True):
                    if not first:
                        round_half(e - 1, DOWN[0])
                    silu(e, half)
                    if not first:
                        round_half(e - 1, DOWN[1])
                    if not last:
                        round_half(e + 1, GATE[0])
                        rows_T(e + 1, 1 - half)
                        round_half(e + 1, GATE[1])
                    if load:
                        load_rows(e + 3, 1 - half)
                    if not last:
                        round_half(e + 1, UP[0])
                    if not first:
                        out_rows(e - 1, 1 - half, n - 1 + half, checked)
                    hidden_T(e, half)
                    if not last:
                        round_half(e + 1, UP[1])

                act.wait_ge(full[us[0].bank], us[0].n + 1)
                if freed[3] is not None:
                    act.wait_ge(full[freed[3][1].bank], freed[3][1].n + 1)
                for j in GATE + UP:
                    round_half(0, j)
                act.wait_ge(signal("rows_sent").sem, signal("rows_sent").next(act, 16 * T * TOP_K))
                load_rows(0, 0)
                load_rows(1, 1)
                rows_T(0, 0)
                load_rows(2, 0)
                stage(0, 0, 0, first=True)
                stage(1, 1, 0, checked=l > 0)
                stage(2, 0, 1, checked=l > 0)
                with act.Fori(1, EXPERTS // 2 - 2) as i:
                    stage(i * 2 + 1, 1, i)
                    stage(i * 2 + 2, 0, i + 1)
                h = EXPERTS // 2 - 2
                stage(2 * h + 1, 1, h, load=False)
                stage(2 * h + 2, 0, h + 1, load=False)
                stage(2 * h + 3, 1, h + 1, load=False, last=True)
                for j in DOWN:
                    round_half(EXPERTS - 1, j)
                out_rows(EXPERTS - 1, 1, EXPERTS // 2 - 1, True)
                with act.If(overflow(act) > 0):
                    with act.Fori(0, EXPERTS) as i:
                        for t in range(T):
                            act.wait_ge(late(l, "up"), i * T + (t + 1))
                            act.activation(M["lhid"], psum[0][:, :], ACT.Silu).then_inc(late(l, "silu"), 1)
                    act.wait_ge(late(l, "added"), EXPERTS * T)

            def squares(uses, each=None):
                for t in range(T):
                    for u in uses[t] if uses else ():
                        act.wait_ge(drained[u.bank], u.n + 1)
                    if each:
                        act.wait_ge(signal(each).sem, signal(each).next(act))
                    unread = y_sq if uses else XH[:, t, :]
                    act.activation(unread, X[:, t, :], ACT.Square, accum_out=ssq[:, t:t + 1]).then_inc(signal("x_ssq").sem, 1)
                    act.wait_ge(signal("x_ssq").sem, signal("x_ssq").next(act))

            def by_tile(name):
                return list(zip(*U[name]))

            def ffn(l):
                chunks = W[f"ffn{l}_up"] + W[f"ffn{l}_down"]
                for i, us in enumerate(U[f"ffn{l}_up"]):
                    round_chunk(chunks[i + 1])
                    for m in range(2):
                        act.wait_ge(drained[us[2 * m].bank], us[2 * m].n + 1)
                        cg = F_["cg"][:, m, :]
                        act.activation(cg, cg, ACT.Silu).then_inc(signal("ff_silu").sem, 1)
                        act.wait_ge(signal("ff_silu").sem, signal("ff_silu").next(act))
                for c in W[f"ffn{l}_down"][1:]:
                    round_chunk(c)

            load(const[:, :], a["shape_table"], "table_loaded")
            act.wait_ge(signal("table_loaded").sem, signal("table_loaded").next(act, 16))
            rounded_T("x_T")
            for c in W["even_in"][0:2]:
                round_chunk(c)
            n = n_dma = 0
            for name in chan_at:
                v = a[name]
                v = v.rearrange("(r c) -> r c", c=P) if len(v.shape) == 1 else (
                    v.rearrange("l (r c) -> (l r) c", c=P) if len(v.shape) == 2 else v.rearrange("l w (r c) -> (l w r) c", c=P))
                done = 0
                while done < v.shape[0]:
                    r = min(v.shape[0] - done, P - n % P)
                    load(XH[n % P:n % P + r, 0, (n // P) * P:(n // P + 1) * P], v[done:done + r, :], "chan_loaded")
                    done += r
                    n += r
                    n_dma += 1
            rel_rows = a["odd_rel_bias"][0].rearrange("(q h) r c -> q (h r) c", q=2)
            for q in range(2):
                load(XH[0:C_HEADS * REL_R // 2, 1, q * REL_C:(q + 1) * REL_C], rel_rows[q], "chan_loaded")
            chan_dmas.append(n_dma + 2)
            for name in bc_at:
                v = a[name]
                if len(v.shape) == 2:
                    v = v.rearrange("a b -> (a b)")
                load(bcv(name), v.partition_broadcast(P))
            for l in range(2):
                load(router[:, l, :, 0:GROUPS], a["w_router_group"][l].rearrange("(k p) n -> p k n", p=P))
                load(router[:, l, :, GROUPS:ROUTES], a["w_router_expert"][l].rearrange("(k p) n -> p k n", p=P))
            load(ba_w[:, :, :], a["ret_gdn_w_in_2"][0].rearrange("(k p) n -> p k n", p=P)[:, :, 8 * BANK:MIX0_IN])
            linear("even_in", E["H"], EVEN_IN, ahead=2)
            act.activation(one_pass(k("hankel")), k("hankel"), ACT.Copy).then_inc(signal("hankel_rounded").sem, 1)
            act.wait_ge(full[U["chan"][0].bank], U["chan"][0].n + 1)
            act.activation(chan[:, 0:512], ps(U["chan"][0])[:, :], ACT.Copy).then_inc(drained[U["chan"][0].bank], 1)
            act.wait_ge(drained[U["chan"][0].bank], U["chan"][0].n + 1)
            act.wait_ge(full[U["chan"][1].bank], U["chan"][1].n + 1)
            act.activation(chan[:, 512:n_chan], ps(U["chan"][1])[:, 0:n_chan - 512], ACT.Copy).then_inc(
                drained[U["chan"][1].bank], 1)
            act.wait_ge(drained[U["chan"][1].bank], U["chan"][1].n + 1)
            act.wait_ge(signal("small_loaded").sem, signal("small_loaded").next(act, 16 * (len(bc_at) + 5)))
            for j, (o, w) in enumerate(((3 * A_QKV, B_Q_RANK), (3 * A_QKV + B_Q_RANK, B_KV_RANK))):
                for t in range(T):
                    ins = act.activation(E["tmp"][:, 0, 0:w], E["H"][:, t, o:o + w], ACT.Square,
                                         accum_out=ssq[:, j * T + t:j * T + t + 1])
                    if j == 1 and t == T - 1:
                        ins.then_inc(signal("lat_ssq").sem, 1)
                        act.wait_ge(signal("lat_ssq").sem, signal("lat_ssq").next(act))
                    else:
                        ins.then_inc(act_done.sem, 1)
                        act.wait_ge(act_done.sem, act_done.next(act))
            act.wait_ge(signal("lam_dots").sem, signal("lam_dots").next(act))
            act.activation(lam[:, 0:2], lam[:, 0:2], ACT.Exp).then_inc(signal("lam_exp").sem, 1)
            act.wait_ge(signal("lam_exp").sem, signal("lam_exp").next(act))
            transposed("lat_T", E["latT"])
            act.wait_ge(signal("rows_zeroed").sem, signal("rows_zeroed").next(act, 16))
            for t in range(T):
                for j in range(2):
                    u = U["uq"][0][2 * t + j]
                    act.wait_ge(full[u.bank], u.n + 1)
                    act.activation(E["QB"][:, t, 4 * j:4 * j + 4, :], ps(u)[:, 0:4 * B_QK].rearrange("p (h d) -> p h d", h=4), ACT.Copy).then_inc(
                        drained[u.bank], 1)
                    act.wait_ge(drained[u.bank], u.n + 1)
            for t in range(T):
                for j in range(2):
                    u = U["ukv"][0][2 * t + j]
                    kv = ps(u)[:, :].rearrange("p (h d) -> p h d", h=4)
                    act.wait_ge(full[u.bank], u.n + 1)
                    act.activation(E["KC"][:, t, 4 * j:4 * j + 4, 0:B_NOPE], kv[:, :, 0:B_NOPE], ACT.Copy).then_inc(act_done.sem, 1)
                    act.wait_ge(act_done.sem, act_done.next(act))
                    act.activation(E["VB"][:, t, 4 * j:4 * j + 4, :], kv[:, :, B_NOPE:], ACT.Copy).then_inc(drained[u.bank], 1)
                    act.wait_ge(drained[u.bank], u.n + 1)
            if on(2):
                attention("A")
                attention("B", "even_o")
                rounded_T("o0_T")
                round_chunk(W["even_o"][1])
            if on(3):
                transposed("ln10_T", gain="ln1_g", bias="ln1_b")
            if on(4):
                route(0)
                experts(0)
                for c in W["qkv"][0:1]:
                    round_chunk(c)
                rounded_T("ln20_T", gain="ln2_g", bias="ln2_b")
            if on(5):
                linear("qkv", C["H"], 3 * D)
                act.wait_ge(signal("x_applied").sem, signal("x_applied").next(act, 2 * T))
                attention("C", "odd_o")
                rounded_T("o1_T")
                round_chunk(W["odd_o"][1])
                transposed("ln11_T", gain="ln1_g", bias="ln1_b", gain_at=KD)
            if on(6):
                route(1)
                experts(1)
            if on(7):
                round_chunk(W["mix_in"][0])
                act.wait_ge(signal("x_applied").sem, signal("x_applied").next(act, T))
                squares(None, "x_applied")
                rounded_T("rms0_T", gain="norm_mix_2")
                for i in range(8):
                    round_next("mix_in", i)
                    if i == 7:
                        act.wait_ge(signal("rotated").sem, signal("rotated").next(act))
                        load(N_["dret"], a["retention_decay"], "decay_loaded")
                    us = U["mix_in"][i]
                    if i in (4, 5, 6):
                        for m, u in enumerate(us):
                            act.wait_ge(drained[u.bank], u.n + 1)
                            v = N_["QKVT"][:, 4 * (i - 4) + m, :]
                            act.activation(v, v, ACT.Silu).then_inc(signal("conv_silu").sem, 1)
                            act.wait_ge(signal("conv_silu").sem, signal("conv_silu").next(act))
                        continue
                    dst = {0: N_["RQK"][:, :, 0:512], 1: N_["RQK"][:, :, 512:1024], 2: N_["VR"], 3: N_["GR"], 7: N_["GD"]}[i]
                    for t, u in enumerate(us):
                        act.wait_ge(full[u.bank], u.n + 1)
                        act.activation(dst[:, t, :], ps(u)[:, :], ACT.Silu if i in (3, 7) else ACT.Copy).then_inc(
                            drained[u.bank], 1)
                        act.wait_ge(drained[u.bank], u.n + 1)
                act.wait_ge(signal("ab_ready").sem, signal("ab_ready").next(act))
                act.activation(beta, gb[:, :, 0:GDN_HEADS], ACT.Tanh, scale=0.5).then_inc(act_done.sem, 1)
                act.wait_ge(act_done.sem, act_done.next(act))
                act.activation(sp1, sp1, ACT.Exp, scale=-1.0).then_inc(act_done.sem, 1)
                act.wait_ge(act_done.sem, act_done.next(act))
                act.activation(lam[:, 4:8], bcv("gdn_a_log_2"), ACT.Exp).then_inc(signal("ab_exp").sem, 1)
                act.wait_ge(signal("ab_exp").sem, signal("ab_exp").next(act))
                act.wait_ge(signal("ln_arg").sem, signal("ln_arg").next(act))
                act.activation(sp3, sp2, ACT.Ln).then_inc(signal("ln_done").sem, 1)
                act.wait_ge(signal("ln_done").sem, signal("ln_done").next(act))
                act.wait_ge(full[U["ba"][0].bank], U["ba"][0].n + 1)
                for h in range(RET_HEADS):
                    for i in (2 * h, 2 * h + 1):
                        if i >= 2:
                            act.wait_ge(full[U["l2"][i - 2].bank], U["l2"][i - 2].n + 1)
                        act.activation(l2_buf[i % 2], N_["QKVT"][:, i, :], ACT.Square).then_inc(signal("l2_square").sem, 1)
                        act.wait_ge(signal("l2_square").sem, signal("l2_square").next(act))
                    for j in range(2):
                        u = U["ret"][h]["qk"][j]
                        act.wait_ge(full[u.bank], u.n + 1)
                        act.activation(N_["QKT"][:, h % 2, j, :], ps(u)[:, :], ACT.Copy).then_inc(drained[u.bank], 1)
                        act.wait_ge(drained[u.bank], u.n + 1)
                    for i in (2 * h, 2 * h + 1):
                        u = U["l2"][i]
                        if i >= 2:
                            act.wait_ge(signal("l2_normed").sem, signal("l2_normed").next(act))
                        act.wait_ge(full[u.bank], u.n + 1)
                        act.activation(l2_buf[2 + i % 2], ps(u)[:, :], ACT.Sqrt, bias=k("eps")).then_inc(drained[u.bank], 1)
                        act.wait_ge(drained[u.bank], u.n + 1)
                for t in range(T):
                    if t in (1, 2):
                        round_chunk(W["mix_out"][t - 1])
                    g = U["gdn"][t]
                    act.wait_ge(signal("dec_raw").sem, signal("dec_raw").next(act))
                    act.activation(G["eg"], ps(g["gc"][0])[:, :].rearrange("p (h c) -> p h c", h=GDN_HEADS), ACT.Exp).then_inc(
                        drained[g["gc"][0].bank], 1)
                    act.wait_ge(drained[g["gc"][0].bank], g["gc"][0].n + 1)
                    act.activation(ge8, gcol8, ACT.Exp).then_inc(act_done.sem, 1)
                    act.wait_ge(act_done.sem, act_done.next(act))
                    act.activation(G["dec"], G["dec"], ACT.Exp).then_inc(signal("dec_exp").sem, 1)
                    act.wait_ge(signal("dec_exp").sem, signal("dec_exp").next(act))
                    act.wait_ge(full[g["vt"][0].bank], g["vt"][0].n + 1)
                    act.activation(G["v"], ps(g["vt"][0])[:, :].rearrange("p (h c) -> p h c", h=GDN_HEADS), ACT.Copy).then_inc(
                        drained[g["vt"][0].bank], 1)
                    act.wait_ge(drained[g["vt"][0].bank], g["vt"][0].n + 1)
                    for l in range(LEVELS):
                        for q, (u, _, _) in enumerate(g["inv"][l]):
                            act.wait_ge(full[u.bank], u.n + 1)
                            act.activation(G["T1"][:, pair(q), :], ps(u)[:, 0:2 * P].rearrange("p (h c) -> p h c", h=2), ACT.Copy).then_inc(
                                drained[u.bank], 1)
                            act.wait_ge(drained[u.bank], u.n + 1)
                    u = g["w"][0]
                    act.wait_ge(full[u.bank], u.n + 1)
                    act.activation(G["wT"], ps(u)[:, :].rearrange("p (h c) -> p h c", h=GDN_HEADS), ACT.Copy).then_inc(
                        drained[u.bank], 1)
                    act.wait_ge(drained[u.bank], u.n + 1)
                    u = g["o"][0]
                    act.wait_ge(full[u.bank], u.n + 1)
                    act.activation(XH[:, t, 512:1024], ps(u)[:, :], ACT.Copy).then_inc(drained[u.bank], 1)
                    act.wait_ge(drained[u.bank], u.n + 1)
                rounded_T("y_T")
            if on(8):
                round_chunk(W["ffn0_up"][0])
                squares(by_tile("mix_out"))
                rounded_T("rmsf0_T", gain="norm_ffn_2")
                ffn(0)
            if on(9):
                round_chunk(W["lru_in"][0])
                squares([U["ffn0_down"][2 * t:2 * t + 2] for t in range(T)])
                rounded_T("rms1_T", gain="norm_mix_2", gain_at=KD)
                act.wait_ge(signal("lam_arg").sem, signal("lam_arg").next(act))
                act.activation(sl1, sl1, ACT.Exp, scale=-1.0).then_inc(signal("lam_e").sem, 1)
                act.wait_ge(signal("lam_e").sem, signal("lam_e").next(act))
                act.wait_ge(signal("lam_w").sem, signal("lam_w").next(act))
                act.activation(sl3, sl2, ACT.Ln).then_inc(signal("lam_ln").sem, 1)
                act.wait_ge(signal("lam_ln").sem, signal("lam_ln").next(act))
                for i in range(2):
                    round_next("lru_in", i)
                    for m, u in enumerate(U["lru_in"][i]):
                        act.wait_ge(full[u.bank], u.n + 1)
                        act.activation(L_["gate"][:, 4 * i + m, :], ps(u)[:, :], ACT.Gelu_apprx_tanh).then_inc(drained[u.bank], 1)
                        act.wait_ge(drained[u.bank], u.n + 1)
                for i, v in enumerate((a["lru_w_a_2"], a["lru_w_x_2"])):
                    load(L_["w"][:, i, :, :], v[0].rearrange("n i j -> i n j"), "gates_loaded")
                round_chunk(W["lru_in"][3])
                round_chunk(W["lru_out"][0])
                for m in range(KD):
                    if m == 2:
                        round_chunk(W["lru_out"][1])
                    ur, ui = U["lru"][m]
                    act.wait_ge(full[ur.bank], ur.n + 1)
                    act.activation(XT[:, m, :], ps(ur)[:, :], ACT.Sigmoid, bias=col("lru_b_a_2", m)).then_inc(drained[ur.bank], 1)
                    act.wait_ge(drained[ur.bank], ur.n + 1)
                    act.wait_ge(full[ui.bank], ui.n + 1)
                    act.activation(L_["i"][:, m, :], ps(ui)[:, :], ACT.Sigmoid, bias=col("lru_b_x_2", m)).then_inc(
                        drained[ui.bank], 1)
                    act.wait_ge(drained[ui.bank], ui.n + 1)
                act.wait_ge(signal("cvec_ready").sem, signal("cvec_ready").next(act))
                for half in range(2):
                    ms = range(half * KD // 2, (half + 1) * KD // 2)
                    for m in ms:
                        act.wait_ge(signal("lru_x").sem, signal("lru_x").next(act))
                        r = XT[:, m, :]
                        act.activation(L_["xr"][:, m, :], r, ACT.Exp, scale=cvec[:, m:m + 1]).then_inc(signal("lru_a").sem, 1)
                        act.wait_ge(signal("lru_a").sem, signal("lru_a").next(act))
                        act.activation(r, r, ACT.Tanh, scale=cvec[:, m:m + 1]).then_inc(act_done.sem, 1)
                        act.wait_ge(act_done.sem, act_done.next(act))
                        if m >= ms[2]:
                            act.wait_ge(signal("lru_arg").sem, signal("lru_arg").next(act))
                        act.activation(L_["q"][:, m % 2, :], L_["xr"][:, m, :], ACT.Square).then_inc(signal("lru_square").sem, 1)
                    for m in ms:
                        if m >= ms[2]:
                            act.wait_ge(signal("lru_arg").sem, signal("lru_arg").next(act))
                        act.activation(XT[:, m, :], XT[:, m, :], ACT.Sqrt, scale=-1.0).then_inc(signal("lru_root").sem, 1)
                for m in range(KD):
                    act.wait_ge(signal("lru_gated").sem, signal("lru_gated").next(act))
                    act.activation(one_pass(XT[:, m, :]), L_["gate"][:, m, :], ACT.Copy).then_inc(signal("lru_rounded").sem, 1)
            if on(10):
                round_chunk(W["ffn1_up"][0])
                squares(by_tile("lru_out"))
                rounded_T("rmsf1_T", gain="norm_ffn_2", gain_at=KD)
                ffn(1)
            if on(11):
                squares([U["ffn1_down"][2 * t:2 * t + 2] for t in range(T)])

        @block.tensor
        def _(pe):
            def turn(name, src, told, per_tile=True):
                if told is not None:
                    pe.wait_ge(signal(told).sem, signal(told).next(pe, T))
                for i, u in enumerate(U[name]):
                    if u.n:
                        pe.wait_ge(drained[u.bank], u.n)
                    for t in range(T):
                        ins = pe.transpose(ps(u)[:, t * P:(t + 1) * P], src[:, t, i * P:(i + 1) * P], ident)
                    ins.then_inc(full[u.bank], 1)

            def ready(name):
                for u in U[name]:
                    pe.wait_ge(drained[u.bank], u.n + 1)

            def linear_raw(name, n, nk, width, src):
                for c, us in zip(W[name], U[name]):
                    pe.wait_ge(loaded[c.slot], 16 * c.loads)
                    w, m = raw(c), n // 2
                    for q, u in enumerate(us):
                        t, h = divmod(q, 2)
                        if u.n:
                            pe.wait_ge(drained[u.bank], u.n)
                        for kk in range(nk):
                            ins = pe.matmul(ps(u)[:, 0:m], src[:, kk, t * P:(t + 1) * P], w[:, kk, h * m:h * m + m],
                                            start=(kk == 0), stop=(kk == nk - 1))
                        ins.then_inc(full[u.bank], 1)

            def product(dst, x_hi, x_lo, y_hi, y_lo, first, last):
                x_hi, x_lo, y_hi, y_lo = one_pass(x_hi), one_pass(x_lo), one_pass(y_hi), one_pass(y_lo)
                pe.matmul(dst, x_hi, y_hi, start=first, stop=False)
                pe.matmul(dst, x_hi, y_lo, start=False, stop=False)
                return pe.matmul(dst, x_lo, y_hi, start=False, stop=last)

            def linear(name, lo=XH, turned=None):
                for i, (c, us) in enumerate(zip(W[name], U[name])):
                    linear_chunk(c, us, lo, turned if i == 0 else None)

            def linear_chunk(c, us, lo=XH, turned=None):
                for t, u in enumerate(us):
                    if u.n:
                        pe.wait_ge(drained[u.bank], u.n)
                    for kk in range(c.nk):
                        if t == 0 and turned:
                            pe.wait_ge(drained[U[turned][kk].bank], U[turned][kk].n + 1)
                        if t == 0 and kk == 0:
                            pe.wait_ge(split[c.pair], 2 * c.nth - 1)
                        if t == 0 and kk == c.nk // 2:
                            pe.wait_ge(split[c.pair], 2 * c.nth)
                        ins = product(ps(u)[:, 0:c.cols], XT[:, kk, t * P:(t + 1) * P], lo[:, t, kk * P:(kk + 1) * P], hi(c)[:, kk, :], raw(c)[:, kk, :],
                                      kk == 0, kk == c.nk - 1)
                    ins.then_inc(full[u.bank], 1)

            def linear_T(c, us, tiles, turned=None):
                for q, (u, m) in enumerate(zip(us, tiles)):
                    if u.n:
                        pe.wait_ge(drained[u.bank], u.n)
                    for kk in range(KD):
                        if q == 0 and turned:
                            pe.wait_ge(drained[U[turned][kk].bank], U[turned][kk].n + 1)
                        if q == 0 and kk == 0:
                            pe.wait_ge(split[c.pair], 2 * c.nth - 1)
                        if q == 0 and kk == KD // 2:
                            pe.wait_ge(split[c.pair], 2 * c.nth)
                        ins = product(ps(u)[:, :].rearrange("p (t c) -> p t c", t=T), hi(c)[:, kk, m * P:(m + 1) * P], raw(c)[:, kk, m * P:(m + 1) * P],
                                      XT[:, kk, :].rearrange("p (t c) -> p t c", t=T), XH[:, :, kk * P:(kk + 1) * P], kk == 0, kk == KD - 1)
                    ins.then_inc(full[u.bank], 1)

            def attention(name):
                c = att[name]
                u, buf, n, w = U[name], c["buf"], c["groups"] * T, c["width"]

                def group(g):
                    for j, src in enumerate((c["q"], c["k"])):
                        v = u["qk"][g][j]
                        if v.n:
                            pe.wait_ge(drained[v.bank], v.n)
                        for t in range(T):
                            ins = pe.transpose(ps(v)[0:w, t * P:(t + 1) * P], src(g, t), ident)
                        ins.then_inc(full[v.bank], 1)
                    if name == "C":
                        for (half, b), v in u["bias"][g]:
                            if v.n:
                                pe.wait_ge(drained[v.bank], v.n)
                            for jj in range(4):
                                j = 4 * b + jj
                                sel = one_pass(k("hankel")[:, GRID_W - 1 - j:GRID_W - 1 - j + P])
                                ins = pe.matmul(ps(v)[:, P * jj:P * jj + P], sel, one_pass(rel_sb[:, P * half:P * half + P]),
                                                start=True, stop=True)
                            ins.then_inc(full[v.bank], 1)

                group(0)
                for i in range(n + 3):
                    g, t = divmod(i, T)
                    if i < n:
                        if t == 0:
                            for v in u["qk"][g]:
                                pe.wait_ge(drained[v.bank], v.n + 1)
                        for m in range(c["maps"]):
                            v = u["s"][i][m]
                            if v.n:
                                pe.wait_ge(drained[v.bank], v.n)
                            r = slice(c["rows"] * m, c["rows"] * (m + 1))
                            ins = pe.matmul(ps(v)[:, :], buf["QKT"][r, g % 2, 0, t * P:(t + 1) * P], buf["QKT"][r, g % 2, 1, :],
                                            start=True, stop=True)
                            ins.then_inc(full[v.bank], 1)
                        if t == 2 and g + 1 < c["groups"]:
                            group(g + 1)
                    if 2 <= i < n + 2:
                        for o in range(c["outs"]):
                            v = u["t"][i - 2][o]
                            if name == "A":
                                pe.wait_ge(signal("mixed").sem, signal("mixed").next(pe))
                            elif name == "B":
                                pe.wait_ge(drained[u["s"][i - 2][o].bank], u["s"][i - 2][o].n + 1)
                            else:
                                pe.wait_ge(signal("exp_done").sem, signal("exp_done").next(pe))
                            if v.n:
                                pe.wait_ge(drained[v.bank], v.n)
                            for kt in range(T):
                                ins = pe.transpose(ps(v)[:, kt * P:(kt + 1) * P], buf["p"][(i - 2) % 3][:, o, kt * P:(kt + 1) * P], ident)
                            ins.then_inc(full[v.bank], 1)
                    if i >= 3:
                        for o in range(c["outs"]):
                            pe.wait_ge(drained[u["t"][i - 3][o].bank], u["t"][i - 3][o].n + 1)
                            v = u["o"][i - 3][o]
                            if v.n:
                                pe.wait_ge(drained[v.bank], v.n)
                            for kt in range(T):
                                ins = pe.matmul(ps(v)[:, 0:c["dv"]], buf["WT"][:, (i - 3) % 2, o, kt, :], c["v"]((i - 3) // T, o, kt),
                                                start=(kt == 0), stop=(kt == T - 1))
                            ins.then_inc(full[v.bank], 1)

            def experts(l):
                base = U[f"moe{l}"]
                us = U[f"route{l}"]
                for kk in range(KD):
                    pe.wait_ge(drained[U[f"ln1{l}_T"][kk].bank], U[f"ln1{l}_T"][kk].n + 1)
                    for t in range(T):
                        if kk == 0:
                            if us[t].n:
                                pe.wait_ge(drained[us[t].bank], us[t].n)
                        ins = pe.matmul(ps(us[t])[:, 0:ROUTES], XT[:, kk, t * P:(t + 1) * P], router[:, l, kk, :],
                                        start=(kk == 0), stop=(kk == KD - 1))
                        if kk == KD - 1:
                            ins.then_inc(full[us[t].bank], 1)
                u = us[T]
                if u.n:
                    pe.wait_ge(drained[u.bank], u.n)
                pe.wait_ge(signal("chosen").sem, signal("chosen").next(pe))
                n = (T + 1) * EXPERTS
                pe.matmul(ps(u)[:, 0:n], ones[:, :], R["Mc"].rearrange("p t e -> p (t e)"), start=True, stop=False)
                ins = pe.matmul(ps(u)[:, 0:T * EXPERTS], k("before"), R["M"].rearrange("p t e -> p (t e)"), start=False, stop=True)
                ins.then_inc(full[u.bank], 1)

                def wait_use(sems, b, e, more=0):
                    pe.wait_ge(sems[b], e + (base[b] + more))

                def rows_T(e, half, n):
                    pe.wait_ge(signal(f"rows_loaded{half}").sem, n * 16 + 16 * (1 + EXPERTS // 2 * l))
                    for b in range(2):
                        wait_use(drained, b, e)
                        for j in range(4):
                            kk = 4 * b + j
                            ins = pe.transpose(psum[b][:, j * CAP:(j + 1) * CAP], M["XE"][0:CAP, half, kk * P:(kk + 1) * P], ident[0:CAP, 0:CAP])
                        ins.then_inc(full[b], 1)

                def up(e, half, first=False):
                    for b in range(2):
                        wait_use(drained, b, e, 1)
                    for js, b in ((GATE, 2), (UP, 3)):
                        wait_use(drained, b, e)
                        for kk in range(KD):
                            j = js[kk // 4]
                            if kk % 4 == 0:
                                pe.wait_ge(signal("half_split").sem, nth_split(l, e, j, first=first))
                            ins = product(psum[b][0:CAP, :], M["XET"][:, half, kk, :], M["XET_lo"][:, half, kk, :],
                                          expert_hi(j)[:, kk % 4, :], expert_raw(j)[:, kk % 4, :], kk == 0, kk == KD - 1)
                        ins.then_inc(full[b], 1)

                def hidden_T(e, half):
                    wait_use(drained, 3, e, 1)
                    wait_use(drained, 4, e)
                    for kk in range(KE):
                        ins = pe.transpose(psum[4][:, kk * CAP:(kk + 1) * CAP], M["hid"][0:CAP, half, kk * P:(kk + 1) * P], ident[0:CAP, 0:CAP])
                    ins.then_inc(full[4], 1)

                def down(e, half, last=False):
                    wait_use(drained, 4, e, 1)
                    for j, b in zip(DOWN, (5, 6)):
                        wait_use(drained, b, e)
                        pe.wait_ge(signal("half_split").sem, nth_split(l, e, j, last=last))
                        for kk in range(KE):
                            ins = product(psum[b][0:CAP, :], M["HT"][:, half, kk, :], M["HT_lo"][:, half, kk, :],
                                          expert_hi(j)[:, kk, :], expert_raw(j)[:, kk, :], kk == 0, kk == KE - 1)
                        ins.then_inc(full[b], 1)

                def stage(e, half, n, first=False, last=False):
                    up(e, half, first)
                    if not last:
                        rows_T(e + 1, 1 - half, n + half)
                    if not first:
                        down(e - 1, 1 - half)
                    hidden_T(e, half)

                rows_T(0, 0, 0)
                stage(0, 0, 0, first=True)
                with pe.Fori(0, EXPERTS // 2 - 1) as i:
                    stage(i * 2 + 1, 1, i)
                    stage(i * 2 + 2, 0, i + 1)
                stage(EXPERTS - 1, 1, EXPERTS // 2 - 1, last=True)
                down(EXPERTS - 1, 1, last=True)
                with pe.If(overflow(pe) > 0):
                    for b in range(7):
                        pe.wait_ge(drained[b], base[b] + EXPERTS)

                    def late_tile(e, t, first=False):
                        if not first:
                            pe.wait_ge(late(l, "added"), e * T + t)
                        for j in range(2):
                            w = slot_kn(j)
                            for kk in range(KD):
                                ins = pe.matmul(psum[j][:, :], XT[:, kk, t * P:(t + 1) * P], w[:, kk, :], start=(kk == 0), stop=(kk == KD - 1))
                        ins.then_inc(late(l, "up"), 1)
                        pe.wait_ge(late(l, "hidden"), e * T + (t + 1))
                        for kk in range(KE):
                            ins = pe.transpose(psum[2][:, kk * P:(kk + 1) * P], M["lhid"][:, kk * P:(kk + 1) * P], ident)
                        ins.then_inc(late(l, "turned"), 1)
                        pe.wait_ge(late(l, "hidden_T"), e * T + (t + 1))
                        w = slot_kn(2, KE, D)
                        for j in range(2):
                            for kk in range(KE):
                                ins = pe.matmul(psum[3 + j][:, :], M["lHT"][:, kk, :], w[:, kk, j * BANK:(j + 1) * BANK],
                                                start=(kk == 0), stop=(kk == KE - 1))
                        ins.then_inc(late(l, "down"), 1)

                    pe.wait_ge(late(l, "loaded"), 16 * 3)
                    for t in range(T):
                        late_tile(0, t, first=(t == 0))
                    with pe.Fori(1, EXPERTS) as e:
                        pe.wait_ge(late(l, "loaded"), e * 48 + 48)
                        for t in range(T):
                            late_tile(e, t)
                    pe.wait_ge(late(l, "added"), EXPERTS * T)

            def ffn(l):
                for i, (c, us) in enumerate(zip(W[f"ffn{l}_up"], U[f"ffn{l}_up"])):
                    linear_T(c, us, (0, 2, 1, 3), f"rmsf{l}_T" if i == 0 else None)
                us = U[f"ffn{l}_down"]
                for i, c in enumerate(W[f"ffn{l}_down"]):
                    pe.wait_ge(signal("ff_act").sem, signal("ff_act").next(pe, c.nk))
                    pe.wait_ge(split[c.pair], 2 * c.nth)
                    for q, u in enumerate(us):
                        t, h = divmod(q, 2)
                        if i == 0:
                            if u.n:
                                pe.wait_ge(drained[u.bank], u.n)
                        for kk in range(c.nk):
                            f = 4 * i + kk
                            ins = product(ps(u)[:, :], act_hi(f)[:, t * P:(t + 1) * P], F_["act"][:, f, t * P:(t + 1) * P],
                                          hi(c)[:, kk, h * BANK:(h + 1) * BANK], raw(c)[:, kk, h * BANK:(h + 1) * BANK], f == 0, f == KF - 1)
                        if f == KF - 1:
                            ins.then_inc(full[u.bank], 1)
                    if f < KF - 1:
                        ins.then_inc(signal("down_used").sem, 1)

            pe.wait_ge(signal("table_loaded").sem, signal("table_loaded").next(pe, 16))
            pe.wait_ge(signal("x_loaded").sem, signal("x_loaded").next(pe, 16))
            turn("x_T", X, None)
            linear("even_in", x_lo, "x_T")
            pe.wait_ge(signal("chan_loaded").sem, signal("chan_loaded").next(pe, 16 * chan_dmas[0]))
            for i, u in enumerate(U["chan"]):
                if u.n:
                    pe.wait_ge(drained[u.bank], u.n)
                for q in range(4 * i, min(4 * i + 4, -(-n_chan // P))):
                    r = min(P, n_chan - q * P)
                    ins = pe.transpose(ps(u)[:, (q - 4 * i) * P:(q - 4 * i) * P + r], XH[0:r, 0, q * P:(q + 1) * P], ident[0:r, 0:r])
                ins.then_inc(full[u.bank], 1)
            u = U["rel"][0]
            if u.n:
                pe.wait_ge(drained[u.bank], u.n)
            for q in range(2):
                r = C_HEADS * REL_R // 2
                ins = pe.transpose(ps(u)[0:REL_C, q * r:(q + 1) * r], XH[0:r, 1, q * REL_C:(q + 1) * REL_C], ident[0:r, 0:r])
            ins.then_inc(full[u.bank], 1)
            pe.wait_ge(signal("lat_ready").sem, signal("lat_ready").next(pe, 2 * T))
            for j, u in enumerate(U["lat_T"]):
                if u.n:
                    pe.wait_ge(drained[u.bank], u.n)
                for t in range(T):
                    ins = pe.transpose(ps(u)[:, t * P:(t + 1) * P], E["H"][:, t, 3 * A_QKV + j * P:3 * A_QKV + (j + 1) * P], ident)
                ins.then_inc(full[u.bank], 1)
            ready("lat_T")
            linear_raw("uq", B_HEADS * B_QK, 2, B_HEADS * B_QK, E["latT"])
            linear_raw("ukv", B_HEADS * 128, 1, B_HEADS * 128, E["latT"][:, 2:3, :])
            if on(2):
                pe.wait_ge(signal("rope_a").sem, signal("rope_a").next(pe))
                pe.wait_ge(signal("rope_b").sem, signal("rope_b").next(pe, 2))
                attention("A")
                attention("B")
                pe.wait_ge(signal("a_normed").sem, signal("a_normed").next(pe))
                for v in U["B"]["o"][-2:]:
                    pe.wait_ge(drained[v[0].bank], v[0].n + 1)
                turn("o0_T", XH, None)
                linear("even_o", turned="o0_T")
            if on(3):
                turn("ln10_T", XH, "xh_ready")
            if on(4):
                experts(0)
                turn("ln20_T", XH, "xh_ready")
            if on(5):
                linear("qkv", x_lo, "ln20_T")
                for us in U["qkv"]:
                    for v in us:
                        pe.wait_ge(drained[v.bank], v.n + 1)
                pe.wait_ge(signal("hankel_rounded").sem, signal("hankel_rounded").next(pe))
                pe.wait_ge(signal("rel_split").sem, signal("rel_split").next(pe))
                attention("C")
                for v in U["C"]["o"][-2:]:
                    for w in v:
                        pe.wait_ge(drained[w.bank], w.n + 1)
                turn("o1_T", XH, None)
                linear("odd_o", turned="o1_T")
                turn("ln11_T", XH, "xh_ready")
            if on(6):
                experts(1)
            if on(7):
                turn("rms0_T", XH, "xh_ready")
                for i, (c, us) in enumerate(zip(W["mix_in"], U["mix_in"])):
                    if i in (4, 5, 6):
                        linear_T(c, us, range(4))
                    else:
                        linear_chunk(c, us, turned="rms0_T" if i == 0 else None)
                u = U["ba"][0]
                pe.wait_ge(signal("ba_split").sem, signal("ba_split").next(pe))
                if u.n:
                    pe.wait_ge(drained[u.bank], u.n)
                for t in range(T):
                    for kk in range(KD):
                        ins = product(ps(u)[:, t * 8:t * 8 + 8], XT[:, kk, t * P:(t + 1) * P], XH[:, t, kk * P:(kk + 1) * P],
                                      ba_hi[:, kk, :], ba_w[:, kk, :], kk == 0, kk == KD - 1)
                ins.then_inc(full[u.bank], 1)
                pe.wait_ge(signal("rotated").sem, signal("rotated").next(pe))
                for u in U["mix_in"][2]:
                    pe.wait_ge(drained[u.bank], u.n + 1)
                for h, r in enumerate(U["ret"]):
                    for i in (2 * h, 2 * h + 1):
                        u = U["l2"][i]
                        pe.wait_ge(signal("l2_square").sem, signal("l2_square").next(pe))
                        if u.n:
                            pe.wait_ge(drained[u.bank], u.n)
                        pe.matmul(ps(u)[:, :], ones[:, :], l2_buf[i % 2], start=True, stop=True).then_inc(full[u.bank], 1)
                    for j, u in enumerate(r["qk"]):
                        if u.n:
                            pe.wait_ge(drained[u.bank], u.n)
                        for t in range(T):
                            ins = pe.transpose(ps(u)[:, t * P:(t + 1) * P], N_["RQK"][:, t, 512 * j + 128 * h:512 * j + 128 * h + 128], ident)
                        ins.then_inc(full[u.bank], 1)
                    for u in r["qk"]:
                        pe.wait_ge(drained[u.bank], u.n + 1)
                    for kc, u in enumerate(r["s"]):
                        if u.n:
                            pe.wait_ge(drained[u.bank], u.n)
                        pe.matmul(ps(u)[:, 0:S - kc * P], N_["QKT"][:, h % 2, 1, kc * P:(kc + 1) * P], N_["QKT"][:, h % 2, 0, kc * P:S], start=True, stop=True).then_inc(
                            full[u.bank], 1)
                    u = r["o"][0]
                    for v in r["s"]:
                        pe.wait_ge(drained[v.bank], v.n + 1)
                    if u.n:
                        pe.wait_ge(drained[u.bank], u.n)
                    for t in range(T):
                        for kc in range(t + 1):
                            at = sc_at[kc] + (t - kc) * P
                            ins = pe.matmul(ps(u)[:, t * P:(t + 1) * P], N_["sc"][:, at:at + P], N_["VR"][:, kc, 128 * h:128 * h + 128],
                                            start=(kc == 0), stop=(kc == t))
                    ins.then_inc(full[u.bank], 1)

                def heads(u, lhsT, rhs, start=True, stop=True):
                    for h in range(GDN_HEADS):
                        ins = pe.matmul(ps(u)[:, h * P:(h + 1) * P], lhsT(h), rhs(h), start=start, stop=stop)
                    ins.then_inc(full[u.bank], 1)

                def pair_product(u, q, lhsT, rhs):
                    for i in range(2):
                        ins = pe.matmul(ps(u)[:, i * P:(i + 1) * P], lhsT[:, 2 * q + i, :], rhs[:, 2 * q + i, :], start=True, stop=True)
                    ins.then_inc(full[u.bank], 1)

                for t in range(T):
                    g = U["gdn"][t]
                    tok = slice(t * P, (t + 1) * P)
                    pe.wait_ge(signal("gm_ready").sem, signal("gm_ready").next(pe))
                    if g["gc"][0].n:
                        pe.wait_ge(drained[g["gc"][0].bank], g["gc"][0].n)
                    pe.matmul(ps(g["gc"][0])[:, :], ones[:, :], G["gm"].rearrange("p h c -> p (h c)"), start=True, stop=True).then_inc(
                        full[g["gc"][0].bank], 1)
                    if g["gc"][1].n:
                        pe.wait_ge(drained[g["gc"][1].bank], g["gc"][1].n)
                    pe.matmul(ps(g["gc"][1])[:, 0:GDN_HEADS], k("upto"), gg[:, t, :], start=True, stop=True).then_inc(
                        full[g["gc"][1].bank], 1)
                    QT = lambda h: N_["QKVT"][:, h, tok]
                    KT = lambda h: N_["QKVT"][:, 4 + h, tok]
                    VT = lambda h: N_["QKVT"][:, 8 + h, tok]
                    if g["kk"][0].n:
                        pe.wait_ge(drained[g["kk"][0].bank], g["kk"][0].n)
                    heads(g["kk"][0], KT, KT)
                    if g["kq"][0].n:
                        pe.wait_ge(drained[g["kq"][0].bank], g["kq"][0].n)
                    heads(g["kq"][0], KT, QT)
                    for name, src in (("kt", KT), ("vt", VT)):
                        u = g[name][0]
                        if u.n:
                            pe.wait_ge(drained[u.bank], u.n)
                        for h in range(GDN_HEADS):
                            ins = pe.transpose(ps(u)[:, h * P:(h + 1) * P], src(h), ident)
                        ins.then_inc(full[u.bank], 1)
                    for l in range(LEVELS):
                        pe.wait_ge(signal("level_ready").sem, signal("level_ready").next(pe))
                        for q, (u1, _, _) in enumerate(g["inv"][l]):
                            if l:
                                pe.wait_ge(drained[g["inv"][l - 1][q][1].bank], g["inv"][l - 1][q][1].n + 1)
                                pe.wait_ge(drained[g["inv"][l - 1][q][2].bank], g["inv"][l - 1][q][2].n + 1)
                            if u1.n:
                                pe.wait_ge(drained[u1.bank], u1.n)
                            pair_product(u1, q, CT[l % 2], G["Inv"])
                        for q, (u1, u2, u3) in enumerate(g["inv"][l]):
                            pe.wait_ge(drained[u1.bank], u1.n + 1)
                            if u2:
                                if u2.n:
                                    pe.wait_ge(drained[u2.bank], u2.n)
                                pair_product(u2, q, G["InvT"], G["T1"])
                            if u3.n:
                                pe.wait_ge(drained[u3.bank], u3.n)
                            pair_product(u3, q, G["T1"], G["InvT"])
                    u = g["u"][0]
                    for q in range(2):
                        pe.wait_ge(drained[g["inv"][-1][q][2].bank], g["inv"][-1][q][2].n + 1)
                    pe.wait_ge(drained[g["vt"][0].bank], g["vt"][0].n + 1)
                    if u.n:
                        pe.wait_ge(drained[u.bank], u.n)
                    heads(u, lambda h: G["InvT"][:, h, :], lambda h: G["v"][:, h, :])
                    u = g["w"][0]
                    if u.n:
                        pe.wait_ge(drained[u.bank], u.n)
                    heads(u, lambda h: G["kg"][:, h, :], lambda h: G["InvT"][:, h, :])
                    pe.wait_ge(drained[u.bank], u.n + 1)
                    u = g["ws"][0]
                    if t == 0:
                        pe.wait_ge(signal("state_ready").sem, signal("state_ready").next(pe))
                    else:
                        pe.wait_ge(drained[U["gdn"][t - 1]["s"][0].bank], U["gdn"][t - 1]["s"][0].n + 1)
                    if u.n:
                        pe.wait_ge(drained[u.bank], u.n)
                    heads(u, lambda h: G["wT"][:, h, :], lambda h: G["S"][:, h, :])
                    u = g["o"][0]
                    pe.wait_ge(signal("v_new").sem, signal("v_new").next(pe))
                    if u.n:
                        pe.wait_ge(drained[u.bank], u.n)
                    for h in range(GDN_HEADS):
                        pe.matmul(ps(u)[:, h * P:(h + 1) * P], G["qd"][:, h, :], G["S"][:, h, :], start=True, stop=False)
                        ins = pe.matmul(ps(u)[:, h * P:(h + 1) * P], G["attnT"][:, h, :], G["vn"][:, h, :], start=False, stop=True)
                    ins.then_inc(full[u.bank], 1)
                    u = g["s"][0]
                    if u.n:
                        pe.wait_ge(drained[u.bank], u.n)
                    heads(u, lambda h: G["ktail"][:, h, :], lambda h: G["vn"][:, h, :])
                turn("y_T", XH, "y_ready")
                linear("mix_out", turned="y_T")
            if on(8):
                turn("rmsf0_T", XH, "xh_ready")
                ffn(0)
            if on(9):
                turn("rms1_T", XH, "xh_ready")
                for i, (c, us) in enumerate(zip(W["lru_in"], U["lru_in"])):
                    linear_T(c, us, range(4), "rms1_T" if i == 0 else None)
                pe.wait_ge(signal("gates_loaded").sem, signal("gates_loaded").next(pe, 32))
                for m in range(KD):
                    pe.wait_ge(drained[U["lru_in"][2 + m // 4][m % 4].bank], U["lru_in"][2 + m // 4][m % 4].n + 1)
                    for j, u in enumerate(U["lru"][m]):
                        if u.n:
                            pe.wait_ge(drained[u.bank], u.n)
                        pe.matmul(ps(u)[:, :], L_["w"][:, j, m, :], L_["xr"][:, m, :], start=True, stop=True).then_inc(
                            full[u.bank], 1)
                pe.wait_ge(signal("lru_y").sem, signal("lru_y").next(pe, KD))
                linear("lru_out")
            if on(10):
                turn("rmsf1_T", XH, "xh_ready")
                ffn(1)

        @block.vector
        def _(dve):
            def rope(x1, x2, cos, sin, tmp, told):
                dve.tensor_tensor(tmp[0], x1, cos, ALU.mult).then_inc(dve_done.sem, 1)
                dve.wait_ge(dve_done.sem, dve_done.next(dve))
                dve.tensor_tensor(tmp[1], x2, sin, ALU.mult).then_inc(dve_done.sem, 1)
                dve.wait_ge(dve_done.sem, dve_done.next(dve))
                dve.tensor_tensor(tmp[2], x2, cos, ALU.mult).then_inc(dve_done.sem, 1)
                dve.wait_ge(dve_done.sem, dve_done.next(dve))
                dve.tensor_tensor(tmp[3], x1, sin, ALU.mult).then_inc(dve_done.sem, 1)
                dve.wait_ge(dve_done.sem, dve_done.next(dve))
                dve.tensor_tensor(x1, tmp[0], tmp[1], ALU.subtract).then_inc(dve_done.sem, 1)
                dve.wait_ge(dve_done.sem, dve_done.next(dve))
                ins = dve.tensor_tensor(x2, tmp[2], tmp[3], ALU.add)
                if told:
                    ins.then_inc(signal(told).sem, 1)
                    dve.wait_ge(signal(told).sem, signal(told).next(dve))
                else:
                    ins.then_inc(dve_done.sem, 1)
                    dve.wait_ge(dve_done.sem, dve_done.next(dve))

            def rest_of_chunk(c):
                for i, ks in enumerate(pieces(c)):
                    w = raw(c)[:, ks, :]
                    dve.wait_ge(rounded[c.pair], 2 * c.nth - 1 + i)
                    dve.tensor_tensor(one_pass(w), w, parts(hi(c)[:, ks, :]), ALU.subtract).then_inc(split[c.pair], 1)

            def rest_of_T(name, gain=None, bias=None, gain_at=0, dst=XH):
                for i, u in enumerate(U[name]):
                    dve.wait_ge(signal("xt_rounded").sem, signal("xt_rounded").next(dve))
                    lo = dst[:, :, i * P:(i + 1) * P]
                    x = ps(u)[:, :].rearrange("p (t c) -> p t c", t=T)
                    h = parts(XT[:, i, :].rearrange("p (t c) -> p t c", t=T))
                    if gain is None:
                        dve.tensor_tensor(one_pass(lo), x, h, ALU.subtract).then_inc(drained[u.bank], 1)
                    elif bias is None:
                        dve.scalar_tensor_tensor(one_pass(lo), x, col(gain, gain_at + i), h, ALU.mult, ALU.subtract).then_inc(
                            drained[u.bank], 1)
                    else:
                        dve.tensor_scalar(lo, x, col(gain, gain_at + i), col(bias, gain_at + i), ALU.mult, ALU.add).then_inc(
                            dve_done.sem, 1)
                        dve.wait_ge(dve_done.sem, dve_done.next(dve))
                        dve.tensor_tensor(one_pass(lo), lo, h, ALU.subtract).then_inc(drained[u.bank], 1)

            def cut(hi, x):
                dve.tensor_copy(one_pass(hi), x).then_inc(dve_done.sem, 1)
                dve.wait_ge(dve_done.sem, dve_done.next(dve))

            def half_stats(t, h):
                dve.bn_stats(bnst[:, t, h, :], X[:, t, h * BANK:(h + 1) * BANK]).then_inc(dve_done.sem, 1)
                dve.wait_ge(dve_done.sem, dve_done.next(dve))

            def mean_var(t):
                ins = dve.bn_aggr(mv[:, t, :], bnst[:, t, :, :].rearrange("p a b -> p (a b)"))
                if t == T - 1:
                    ins.then_inc(signal("ln_stats").sem, 1)
                    dve.wait_ge(signal("ln_stats").sem, signal("ln_stats").next(dve))
                else:
                    ins.then_inc(dve_done.sem, 1)
                    dve.wait_ge(dve_done.sem, dve_done.next(dve))

            def residual(name, scale, after=None, norm=False):
                for i, us in enumerate(U[name]):
                    if i == 1 and after:
                        rest_of_chunk(W[after][0])
                    for q, u in enumerate(us):
                        t, c = q, i
                        dve.wait_ge(full[u.bank], u.n + 1)
                        x = X[:, t, c * BANK:(c + 1) * BANK]
                        dve.scalar_tensor_tensor(x, x, scale, ps(u)[:, :], ALU.mult, ALU.add).then_inc(drained[u.bank], 1)
                        dve.wait_ge(drained[u.bank], u.n + 1)
                        if norm:
                            half_stats(t, c)
                            if c == 1:
                                mean_var(t)

            def ffn_residual(l):
                for q, u in enumerate(U[f"ffn{l}_down"]):
                    t, c = divmod(q, 2)
                    dve.wait_ge(full[u.bank], u.n + 1)
                    x = X[:, t, c * BANK:(c + 1) * BANK]
                    dve.tensor_tensor(x, x, ps(u)[:, :], ALU.add).then_inc(drained[u.bank], 1)
                    dve.wait_ge(drained[u.bank], u.n + 1)

            def layer_norm(stats=True):
                if stats:
                    for t in range(T):
                        for h in range(2):
                            half_stats(t, h)
                        mean_var(t)
                dve.wait_ge(signal("rstd_ready").sem, signal("rstd_ready").next(dve))
                for t in range(T):
                    dve.tensor_scalar(XH[:, t, :], X[:, t, :], mv[:, t, 0:1], rstd[:, t:t + 1], ALU.subtract, ALU.mult).then_inc(
                        signal("xh_ready").sem, 1)
                    dve.wait_ge(signal("xh_ready").sem, signal("xh_ready").next(dve))

            def layer_norm_in_place():
                for t in range(T):
                    for h in range(2):
                        half_stats(t, h)
                    mean_var(t)
                dve.wait_ge(signal("rstd_ready").sem, signal("rstd_ready").next(dve))
                dve.wait_ge(signal("ln_loaded").sem, signal("ln_loaded").next(dve, 16 * 8))
                for t in range(T):
                    x = X[:, t, :]
                    dve.scalar_tensor_tensor(x, x, mv[:, t, 0:1], lnp[:, 0, :], ALU.subtract, ALU.mult).then_inc(dve_done.sem, 1)
                    dve.wait_ge(dve_done.sem, dve_done.next(dve))
                    dve.scalar_tensor_tensor(x, x, rstd[:, t:t + 1], lnp[:, 1, :], ALU.mult, ALU.add).then_inc(
                        signal("x_applied").sem, 1)
                    dve.wait_ge(signal("x_applied").sem, signal("x_applied").next(dve))

            def rms():
                for t in range(T):
                    dve.wait_ge(signal("rstd_ready").sem, signal("rstd_ready").next(dve))
                    dve.tensor_scalar(XH[:, t, :], X[:, t, :], rstd[:, t:t + 1], None, ALU.mult).then_inc(signal("xh_ready").sem, 1)
                    dve.wait_ge(signal("xh_ready").sem, signal("xh_ready").next(dve))

            def attention(name, then=None):
                c = att[name]
                u, buf, n = U[name], c["buf"], c["groups"] * T

                def bias(g):
                    for (half, b), v in u["bias"][g]:
                        dve.wait_ge(full[v.bank], v.n + 1)
                        dst = buf["bias"][half][:, :, :, :, 4 * b:4 * b + 4].rearrange("p b h s j -> p (b h s) j")
                        src = ps(v)[:, :].rearrange("p (j q) -> p q j", j=4)
                        dve.tensor_tensor(dst, src, rep(k("window")[:, 4 * b:4 * b + 4], 1, P), ALU.add).then_inc(
                            drained[v.bank], 1)
                        dve.wait_ge(drained[v.bank], v.n + 1)

                if name == "C":
                    bias(0)
                for i in range(n + 3):
                    g, t = divmod(i, T)
                    if then and i == (n // 2 + 6 if name == "C" else 6):
                        rest_of_chunk(W[then][0])
                    if i < n:
                        for m in range(c["maps"]):
                            s = (i * c["maps"] + m) % 64
                            v = u["s"][i][m]
                            dve.wait_ge(full[v.bank], v.n + 1)
                            if name == "C":
                                if i >= 3:
                                    dve.wait_ge(full[u["t"][i - 3][m].bank], u["t"][i - 3][m].n + 1)
                                p = buf["p"][i % 3][:, m, :]
                                b = buf["bias"][2 * g // c["groups"]][:, g % (c["groups"] // 2), m, 7 - 2 * t:15 - 2 * t, :].rearrange("p s j -> p (s j)")
                                dve.scalar_tensor_tensor(p, ps(v)[:, :], c["scale"], b, ALU.mult, ALU.add).then_inc(
                                    drained[v.bank], 1)
                                dve.wait_ge(drained[v.bank], v.n + 1)
                                dve.tensor_reduce(negmax[:, s:s + 1], p, AX_X, ALU.max).then_inc(dve_done.sem, 1)
                                dve.wait_ge(dve_done.sem, dve_done.next(dve))
                            else:
                                dve.tensor_reduce(negmax[:, s:s + 1], ps(v)[:, :], AX_X, ALU.max).then_inc(dve_done.sem, 1)
                                dve.wait_ge(dve_done.sem, dve_done.next(dve))
                            dve.tensor_scalar(negmax[:, s:s + 1], negmax[:, s:s + 1], -1.0 if name == "C" else -c["scale"], None, ALU.mult).then_inc(
                                signal("max_ready").sem, 1)
                            dve.wait_ge(signal("max_ready").sem, signal("max_ready").next(dve))
                        if name == "C" and t == 2 and g + 1 < c["groups"]:
                            bias(g + 1)
                    if 1 <= i <= n:
                        s = ((i - 1) * c["maps"]) % 64
                        for m in range(c["maps"]):
                            if name == "C":
                                dve.wait_ge(signal("exp_done").sem, signal("exp_done").next(dve))
                            else:
                                dve.wait_ge(drained[u["s"][i - 1][m].bank], u["s"][i - 1][m].n + 1)
                        dve.reciprocal(rcp[:, s:s + c["maps"]], sums[:, s:s + c["maps"]]).then_inc(dve_done.sem, 1)
                        dve.wait_ge(dve_done.sem, dve_done.next(dve))
                        if name == "A":
                            p0, p1 = (buf["p"][(i - 1) % 3][:, m, :] for m in range(2))
                            dve.tensor_scalar(p1, p1, rcp[:, s + 1:s + 2], lam[:, 2:3], ALU.mult, ALU.mult).then_inc(
                                dve_done.sem, 1)
                            dve.wait_ge(dve_done.sem, dve_done.next(dve))
                            dve.scalar_tensor_tensor(p0, p0, rcp[:, s:s + 1], p1, ALU.mult, ALU.add).then_inc(
                                signal("mixed").sem, 1)
                            dve.wait_ge(signal("mixed").sem, signal("mixed").next(dve))
                    if i >= 3:
                        g2, t2 = divmod(i - 3, T)
                        for o in range(c["outs"]):
                            v = u["o"][i - 3][o]
                            s = ((i - 3) * c["maps"] + o) % 64
                            dve.wait_ge(full[v.bank], v.n + 1)
                            if name == "A":
                                dve.tensor_copy(c["o"](g2, o, t2), ps(v)[:, 0:c["dv"]]).then_inc(drained[v.bank], 1)
                                dve.wait_ge(drained[v.bank], v.n + 1)
                            else:
                                dve.tensor_scalar(c["o"](g2, o, t2), ps(v)[:, 0:c["dv"]], rcp[:, s:s + 1], None, ALU.mult).then_inc(
                                    drained[v.bank], 1)
                                dve.wait_ge(drained[v.bank], v.n + 1)

            def route(l):
                bg, be = bcv("b_router_group")[:, 4 * l:4 * l + 4], bcv("b_router_expert")[:, 32 * l:32 * l + 32]
                for t in range(T):
                    u = U[f"route{l}"][t]
                    dve.wait_ge(full[u.bank], u.n + 1)
                    dve.tensor_tensor(R["L"][:, t, 0:GROUPS], ps(u)[:, 0:GROUPS], bg, ALU.add).then_inc(dve_done.sem, 1)
                    dve.wait_ge(dve_done.sem, dve_done.next(dve))
                    dve.tensor_tensor(R["L"][:, t, GROUPS:], ps(u)[:, GROUPS:ROUTES], be, ALU.add).then_inc(drained[u.bank], 1)
                    dve.wait_ge(drained[u.bank], u.n + 1)
                dve.memset(R["LP"], -3e38).then_inc(dve_done.sem, 1)
                dve.wait_ge(dve_done.sem, dve_done.next(dve))
                dve.tensor_copy(R["LP"][:, :, 0:GROUPS], R["L"][:, :, 0:GROUPS]).then_inc(dve_done.sem, 1)
                dve.wait_ge(dve_done.sem, dve_done.next(dve))
                for t in range(T):
                    dve.max(R["g8"][:, t, :], R["LP"][:, t, :]).then_inc(dve_done.sem, 1)
                    dve.wait_ge(dve_done.sem, dve_done.next(dve))
                    dve.max_index(gidx[:, t, :], R["g8"][:, t, :], R["LP"][:, t, :]).then_inc(dve_done.sem, 1)
                    dve.wait_ge(dve_done.sem, dve_done.next(dve))
                dve.tensor_tensor(gdiff, R["L"][:, :, 0:GROUPS], rep(R["g8"][:, :, 0], 2, GROUPS), ALU.subtract).then_inc(
                    signal("gdiff").sem, 1)
                dve.wait_ge(signal("gdiff").sem, signal("gdiff").next(dve))
                dve.tensor_copy(grp, gidx[:, :, 0]).then_inc(dve_done.sem, 1)
                dve.wait_ge(dve_done.sem, dve_done.next(dve))
                dve.tensor_tensor(ohg, rep(k("iota")[:, 0:GROUPS], 1, T), rep(grp, 2, GROUPS), ALU.is_equal).then_inc(
                    dve_done.sem, 1)
                dve.wait_ge(dve_done.sem, dve_done.next(dve))
                dve.tensor_tensor(R["sel"], R["L"][:, :, GROUPS:].rearrange("p t (g j) -> p t j g", g=GROUPS), rep(ohg, 2, PER_GROUP), ALU.mult).then_inc(
                    dve_done.sem, 1)
                dve.wait_ge(dve_done.sem, dve_done.next(dve))
                dve.tensor_reduce(R["e8"], R["sel"], AX_X, ALU.add).then_inc(dve_done.sem, 1)
                dve.wait_ge(dve_done.sem, dve_done.next(dve))
                for t in range(T):
                    dve.max(R["v8"][:, t, :], R["e8"][:, t, :]).then_inc(dve_done.sem, 1)
                    dve.wait_ge(dve_done.sem, dve_done.next(dve))
                    dve.max_index(eidx[:, t, :], R["v8"][:, t, :], R["e8"][:, t, :]).then_inc(dve_done.sem, 1)
                    dve.wait_ge(dve_done.sem, dve_done.next(dve))
                dve.tensor_tensor(ediff, R["v8"][:, :, 1], R["v8"][:, :, 0], ALU.subtract).then_inc(signal("ediff").sem, 1)
                dve.wait_ge(signal("ediff").sem, signal("ediff").next(dve))
                dve.tensor_copy(pos2, eidx[:, :, 0:TOP_K]).then_inc(dve_done.sem, 1)
                dve.wait_ge(dve_done.sem, dve_done.next(dve))
                dve.scalar_tensor_tensor(ek, rep(grp, 2, TOP_K), float(PER_GROUP), pos2, ALU.mult, ALU.add).then_inc(
                    dve_done.sem, 1)
                dve.wait_ge(dve_done.sem, dve_done.next(dve))
                dve.tensor_tensor(R["A"], rep(rep(k("iota"), 1, TOP_K), 1, T), rep(ek, 3, EXPERTS), ALU.is_equal).then_inc(
                    dve_done.sem, 1)
                dve.wait_ge(dve_done.sem, dve_done.next(dve))
                dve.tensor_tensor(R["M"], R["A"][:, :, 0, :], R["A"][:, :, 1, :], ALU.add).then_inc(dve_done.sem, 1)
                dve.wait_ge(dve_done.sem, dve_done.next(dve))
                dve.memset(R["Mc"][:, 0, :], 0.0).then_inc(dve_done.sem, 1)
                dve.wait_ge(dve_done.sem, dve_done.next(dve))
                for t in range(T):
                    ins = dve.tensor_tensor(R["Mc"][:, t + 1, :], R["Mc"][:, t, :], R["M"][:, t, :], ALU.add)
                    if t == T - 1:
                        ins.then_inc(signal("chosen").sem, 1)
                        dve.wait_ge(signal("chosen").sem, signal("chosen").next(dve))
                    else:
                        ins.then_inc(dve_done.sem, 1)
                        dve.wait_ge(dve_done.sem, dve_done.next(dve))
                dve.wait_ge(signal("gexp").sem, signal("gexp").next(dve))
                dve.tensor_reduce(gsum, gdiff, AX_X, ALU.add).then_inc(dve_done.sem, 1)
                dve.wait_ge(dve_done.sem, dve_done.next(dve))
                dve.reciprocal(gw, gsum).then_inc(dve_done.sem, 1)
                dve.wait_ge(dve_done.sem, dve_done.next(dve))
                dve.wait_ge(signal("eexp").sem, signal("eexp").next(dve))
                dve.tensor_scalar(gsum, ediff, 1.0, None, ALU.add).then_inc(dve_done.sem, 1)
                dve.wait_ge(dve_done.sem, dve_done.next(dve))
                dve.reciprocal(gsum, gsum).then_inc(dve_done.sem, 1)
                dve.wait_ge(dve_done.sem, dve_done.next(dve))
                dve.tensor_tensor(wts[:, :, 0], gw, gsum, ALU.mult).then_inc(dve_done.sem, 1)
                dve.wait_ge(dve_done.sem, dve_done.next(dve))
                dve.tensor_tensor(wts[:, :, 1], wts[:, :, 0], ediff, ALU.mult).then_inc(dve_done.sem, 1)
                dve.wait_ge(dve_done.sem, dve_done.next(dve))
                u = U[f"route{l}"][T]
                dve.wait_ge(full[u.bank], u.n + 1)
                pos = ps(u)[:, 0:T * EXPERTS].rearrange("p (t e) -> p t e", t=T)
                dve.tensor_reduce(gsum[:, 0:1], ps(u)[:, T * EXPERTS:(T + 1) * EXPERTS], AX_X, ALU.max).then_inc(dve_done.sem, 1)
                dve.wait_ge(dve_done.sem, dve_done.next(dve))
                dve.tensor_scalar(gsum[:, 0:1], gsum[:, 0:1], -float(CAP), 0.0, ALU.add, ALU.max).then_inc(dve_done.sem, 1)
                dve.wait_ge(dve_done.sem, dve_done.next(dve))
                dve.tensor_copy(n_over[0:1, 0:1], gsum[0:1, 0:1]).then_inc(dve_done.sem, 1)
                dve.wait_ge(dve_done.sem, dve_done.next(dve))
                dve.tensor_tensor(R["tmp"], R["A"], rep(pos, 2, TOP_K), ALU.mult).then_inc(drained[u.bank], 1)
                dve.wait_ge(drained[u.bank], u.n + 1)
                dve.tensor_reduce(pos2, R["tmp"], AX_X, ALU.add).then_inc(dve_done.sem, 1)
                dve.wait_ge(dve_done.sem, dve_done.next(dve))
                dve.tensor_scalar(over, pos2, float(CAP), None, ALU.is_ge).then_inc(dve_done.sem, 1)
                dve.wait_ge(dve_done.sem, dve_done.next(dve))
                dve.tensor_scalar(keep, over, -1.0, 1.0, ALU.mult, ALU.add).then_inc(dve_done.sem, 1)
                dve.wait_ge(dve_done.sem, dve_done.next(dve))
                dve.scalar_tensor_tensor(slotf, ek, float(CAP), pos2, ALU.mult, ALU.add).then_inc(dve_done.sem, 1)
                dve.wait_ge(dve_done.sem, dve_done.next(dve))
                dve.scalar_tensor_tensor(wtmp, over, 1e6, slotf, ALU.mult, ALU.add).then_inc(dve_done.sem, 1)
                dve.wait_ge(dve_done.sem, dve_done.next(dve))
                dve.tensor_copy(scat.rearrange("p (t j) -> p t j", t=T), wtmp).then_inc(dve_done.sem, 1)
                dve.wait_ge(dve_done.sem, dve_done.next(dve))
                dve.tensor_tensor(wtmp, slotf, keep, ALU.mult).then_inc(dve_done.sem, 1)
                dve.wait_ge(dve_done.sem, dve_done.next(dve))
                dve.tensor_tensor(slotf, wts, over, ALU.mult).then_inc(
                    dve_done.sem, 1)
                dve.wait_ge(dve_done.sem, dve_done.next(dve))
                dve.tensor_tensor(wts, wts, keep, ALU.mult).then_inc(dve_done.sem, 1)
                dve.wait_ge(dve_done.sem, dve_done.next(dve))
                dve.tensor_copy(gath.rearrange("p (t j) -> p t j", t=T), wtmp).then_inc(signal("slots_ready").sem, 1)
                dve.wait_ge(signal("slots_ready").sem, signal("slots_ready").next(dve))

            def experts(l):
                base = U[f"moe{l}"]

                def wait_use(sems, b, e):
                    dve.wait_ge(sems[b], e + (base[b] + 1))

                def hidden(e, half):
                    wait_use(full, 3, e)
                    wait_use(drained, 2, e)
                    h = M["hid"][0:CAP, half, :]
                    dve.tensor_tensor(h, h, psum[3][0:CAP, :], ALU.mult).then_inc(drained[3], 1)

                def rest_of_half(e, j, first=False, last=False):
                    dve.wait_ge(signal("half_rounded").sem, nth_split(l, e, j, first, last))
                    dve.tensor_tensor(one_pass(expert_raw(j)), expert_raw(j), parts(expert_hi(j)), ALU.subtract).then_inc(signal("half_split").sem, 1)

                def rows_T(e, half):
                    for b in range(2):
                        dve.wait_ge(signal("rows_rounded").sem, e * 2 + (2 * EXPERTS * l + b + 1))
                        dve.tensor_tensor(one_pass(M["XET_lo"][:, half, 4 * b:4 * b + 4, :].rearrange("p k c -> p (k c)")), psum[b][:, 0:4 * CAP], parts(M["XET"][:, half, 4 * b:4 * b + 4, :].rearrange("p k c -> p (k c)")), ALU.subtract).then_inc(drained[b], 1)

                def hidden_T(e, half):
                    dve.wait_ge(signal("hidden_rounded").sem, e + (EXPERTS * l + 1))
                    dve.tensor_tensor(one_pass(M["HT_lo"][:, half, :, :].rearrange("p k c -> p (k c)")), psum[4][:, 0:KE * CAP], parts(M["HT"][:, half, :, :].rearrange("p k c -> p (k c)")), ALU.subtract).then_inc(drained[4], 1)

                def stage(e, half, first=False, last=False):
                    if not first:
                        for j in DOWN:
                            rest_of_half(e - 1, j)
                    if not last:
                        rest_of_half(e + 1, GATE[0])
                    hidden(e, half)
                    if not last:
                        rows_T(e + 1, 1 - half)
                        rest_of_half(e + 1, GATE[1])
                        rest_of_half(e + 1, UP[0])
                    hidden_T(e, half)
                    if not last:
                        rest_of_half(e + 1, UP[1])

                for j in GATE + UP:
                    rest_of_half(0, j, first=True)
                dve.wait_ge(signal("rows_sent").sem, signal("rows_sent").next(dve, 16 * T * TOP_K))
                for t in range(T):
                    dve.tensor_scalar(X[:, t, :], X[:, t, :], ALPHA, None, ALU.mult).then_inc(dve_done.sem, 1)
                    dve.wait_ge(dve_done.sem, dve_done.next(dve))
                rows_T(0, 0)
                stage(0, 0, first=True)
                with dve.Fori(0, EXPERTS // 2 - 1) as i:
                    stage(i * 2 + 1, 1)
                    stage(i * 2 + 2, 0)
                stage(EXPERTS - 1, 1, last=True)
                for j in DOWN:
                    rest_of_half(EXPERTS - 1, j, last=True)
                for t in range(T):
                    dve.wait_ge(signal(f"rows_back{t}").sem, signal(f"rows_back{t}").next(dve, 16 * TOP_K))
                    for j, y in enumerate((XH[:, t, :], M["YG"][:, t, :])):
                        dve.scalar_tensor_tensor(X[:, t, :], y, wts[:, t, j:j + 1], X[:, t, :], ALU.mult, ALU.add).then_inc(
                            dve_done.sem, 1)
                        dve.wait_ge(dve_done.sem, dve_done.next(dve))
                with dve.If(overflow(dve, waits=False) > 0):
                    late_n = Signal(late(l, "steps"))

                    dve.tensor_tensor(R["tmp"], R["A"], rep(slotf, 3, EXPERTS), ALU.mult).then_inc(late_n.sem, 1)
                    dve.wait_ge(late_n.sem, late_n.next(dve))
                    dve.tensor_tensor(R["M"], R["tmp"][:, :, 0, :], R["tmp"][:, :, 1, :], ALU.add).then_inc(late_n.sem, 1)
                    dve.wait_ge(late_n.sem, late_n.next(dve))
                    with dve.Fori(0, EXPERTS) as e:
                        for t in range(T):
                            n = e * T + (t + 1)
                            dve.wait_ge(late(l, "silu"), n)
                            dve.tensor_tensor(M["lhid"], M["lhid"], psum[1][:, :], ALU.mult).then_inc(late(l, "hidden"), 1)
                            dve.wait_ge(late(l, "turned"), n)
                            dve.tensor_copy(M["lHT"].rearrange("p k c -> p (k c)"), psum[2][:, :]).then_inc(late(l, "hidden_T"), 1)
                            dve.wait_ge(late(l, "down"), n)
                            for j in range(2):
                                x = X[:, t, j * BANK:(j + 1) * BANK]
                                dve.scalar_tensor_tensor(x, psum[3 + j][:, :], R["M"][:, t, bass.ds(e, 1)], x, ALU.mult, ALU.add).then_inc(
                                    late(l, "added" if j else "half"), 1)
                    dve.wait_ge(late(l, "added"), EXPERTS * T)
                    dve.wait_ge(late(l, "half"), EXPERTS * T)

            def conv(dst, u, taps, bias=None, told=None):
                dve.wait_ge(full[u.bank], u.n + 1)
                n = len(taps)
                if bias is None:
                    dve.tensor_scalar(dst, ps(u)[:, :], taps[-1], None, ALU.mult).then_inc(dve_done.sem, 1)
                    dve.wait_ge(dve_done.sem, dve_done.next(dve))
                else:
                    dve.tensor_scalar(dst, ps(u)[:, :], taps[-1], bias, ALU.mult, ALU.add).then_inc(dve_done.sem, 1)
                    dve.wait_ge(dve_done.sem, dve_done.next(dve))
                for d in range(1, n):
                    ins = dve.scalar_tensor_tensor(dst[:, d:S], ps(u)[:, 0:S - d], taps[n - 1 - d], dst[:, d:S], ALU.mult, ALU.add)
                    if d < n - 1:
                        ins.then_inc(dve_done.sem, 1)
                        dve.wait_ge(dve_done.sem, dve_done.next(dve))
                ins.then_inc(drained[u.bank], 1)
                dve.wait_ge(drained[u.bank], u.n + 1)

            def log1p_arg(dst, e):
                dve.tensor_scalar(dst, e, 1.0, None, ALU.add).then_inc(dve_done.sem, 1)
                dve.wait_ge(dve_done.sem, dve_done.next(dve))

            def log1p(dst, e, w, ln, tmp):
                dve.tensor_scalar(tmp, w, 1.0, 1e-30, ALU.subtract, ALU.max).then_inc(dve_done.sem, 1)
                dve.wait_ge(dve_done.sem, dve_done.next(dve))
                dve.reciprocal(tmp, tmp).then_inc(dve_done.sem, 1)
                dve.wait_ge(dve_done.sem, dve_done.next(dve))
                dve.tensor_tensor(tmp, tmp, ln, ALU.mult).then_inc(dve_done.sem, 1)
                dve.wait_ge(dve_done.sem, dve_done.next(dve))
                dve.tensor_tensor(tmp, tmp, e, ALU.mult).then_inc(dve_done.sem, 1)
                dve.wait_ge(dve_done.sem, dve_done.next(dve))
                dve.tensor_scalar(dst, w, 1.0, None, ALU.is_equal).then_inc(dve_done.sem, 1)
                dve.wait_ge(dve_done.sem, dve_done.next(dve))
                dve.tensor_tensor(dst, dst, e, ALU.mult).then_inc(dve_done.sem, 1)
                dve.wait_ge(dve_done.sem, dve_done.next(dve))
                dve.tensor_tensor(dst, dst, tmp, ALU.add).then_inc(dve_done.sem, 1)
                dve.wait_ge(dve_done.sem, dve_done.next(dve))

            def y_lengths(t):
                dve.tensor_reduce(ssq[:, 8 * t:8 * t + 8], y_sq.rearrange("p (h d) -> p h d", d=128), AX_X, ALU.add).then_inc(
                    signal("y_ssq").sem, 1)
                dve.wait_ge(signal("y_ssq").sem, signal("y_ssq").next(dve))

            def delta_rule():
                dve.memset(G["S"], 0.0).then_inc(signal("state_ready").sem, 1)
                dve.wait_ge(signal("state_ready").sem, signal("state_ready").next(dve))
                for t in range(T):
                    if t in (1, 2):
                        rest_of_chunk(W["mix_out"][t - 1])
                    g = U["gdn"][t]
                    tok = slice(t * P, (t + 1) * P)

                    def heads(u):
                        return ps(u)[:, :].rearrange("p (h c) -> p h c", h=GDN_HEADS)

                    bt = rep(beta[:, t, :], 2, P)
                    dve.tensor_tensor(G["gm"], rep(k("upto"), 1, GDN_HEADS), rep(gg[:, t, :], 2, P), ALU.mult).then_inc(
                        signal("gm_ready").sem, 1)
                    dve.wait_ge(signal("gm_ready").sem, signal("gm_ready").next(dve))
                    u = g["gc"][1]
                    dve.wait_ge(full[u.bank], u.n + 1)
                    dve.tensor_copy(gcol8[:, 0, :], ps(u)[:, 0:GDN_HEADS]).then_inc(drained[u.bank], 1)
                    dve.wait_ge(drained[u.bank], u.n + 1)
                    u = g["gc"][0]
                    dve.wait_ge(full[u.bank], u.n + 1)
                    dve.tensor_tensor(gcol8[:, 1, :], heads(u)[:, :, P - 1], gcol8[:, 0, :], ALU.subtract).then_inc(dve_done.sem, 1)
                    dve.wait_ge(dve_done.sem, dve_done.next(dve))
                    dve.tensor_tensor(G["dec"], heads(u), rep(gcol8[:, 0, :], 2, P), ALU.subtract).then_inc(dve_done.sem, 1)
                    dve.wait_ge(dve_done.sem, dve_done.next(dve))
                    dve.tensor_scalar(G["dec"], G["dec"], 0.0, None, ALU.min).then_inc(signal("dec_raw").sem, 1)
                    dve.wait_ge(signal("dec_raw").sem, signal("dec_raw").next(dve))
                    dve.wait_ge(signal("dec_exp").sem, signal("dec_exp").next(dve))
                    dve.tensor_tensor(G["dec"], G["dec"], rep(k("upto"), 1, GDN_HEADS), ALU.mult).then_inc(dve_done.sem, 1)
                    dve.wait_ge(dve_done.sem, dve_done.next(dve))
                    u = g["kq"][0]
                    dve.wait_ge(full[u.bank], u.n + 1)
                    dve.tensor_tensor(G["attnT"], heads(u), G["dec"], ALU.mult).then_inc(drained[u.bank], 1)
                    dve.wait_ge(drained[u.bank], u.n + 1)
                    dve.tensor_tensor(G["dec"], G["dec"], rep(k("before"), 1, GDN_HEADS), ALU.mult).then_inc(dve_done.sem, 1)
                    dve.wait_ge(dve_done.sem, dve_done.next(dve))
                    dve.tensor_tensor(G["dec"], G["dec"], bt, ALU.mult).then_inc(dve_done.sem, 1)
                    dve.wait_ge(dve_done.sem, dve_done.next(dve))
                    u = g["kk"][0]
                    dve.wait_ge(full[u.bank], u.n + 1)
                    dve.tensor_tensor(G["LT"], heads(u), G["dec"], ALU.mult).then_inc(drained[u.bank], 1)
                    dve.wait_ge(drained[u.bank], u.n + 1)
                    u = g["kt"][0]
                    dve.wait_ge(full[u.bank], u.n + 1)
                    dve.tensor_tensor(G["kg"], heads(u), rep(ge8[:, 0, :], 2, P), ALU.mult).then_inc(dve_done.sem, 1)
                    dve.wait_ge(dve_done.sem, dve_done.next(dve))
                    dve.tensor_tensor(G["ktail"], heads(u), rep(ge8[:, 1, :], 2, P), ALU.mult).then_inc(drained[u.bank], 1)
                    dve.wait_ge(drained[u.bank], u.n + 1)
                    dve.tensor_tensor(G["qd"], N_["QKVT"][:, 0:GDN_HEADS, tok], G["eg"], ALU.mult).then_inc(dve_done.sem, 1)
                    dve.wait_ge(dve_done.sem, dve_done.next(dve))
                    dve.tensor_copy(G["Inv"], rep(ident, 1, GDN_HEADS)).then_inc(dve_done.sem, 1)
                    dve.wait_ge(dve_done.sem, dve_done.next(dve))
                    dve.tensor_copy(G["InvT"], rep(ident, 1, GDN_HEADS)).then_inc(dve_done.sem, 1)
                    dve.wait_ge(dve_done.sem, dve_done.next(dve))
                    dve.tensor_tensor(CT[0], G["LT"], rep(k("level0"), 1, GDN_HEADS), ALU.mult).then_inc(
                        signal("level_ready").sem, 1)
                    dve.wait_ge(signal("level_ready").sem, signal("level_ready").next(dve))
                    for l in range(LEVELS):
                        if l + 1 < LEVELS:
                            dve.tensor_tensor(CT[(l + 1) % 2], G["LT"], rep(k(f"level{l + 1}"), 1, GDN_HEADS), ALU.mult).then_inc(
                                signal("level_ready").sem, 1)
                            dve.wait_ge(signal("level_ready").sem, signal("level_ready").next(dve))
                        if l == 2 and t:
                            dve.wait_ge(signal("y_squared").sem, signal("y_squared").next(dve))
                            y_lengths(t - 1)
                        for q, (_, u2, u3) in enumerate(g["inv"][l]):
                            for u, dst in ((u2, "Inv"), (u3, "InvT")):
                                if u:
                                    dve.wait_ge(full[u.bank], u.n + 1)
                                    x = G[dst][:, pair(q), :]
                                    dve.tensor_tensor(x, x, ps(u)[:, 0:2 * P].rearrange("p (h c) -> p h c", h=2), ALU.subtract).then_inc(
                                        drained[u.bank], 1)
                    u = g["u"][0]
                    dve.wait_ge(full[u.bank], u.n + 1)
                    dve.tensor_tensor(G["ub"], heads(u), bt, ALU.mult).then_inc(drained[u.bank], 1)
                    dve.wait_ge(drained[u.bank], u.n + 1)
                    u = g["ws"][0]
                    dve.wait_ge(full[u.bank], u.n + 1)
                    dve.tensor_tensor(G["t2"], heads(u), bt, ALU.mult).then_inc(drained[u.bank], 1)
                    dve.wait_ge(drained[u.bank], u.n + 1)
                    dve.tensor_tensor(G["vn"], G["ub"], G["t2"], ALU.subtract).then_inc(signal("v_new").sem, 1)
                    dve.wait_ge(signal("v_new").sem, signal("v_new").next(dve))
                    u = g["s"][0]
                    dve.wait_ge(full[u.bank], u.n + 1)
                    dve.tensor_tensor(G["S"], G["S"], rep(G["eg"][:, :, P - 1], 2, P), ALU.mult).then_inc(dve_done.sem, 1)
                    dve.wait_ge(dve_done.sem, dve_done.next(dve))
                    dve.tensor_tensor(G["S"], G["S"], heads(u), ALU.add).then_inc(drained[u.bank], 1)
                    dve.wait_ge(drained[u.bank], u.n + 1)

            def ffn(l):
                chunks = W[f"ffn{l}_up"] + W[f"ffn{l}_down"]
                n = 0
                for i, us in enumerate(U[f"ffn{l}_up"]):
                    rest_of_chunk(chunks[i + 1])
                    for m in range(2):
                        taps = lambda tile: [col("ffn_conv_w_2", (l * FFN_CONV + w) * 2 * KF + tile) for w in range(FFN_CONV)]
                        off = lambda tile: col("ffn_conv_b_2", l * 2 * KF + tile)
                        conv(F_["cg"][:, m, :], us[2 * m], taps(n), off(n))
                        conv(F_["cv"][:, m, :], us[2 * m + 1], taps(KF + n), off(KF + n))
                        dve.wait_ge(signal("ff_silu").sem, signal("ff_silu").next(dve))
                        dve.tensor_tensor(F_["act"][:, n, :], F_["cg"][:, m, :], F_["cv"][:, m, :], ALU.mult).then_inc(
                            dve_done.sem, 1)
                        dve.wait_ge(dve_done.sem, dve_done.next(dve))
                        if n < 7:
                            cut(act_hi(n), F_["act"][:, n, :])
                            dve.tensor_tensor(one_pass(F_["act"][:, n, :]), F_["act"][:, n, :], parts(act_hi(n)), ALU.subtract).then_inc(
                                signal("ff_act").sem, 1)
                            dve.wait_ge(signal("ff_act").sem, signal("ff_act").next(dve))
                        n += 1
                rest_of_chunk(W[f"ffn{l}_down"][1])
                for n in range(7, KF):
                    if n in (12, 16):
                        rest_of_chunk(W[f"ffn{l}_down"][n // 4 - 1])
                    cut(act_hi(n), F_["act"][:, n, :])
                    dve.tensor_tensor(one_pass(F_["act"][:, n, :]), F_["act"][:, n, :], parts(act_hi(n)), ALU.subtract).then_inc(
                        signal("ff_act").sem, 1)
                    dve.wait_ge(signal("ff_act").sem, signal("ff_act").next(dve))
                for c in W[f"ffn{l}_down"][KF // 4 - 1:]:
                    rest_of_chunk(c)

            rest_of_T("x_T", dst=x_lo)
            rest_of_chunk(W["even_in"][0])
            for c in W["even_in"][1:]:
                rest_of_chunk(c)
            dve.memset(rel_sb[0:64, :], 0.0).then_inc(dve_done.sem, 1)
            dve.wait_ge(dve_done.sem, dve_done.next(dve))
            u = U["rel"][0]
            dve.wait_ge(full[u.bank], u.n + 1)
            rel_v = rel_sb[:, :].rearrange("p (h s) -> p h s", s=2 * NA_ROWS)
            rel_u = ps(u)[0:REL_C, 0:C_HEADS * REL_R].rearrange("p (h s) -> p h s", s=REL_R)
            dve.tensor_copy(rel_v[0:REL_C, :, 0:REL_R], rel_u).then_inc(dve_done.sem, 1)
            dve.wait_ge(dve_done.sem, dve_done.next(dve))
            dve.tensor_copy(rel_v[32:32 + REL_C, :, 1:1 + REL_R], rel_u).then_inc(drained[u.bank], 1)
            dve.wait_ge(drained[u.bank], u.n + 1)
            rel_hi = big[0:64, T * EVEN_IN:T * EVEN_IN + C_HEADS * 2 * NA_ROWS]
            dve.tensor_copy(one_pass(rel_hi), rel_sb[0:64, :]).then_inc(dve_done.sem, 1)
            dve.wait_ge(dve_done.sem, dve_done.next(dve))
            dve.tensor_tensor(one_pass(rel_sb[0:64, :]), rel_sb[0:64, :], parts(rel_hi), ALU.subtract).then_inc(dve_done.sem, 1)
            dve.wait_ge(dve_done.sem, dve_done.next(dve))
            dve.tensor_copy(one_pass(rel_sb[64:128, :]), parts(rel_hi)).then_inc(signal("rel_split").sem, 1)
            dve.wait_ge(signal("rel_split").sem, signal("rel_split").next(dve))
            for us in U["even_in"]:
                for u in us:
                    dve.wait_ge(drained[u.bank], u.n + 1)
            dve.wait_ge(signal("table_loaded").sem, signal("table_loaded").next(dve, 16))
            dve.wait_ge(signal("small_loaded").sem, signal("small_loaded").next(dve, 16 * (len(bc_at) + 5)))
            lv = bc[:, bc_at["even_lam_q1"][0]:bc_at["even_lam_q1"][0] + 256].rearrange("p (m a d) -> p m a d", m=2, a=2)
            lt = E["tmp"][:, 3, 0:128].rearrange("p (m d) -> p m d", m=2)
            dve.tensor_tensor(lt, lv[:, :, 0, :], lv[:, :, 1, :], ALU.mult).then_inc(dve_done.sem, 1)
            dve.wait_ge(dve_done.sem, dve_done.next(dve))
            dve.tensor_reduce(lam[:, 0:2], lt, AX_X, ALU.add).then_inc(signal("lam_dots").sem, 1)
            dve.wait_ge(signal("lam_dots").sem, signal("lam_dots").next(dve))
            tmp = [E["p"][i // 2][:, i % 2, :].rearrange("p (t g d) -> p t g d", t=T, g=16) for i in range(4)]
            qk = E["H"][:, :, 0:2 * A_QKV].rearrange("p t (g d) -> p t g d", d=A_DIM)
            h = A_ROT // 2
            cs = [rep(k(f"ra_{f}").rearrange("p (t d) -> p t d", t=T), 2, 16) for f in ("cos", "sin")]
            rope(qk[:, :, :, 0:h], qk[:, :, :, h:2 * h], cs[0], cs[1], tmp, "rope_a")
            dve.wait_ge(signal("rstd_ready").sem, signal("rstd_ready").next(dve))
            for j, (o, n, name) in enumerate(((3 * A_QKV, B_Q_RANK, "even_q_norm_g"), (3 * A_QKV + B_Q_RANK, B_KV_RANK, "even_kv_norm_g"))):
                for t in range(T):
                    x = E["H"][:, t, o:o + n]
                    dve.scalar_tensor_tensor(x, x, rstd[:, j * T + t:j * T + t + 1], bcv(name), ALU.mult, ALU.mult).then_inc(
                        signal("lat_ready").sem, 1)
                    dve.wait_ge(signal("lat_ready").sem, signal("lat_ready").next(dve))
            dve.wait_ge(signal("lam_exp").sem, signal("lam_exp").next(dve))
            dve.tensor_tensor(lam[:, 2:3], lam[:, 1:2], lam[:, 0:1], ALU.subtract).then_inc(dve_done.sem, 1)
            dve.wait_ge(dve_done.sem, dve_done.next(dve))
            dve.tensor_scalar(lam[:, 2:3], lam[:, 2:3], -LAMBDA_INIT, None, ALU.add).then_inc(dve_done.sem, 1)
            dve.wait_ge(dve_done.sem, dve_done.next(dve))
            for name in ("uq", "ukv"):
                for u in U[name][0]:
                    dve.wait_ge(drained[u.bank], u.n + 1)
            h = B_ROPE // 2
            cs = [k(f"rb_{f}").rearrange("p (t d) -> p t d", t=T) for f in ("cos", "sin")]
            tmp = [E["tmp"][:, i, :].rearrange("p (t g d) -> p t g d", t=T, g=B_HEADS) for i in range(4)]
            rope(E["QB"][:, :, :, B_NOPE:B_NOPE + h], E["QB"][:, :, :, B_NOPE + h:], rep(cs[0], 2, B_HEADS), rep(cs[1], 2, B_HEADS), tmp, "rope_b")
            kr = E["H"][:, :, EVEN_IN - B_ROPE:EVEN_IN]
            tmp = [E["tmp"][:, i, 0:T * h].rearrange("p (t d) -> p t d", t=T) for i in range(4)]
            rope(kr[:, :, 0:h], kr[:, :, h:], cs[0], cs[1], tmp, None)
            dve.tensor_copy(E["KC"][:, :, :, B_NOPE:], rep(kr, 2, B_HEADS)).then_inc(signal("rope_b").sem, 1)
            dve.wait_ge(signal("rope_b").sem, signal("rope_b").next(dve))
            if on(2):
                attention("A")
                attention("B", "even_o")
                o = XH[:, :, 0:512]
                sq = E["H"][:, :, 0:512]
                dve.tensor_tensor(sq, o, o, ALU.mult).then_inc(dve_done.sem, 1)
                dve.wait_ge(dve_done.sem, dve_done.next(dve))
                dve.tensor_reduce(ssq[:, 0:16].rearrange("p (t h) -> p t h", t=T), sq.rearrange("p t (h d) -> p t h d", d=128), AX_X, ALU.add).then_inc(
                    signal("a_ssq").sem, 1)
                dve.wait_ge(signal("a_ssq").sem, signal("a_ssq").next(dve))
                dve.wait_ge(signal("rstd_ready").sem, signal("rstd_ready").next(dve))
                dve.tensor_scalar(rstd[:, 0:16], rstd[:, 0:16], 1.0 - LAMBDA_INIT, None, ALU.mult).then_inc(dve_done.sem, 1)
                dve.wait_ge(dve_done.sem, dve_done.next(dve))
                for t in range(T):
                    ov = XH[:, t, 0:512].rearrange("p (h d) -> p h d", d=128)
                    dve.tensor_tensor(ov, ov, rep(rstd[:, 4 * t:4 * t + 4], 2, 128), ALU.mult).then_inc(dve_done.sem, 1)
                    dve.wait_ge(dve_done.sem, dve_done.next(dve))
                    ins = dve.tensor_tensor(ov, ov, rep(bcv("even_subln_g"), 1, A_HEADS), ALU.mult)
                    if t == T - 1:
                        ins.then_inc(signal("a_normed").sem, 1)
                        dve.wait_ge(signal("a_normed").sem, signal("a_normed").next(dve))
                    else:
                        ins.then_inc(dve_done.sem, 1)
                        dve.wait_ge(dve_done.sem, dve_done.next(dve))
                rest_of_T("o0_T")
                rest_of_chunk(W["even_o"][1])
                residual("even_o", ALPHA, norm=True)
            if on(3):
                layer_norm(stats=False)
            if on(4):
                route(0)
                dve.wait_ge(signal("x_applied").sem, signal("x_applied").next(dve, T))
                experts(0)
                layer_norm()
            if on(5):
                rest_of_chunk(W["qkv"][0])
                rest_of_T("ln20_T", gain="ln2_g", bias="ln2_b", dst=x_lo)
                for c in W["qkv"][1:]:
                    rest_of_chunk(c)
                dve.wait_ge(signal("x_applied").sem, signal("x_applied").next(dve, T))
                attention("C", "odd_o")
                rest_of_T("o1_T")
                rest_of_chunk(W["odd_o"][1])
                residual("odd_o", ALPHA, norm=True)
                layer_norm(stats=False)
            if on(6):
                route(1)
                dve.wait_ge(signal("x_applied").sem, signal("x_applied").next(dve, T))
                experts(1)
                layer_norm_in_place()
            if on(7):
                rest_of_chunk(W["mix_in"][0])
                rms()
                rest_of_T("rms0_T", gain="norm_mix_2")
                cut(ba_hi, ba_w[:, :, :])
                dve.tensor_tensor(one_pass(ba_w[:, :, :]), ba_w[:, :, :], parts(ba_hi), ALU.subtract).then_inc(
                    signal("ba_split").sem, 1)
                dve.wait_ge(signal("ba_split").sem, signal("ba_split").next(dve))
                for i in range(8):
                    if i < 7:
                        rest_of_chunk(W["mix_in"][i + 1])
                    if i == 3:
                        for us in U["mix_in"][0:2]:
                            for u in us:
                                dve.wait_ge(drained[u.bank], u.n + 1)
                        h = HEAD // 2
                        for t in range(T):
                            x = N_["RQK"][:, t, :].rearrange("p (g d) -> p g d", d=HEAD)
                            cs = [rep(k(f"rr_{f}")[:, t * h:(t + 1) * h], 1, 8) for f in ("cos", "sin")]
                            tmp = [N_["rt"][:, i, :, :] for i in range(4)]
                            rope(x[:, :, 0:h], x[:, :, h:], cs[0], cs[1], tmp, "rotated" if t == T - 1 else None)
                    if i not in (4, 5, 6):
                        continue
                    for m, u in enumerate(U["mix_in"][i]):
                        tile = 4 * (i - 4) + m
                        conv(N_["QKVT"][:, tile, :], u, [col("gdn_conv_w_2", w * 12 + tile) for w in range(SHORT_CONV)])
                u = U["ba"][0]
                dve.wait_ge(full[u.bank], u.n + 1)
                dve.tensor_copy(gb, ps(u)[:, 0:T * 8].rearrange("p (t c) -> p t c", t=T)).then_inc(drained[u.bank], 1)
                dve.wait_ge(drained[u.bank], u.n + 1)
                ad = gb[:, :, GDN_HEADS:]
                dve.tensor_tensor(ad, ad, rep(bcv("gdn_dt_bias_2"), 1, T), ALU.add).then_inc(dve_done.sem, 1)
                dve.wait_ge(dve_done.sem, dve_done.next(dve))
                dve.tensor_scalar(sp4, ad, -1.0, None, ALU.mult).then_inc(dve_done.sem, 1)
                dve.wait_ge(dve_done.sem, dve_done.next(dve))
                dve.tensor_tensor(sp1, sp4, ad, ALU.max).then_inc(signal("ab_ready").sem, 1)
                dve.wait_ge(signal("ab_ready").sem, signal("ab_ready").next(dve))
                dve.wait_ge(signal("ab_exp").sem, signal("ab_exp").next(dve))
                dve.tensor_scalar(sp2, sp1, 1.0, None, ALU.add).then_inc(signal("ln_arg").sem, 1)
                dve.wait_ge(signal("ln_arg").sem, signal("ln_arg").next(dve))
                dve.tensor_scalar(beta, beta, 0.5, 0.5, ALU.mult, ALU.add).then_inc(dve_done.sem, 1)
                dve.wait_ge(dve_done.sem, dve_done.next(dve))
                dve.wait_ge(signal("ln_done").sem, signal("ln_done").next(dve))
                log1p(sp4, sp1, sp2, sp3, gg)
                dve.scalar_tensor_tensor(sp4, ad, 0.0, sp4, ALU.max, ALU.add).then_inc(dve_done.sem, 1)
                dve.wait_ge(dve_done.sem, dve_done.next(dve))
                dve.tensor_tensor(sp4, sp4, rep(lam[:, 4:8], 1, T), ALU.mult).then_inc(dve_done.sem, 1)
                dve.wait_ge(dve_done.sem, dve_done.next(dve))
                dve.tensor_scalar(gg, sp4, -1.0, None, ALU.mult).then_inc(dve_done.sem, 1)
                dve.wait_ge(dve_done.sem, dve_done.next(dve))
                for i in (3, 7):
                    for u in U["mix_in"][i]:
                        dve.wait_ge(drained[u.bank], u.n + 1)
                dve.wait_ge(signal("decay_loaded").sem, signal("decay_loaded").next(dve, 16))
                for hd, r in enumerate(U["ret"]):
                    for kc, u in enumerate(r["s"]):
                        dve.wait_ge(full[u.bank], u.n + 1)
                        n = S - kc * P
                        dve.tensor_tensor(N_["sc"][:, sc_at[kc]:sc_at[kc] + n], ps(u)[:, 0:n], N_["dret"][:, hd, 0:n], ALU.mult).then_inc(
                            drained[u.bank], 1)
                        dve.wait_ge(drained[u.bank], u.n + 1)
                    for i in (2 * hd, 2 * hd + 1):
                        rn = l2_buf[2 + i % 2]
                        dve.wait_ge(drained[U["l2"][i].bank], U["l2"][i].n + 1)
                        dve.reciprocal(rn, rn).then_inc(dve_done.sem, 1)
                        dve.wait_ge(dve_done.sem, dve_done.next(dve))
                        x = N_["QKVT"][:, i, :]
                        dve.scalar_tensor_tensor(x, x, HEAD ** -0.5 if i < GDN_HEADS else 1.0, rn, ALU.mult, ALU.mult).then_inc(
                            signal("l2_normed").sem, 1)
                        dve.wait_ge(signal("l2_normed").sem, signal("l2_normed").next(dve))
                    u = r["o"][0]
                    dve.wait_ge(full[u.bank], u.n + 1)
                    dve.tensor_copy(XH[:, :, 128 * hd:128 * hd + 128], ps(u)[:, :].rearrange("p (t d) -> p t d", t=T)).then_inc(
                        drained[u.bank], 1)
                    dve.wait_ge(drained[u.bank], u.n + 1)
                delta_rule()
                t = T - 1
                u = U["gdn"][t]["o"][0]
                dve.wait_ge(drained[u.bank], u.n + 1)
                dve.tensor_tensor(y_sq, XH[:, t, :], XH[:, t, :], ALU.mult).then_inc(dve_done.sem, 1)
                dve.wait_ge(dve_done.sem, dve_done.next(dve))
                y_lengths(t)
                dve.wait_ge(signal("gate_gained").sem, signal("gate_gained").next(dve))
                dve.wait_ge(signal("rstd_ready").sem, signal("rstd_ready").next(dve, T))
                y = XH[:, t, :].rearrange("p (h d) -> p h d", d=128)
                dve.tensor_tensor(y, y, rep(rstd[:, 8 * t:8 * t + 8], 2, 128), ALU.mult).then_inc(dve_done.sem, 1)
                dve.wait_ge(dve_done.sem, dve_done.next(dve))
                dve.tensor_tensor(XH[:, t, 0:512], XH[:, t, 0:512], N_["GR"][:, t, :], ALU.mult).then_inc(dve_done.sem, 1)
                dve.wait_ge(dve_done.sem, dve_done.next(dve))
                dve.tensor_tensor(XH[:, t, 512:1024], XH[:, t, 512:1024], N_["GD"][:, t, :], ALU.mult).then_inc(signal("y_ready").sem, 1)
                rest_of_T("y_T")
                residual("mix_out", 1.0, "ffn0_up" if on(8) else None)
            if on(8):
                rms()
                rest_of_T("rmsf0_T", gain="norm_ffn_2")
                ffn(0)
                ffn_residual(0)
            if on(9):
                rest_of_chunk(W["lru_in"][0])
                rms()
                rest_of_T("rms1_T", gain="norm_mix_2", gain_at=KD)
                lm = chan[:, chan_at["lru_lambda_2"]:chan_at["lru_lambda_2"] + KD]
                dve.tensor_scalar(sl2, lm, -1.0, None, ALU.mult).then_inc(dve_done.sem, 1)
                dve.wait_ge(dve_done.sem, dve_done.next(dve))
                dve.tensor_tensor(sl1, sl2, lm, ALU.max).then_inc(signal("lam_arg").sem, 1)
                dve.wait_ge(signal("lam_arg").sem, signal("lam_arg").next(dve))
                dve.wait_ge(signal("lam_e").sem, signal("lam_e").next(dve))
                dve.tensor_scalar(sl2, sl1, 1.0, None, ALU.add).then_inc(signal("lam_w").sem, 1)
                dve.wait_ge(signal("lam_w").sem, signal("lam_w").next(dve))
                dve.wait_ge(signal("lam_ln").sem, signal("lam_ln").next(dve))
                log1p(cvec, sl1, sl2, sl3, bnst.rearrange("p a b c -> p (a b c)")[:, 0:KD])
                dve.tensor_scalar(sl2, lm, -1.0, 0.0, ALU.mult, ALU.max).then_inc(dve_done.sem, 1)
                dve.wait_ge(dve_done.sem, dve_done.next(dve))
                dve.tensor_tensor(cvec, cvec, sl2, ALU.add).then_inc(dve_done.sem, 1)
                dve.wait_ge(dve_done.sem, dve_done.next(dve))
                dve.tensor_scalar(cvec, cvec, -8.0, None, ALU.mult).then_inc(signal("cvec_ready").sem, 1)
                dve.wait_ge(signal("cvec_ready").sem, signal("cvec_ready").next(dve))
                for c in W["lru_in"][1:]:
                    rest_of_chunk(c)
                for i in range(2):
                    if i == 1:
                        rest_of_chunk(W["lru_out"][0])
                    for m, u in enumerate(U["lru_in"][2 + i]):
                        tile = 4 * i + m
                        conv(L_["xr"][:, tile, :], u, [col("lru_conv_w_2", w * KD + tile) for w in range(LRU_CONV)], col("lru_conv_b_2", tile))
                rest_of_chunk(W["lru_out"][1])
                for m in range(KD):
                    dve.wait_ge(drained[U["lru"][m][1].bank], U["lru"][m][1].n + 1)
                    x = L_["i"][:, m, :]
                    dve.tensor_tensor(x, x, L_["xr"][:, m, :], ALU.mult).then_inc(signal("lru_x").sem, 1)
                    dve.wait_ge(signal("lru_x").sem, signal("lru_x").next(dve))
                def root_argument(m):
                    dve.wait_ge(signal("lru_square").sem, signal("lru_square").next(dve))
                    z = XT[:, m, :]
                    dve.scalar_tensor_tensor(z, L_["q"][:, m % 2, :], 1.0, z, ALU.add, ALU.mult).then_inc(signal("lru_arg").sem, 1)
                    dve.wait_ge(signal("lru_arg").sem, signal("lru_arg").next(dve))

                def recurrence(m):
                    dve.wait_ge(signal("lru_in").sem, signal("lru_in").next(dve))
                    x = L_["i"][:, m, :]
                    dve.tensor_tensor_scan(x, L_["xr"][:, m, :], XT[:, m, :], 0.0, ALU.mult, ALU.add).then_inc(dve_done.sem, 1)
                    dve.wait_ge(dve_done.sem, dve_done.next(dve))
                    dve.tensor_tensor(L_["gate"][:, m, :], L_["gate"][:, m, :], x, ALU.mult).then_inc(signal("lru_gated").sem, 1)
                    dve.wait_ge(signal("lru_gated").sem, signal("lru_gated").next(dve))

                def rest_of_gated(m):
                    dve.wait_ge(signal("lru_rounded").sem, signal("lru_rounded").next(dve))
                    dve.tensor_tensor(one_pass(XH[:, :, m * P:(m + 1) * P]), L_["gate"][:, m, :].rearrange("p (t c) -> p t c", t=T), parts(XT[:, m, :].rearrange("p (t c) -> p t c", t=T)), ALU.subtract).then_inc(
                        signal("lru_y").sem, 1)
                    dve.wait_ge(signal("lru_y").sem, signal("lru_y").next(dve))

                half = KD // 2
                for m in range(half):
                    root_argument(m)
                for m in range(half):
                    recurrence(m)
                    root_argument(half + m)
                for m in range(half):
                    recurrence(half + m)
                    rest_of_gated(m)
                for m in range(half):
                    rest_of_gated(half + m)
                residual("lru_out", 1.0, "ffn1_up" if on(10) else None)
            if on(10):
                rms()
                rest_of_T("rmsf1_T", gain="norm_ffn_2", gain_at=KD)
                ffn(1)
                ffn_residual(1)
            if on(11):
                dve.wait_ge(signal("ln_loaded").sem, signal("ln_loaded").next(dve, 16))
                for t in range(T):
                    dve.wait_ge(signal("rstd_ready").sem, signal("rstd_ready").next(dve))
                    dve.scalar_tensor_tensor(XH[:, t, :], X[:, t, :], rstd[:, t:t + 1], lnp[:, 0, :], ALU.mult, ALU.mult).then_inc(
                        signal("out_ready").sem, 1)
                    dve.wait_ge(signal("out_ready").sem, signal("out_ready").next(dve))
            else:
                if stages in (3, 4, 5):
                    dve.wait_ge(full[U[{3: "ln10_T", 4: "ln20_T", 5: "ln11_T"}[stages]][-1].bank], U[{3: "ln10_T", 4: "ln20_T", 5: "ln11_T"}[stages]][-1].n + 1)
                for t in range(T):
                    if stages in (3, 4, 5, 6):
                        dve.wait_ge(signal("x_applied").sem, signal("x_applied").next(dve))
                    dve.tensor_copy(XH[:, t, :], X[:, t, :]).then_inc(signal("out_ready").sem, 1)
                    dve.wait_ge(signal("out_ready").sem, signal("out_ready").next(dve))


def kernel(**inputs):
    import numpy as np
    import concourse.bacc as bacc
    from concourse.bass_utils import run_bass_kernel_spmd

    nc = bacc.Bacc("TRN2", target_bir_lowering=False, num_devices=1)
    arrays = {n: np.ascontiguousarray(v) for n, v in inputs.items()}
    arrays["shape_table"] = shape_constants()[0]
    arrays["retention_decay"] = retention_decay()
    aps = {n: nc.dram_tensor(n, v.shape, mybir.dt.from_np(v.dtype), kind="ExternalInput").ap() for n, v in arrays.items()}
    out = nc.dram_tensor("out", (1, S, D), F32, kind="ExternalOutput").ap()
    build(nc, aps, out)
    return run_bass_kernel_spmd(nc, [arrays], core_ids=[0]).results[0]["out"]
```
